# Optimizing a Trainium2 kernel written in Bass

```python
import math
import jax
import jax.numpy as jnp
from jax import lax
import numpy as np
import jax, jax.numpy as jnp

D_MODEL = 1024
BATCH = 1
SEQ = 512
DEPTH = 2

GRID_W = 64
CTX_LEN = 256

SSD_HEADS = 16
SSD_HEAD_DIM = 64
SSD_INNER = SSD_HEADS * SSD_HEAD_DIM
SSD_GROUPS = 2
SSD_STATE = 128
SSD_CONV = 5
SSD_CHUNK = 128
SSD_XBC = SSD_INNER + 2 * SSD_GROUPS * SSD_STATE

HG_HEADS = 8
HG_DK = 128
HG_DV = D_MODEL // HG_HEADS
HG_INNER_K = HG_HEADS * HG_DK
HG_INNER_V = HG_HEADS * HG_DV
HG_CHUNK = 64

IN_SIZES = (SSD_INNER, SSD_XBC, 2 * SSD_HEADS, HG_INNER_K, 2 * HG_INNER_K, HG_INNER_V, HG_INNER_V)
IN_TOTAL = sum(IN_SIZES)
MIX_OUT = SSD_INNER + HG_INNER_V

CONF_KERNEL = 31
D_FF = 2816
FFN_CONV = 3

N_EVEN = (DEPTH + 1) // 2
N_ODD = DEPTH // 2
ALPHA = (2 * DEPTH) ** 0.25
BETA = (8 * DEPTH) ** -0.25
EPS = 1e-5
F32 = jnp.float32


def _split(t, sizes):
    return jnp.split(t, np.cumsum(sizes)[:-1].tolist(), axis=-1)

def _flip(t, rev):
    return t[:, ::-1] if rev else t

def layer_norm(t, g, b):
    tf = t.astype(F32)
    mu = tf.mean(-1, keepdims=True)
    var = jnp.square(tf - mu).mean(-1, keepdims=True)
    return ((tf - mu) * lax.rsqrt(var + EPS) * g.astype(F32) + b.astype(F32)).astype(t.dtype)

def rms_norm(t, w, groups):
    tf = t.astype(F32)
    tg = tf.reshape(tf.shape[:-1] + (groups, tf.shape[-1] // groups))
    tg = tg * lax.rsqrt(jnp.square(tg).mean(-1, keepdims=True) + EPS)
    return tg.reshape(tf.shape) * w.astype(F32)

def modulate(t, shift, scale):
    return t * (1 + scale) + shift

def dwconv1d(t, w, b):
    k = w.shape[0]
    y = lax.conv_general_dilated(t, w[:, None, :].astype(t.dtype), (1,), [(k // 2, k // 2)],
                                 dimension_numbers=('NWC', 'WIO', 'NWC'), feature_group_count=t.shape[-1])
    return y + b.astype(t.dtype)

def dwconv2d(t, w, b, rows, cols):
    bsz, n, ch = t.shape
    k = w.shape[0]
    y = lax.conv_general_dilated(t.reshape(bsz, rows, cols, ch), w[:, :, None, :].astype(t.dtype), (1, 1),
                                 [(k // 2, k // 2), (k // 2, k // 2)],
                                 dimension_numbers=('NHWC', 'HWIO', 'NHWC'), feature_group_count=ch)
    return y.reshape(bsz, n, ch) + b.astype(t.dtype)

def segsum(a):
    t = a.shape[-1]
    cs = jnp.cumsum(a, -1)
    mask = jnp.tril(jnp.ones((t, t), dtype=bool))
    return jnp.where(mask, cs[..., :, None] - cs[..., None, :], -jnp.inf)

def ssd_scan(xs, dt, a_coef, bm, cm, h0):
    b, l, h, p = xs.shape
    g, n = bm.shape[2:]
    j = h // g
    c = SSD_CHUNK
    nc = l // c
    xdt = (xs.astype(F32) * dt[..., None]).reshape(b, nc, c, g, j, p)
    a = (dt * a_coef).reshape(b, nc, c, h).transpose(0, 3, 1, 2)
    bc = bm.astype(F32).reshape(b, nc, c, g, n)
    cc = cm.astype(F32).reshape(b, nc, c, g, n)
    a_cum = jnp.cumsum(a, -1)
    decay = jnp.exp(segsum(a)).reshape(b, g, j, nc, c, c)
    cb = jnp.einsum('bclgn,bcsgn->bgcls', cc, bc)
    y_diag = jnp.einsum('bgcls,bgjcls,bcsgjp->bclgjp', cb, decay, xdt)
    decay_states = jnp.exp(a_cum[..., -1:] - a_cum).reshape(b, g, j, nc, c)
    states = jnp.einsum('bcsgn,bgjcs,bcsgjp->bcgjpn', bc, decay_states, xdt).reshape(b, nc, h, p, n)
    states = jnp.concatenate([h0[:, None].astype(F32), states], axis=1)
    decay_chunk = jnp.exp(segsum(jnp.pad(a_cum[..., -1], ((0, 0), (0, 0), (1, 0)))))
    states = jnp.einsum('bhzc,bchpn->bzhpn', decay_chunk, states)
    start, final = states[:, :-1], states[:, -1]
    y_off = jnp.einsum('bclgn,bcgjpn,bgjcl->bclgjp', cc, start.reshape(b, nc, g, j, p, n),
                       jnp.exp(a_cum).reshape(b, g, j, nc, c))
    return (y_diag + y_off).reshape(b, l, h, p), final

def gla_scan(q, k, v, log_f, s0):
    b, l, h, dk = q.shape
    dv = v.shape[-1]
    c = HG_CHUNK
    nc = l // c
    q, k, v, log_f = [t.astype(F32).reshape(b, nc, c, h, t.shape[-1]) for t in (q, k, v, log_f)]

    def step(s, inp):
        q_t, k_t, v_t, lf_t = inp
        s = jnp.exp(lf_t)[..., None] * s + k_t[..., None] * v_t[..., None, :]
        return s, jnp.einsum('bchk,bchkv->bchv', q_t, s)

    s_loc, o_loc = lax.scan(step, jnp.zeros((b, nc, h, dk, dv), F32),
                            tuple(jnp.moveaxis(t, 2, 0) for t in (q, k, v, log_f)))
    o_loc = jnp.moveaxis(o_loc, 0, 2)
    a_cum = jnp.cumsum(log_f, axis=2)

    def chunk_step(s, inp):
        s_end_local, a_tot = inp
        return jnp.exp(a_tot)[..., None] * s + s_end_local, s

    s_final, s_start = lax.scan(chunk_step, s0.astype(F32),
                                (jnp.moveaxis(s_loc, 1, 0), jnp.moveaxis(a_cum[:, :, -1], 1, 0)))
    s_start = jnp.moveaxis(s_start, 0, 1)
    o = o_loc + jnp.einsum('bcthk,bchkv->bcthv', q * jnp.exp(a_cum), s_start)
    return o.reshape(b, l, h, dv), s_final

def hgrn_gates(f_logit, lb, first):
    a = f_logit.astype(F32)
    if first:
        return jax.nn.log_sigmoid(a), jax.nn.sigmoid(-a)
    lb = lb.reshape(HG_HEADS, HG_DK)
    return jnp.log(lb + (1 - lb) * jax.nn.sigmoid(a)), (1 - lb) * jax.nn.sigmoid(-a)

def even_mixer(h, hc, w_in, conv_w, conv_b, dt_bias, a_log, d_skip, ssd_nw, lb, first, hg_nw, w_out, ctx_out):
    def branch_inputs(t):
        bsz, L, _ = t.shape
        z, xbc, dt_raw, q, f, v, g = _split(t @ w_in, IN_SIZES)
        xbc = jax.nn.silu(dwconv1d(xbc, conv_w, conv_b))
        xs, bm, cm = _split(xbc, (SSD_INNER, SSD_GROUPS * SSD_STATE, SSD_GROUPS * SSD_STATE))
        return {'z': z, 'g': g,
                'dt': dt_raw.astype(F32).reshape(bsz, L, 2, SSD_HEADS),
                'xs': xs.reshape(bsz, L, SSD_HEADS, SSD_HEAD_DIM),
                'bm': bm.reshape(bsz, L, SSD_GROUPS, SSD_STATE),
                'cm': cm.reshape(bsz, L, SSD_GROUPS, SSD_STATE),
                'q': jax.nn.silu(q).reshape(bsz, L, HG_HEADS, HG_DK),
                'f': f.reshape(bsz, L, 2, HG_HEADS, HG_DK),
                'v': v.reshape(bsz, L, HG_HEADS, HG_DV)}

    lat, cx = branch_inputs(h), branch_inputs(hc)
    bsz = h.shape[0]
    dsk = d_skip.astype(F32)[:, None]
    y_lat, y_ctx = dsk * lat['xs'].astype(F32), dsk * cx['xs'].astype(F32)
    o_lat_parts, o_ctx_parts = [], []
    for d in range(2):
        rev = d == 1
        a_coef = -jnp.exp(a_log[d].astype(F32))
        dt_l = jax.nn.softplus(lat['dt'][:, :, d] + dt_bias[d].astype(F32))
        dt_c = jax.nn.softplus(cx['dt'][:, :, d] + dt_bias[d].astype(F32))
        zeros_ssd = jnp.zeros((bsz, SSD_HEADS, SSD_HEAD_DIM, SSD_STATE), F32)
        yc_d, s_ctx = ssd_scan(_flip(cx['xs'], rev), _flip(dt_c, rev), a_coef,
                               _flip(cx['bm'], rev), _flip(cx['cm'], rev), zeros_ssd)
        yl_d, _ = ssd_scan(_flip(lat['xs'], rev), _flip(dt_l, rev), a_coef,
                           _flip(lat['bm'], rev), _flip(lat['cm'], rev), s_ctx)
        y_lat = y_lat + _flip(yl_d, rev)
        y_ctx = y_ctx + _flip(yc_d, rev)
        lf_l, k_l = hgrn_gates(lat['f'][:, :, d], lb, first)
        lf_c, k_c = hgrn_gates(cx['f'][:, :, d], lb, first)
        zeros_hg = jnp.zeros((bsz, HG_HEADS, HG_DK, HG_DV), F32)
        oc_d, st_ctx = gla_scan(_flip(cx['q'], rev), _flip(k_c, rev), _flip(cx['v'], rev),
                                _flip(lf_c, rev), zeros_hg)
        ol_d, _ = gla_scan(_flip(lat['q'], rev), _flip(k_l, rev), _flip(lat['v'], rev),
                           _flip(lf_l, rev), st_ctx)
        o_lat_parts.append(_flip(ol_d, rev))
        o_ctx_parts.append(_flip(oc_d, rev))

    def merge(s, y, o):
        bsz_, L = s['z'].shape[:2]
        ys = rms_norm(y.reshape(bsz_, L, SSD_INNER) * jax.nn.silu(s['z'].astype(F32)), ssd_nw, SSD_GROUPS)
        os_ = rms_norm(o.reshape(bsz_, L, HG_INNER_V), hg_nw, HG_HEADS) * jax.nn.silu(s['g'].astype(F32))
        return jnp.concatenate([ys, os_], axis=-1).astype(h.dtype) @ w_out

    y = merge(lat, y_lat, o_lat_parts[0] + o_lat_parts[1])
    yc = merge(cx, y_ctx, o_ctx_parts[0] + o_ctx_parts[1]) if ctx_out else None
    return y, yc

def conformer_conv(t, w1, b1, dw_w, dw_b, ln_g, ln_b, w2, b2):
    a, gate = jnp.split(t @ w1 + b1, 2, axis=-1)
    u = dwconv1d(a * jax.nn.sigmoid(gate), dw_w, dw_b)
    u = jax.nn.silu(layer_norm(u, ln_g, ln_b))
    return u @ w2 + b2

def conv_glu_ffn(t, w_up, conv_w, conv_b, w_down, rows, cols):
    v, gate = jnp.split(t @ w_up, 2, axis=-1)
    gate = dwconv2d(gate, conv_w, conv_b, rows, cols)
    return (jax.nn.gelu(gate, approximate=False) * v) @ w_down

def first_inputs(seed: int = 0) -> dict:
    key = jax.random.key(seed)
    keys = iter(jax.random.split(key, 32))

    def nrm(shape, scale):
        return jax.random.normal(next(keys), shape, F32) * scale

    def unif(shape, lo, hi):
        return jax.random.uniform(next(keys), shape, F32, lo, hi)

    d = D_MODEL
    inputs = {}
    inputs['x'] = nrm((BATCH, SEQ, d), 1.0)
    inputs['c'] = nrm((BATCH, d), 1.0)
    inputs['ctx'] = nrm((BATCH, CTX_LEN, d), 1.0)
    inputs['c_ctx'] = nrm((d,), 1.0)
    inputs['ada_w'] = nrm((DEPTH, d, 6 * d), d ** -0.5)
    inputs['ada_b'] = nrm((DEPTH, 6 * d), 0.02)
    inputs['post_ln_g'] = 1.0 + nrm((DEPTH, 2, d), 0.02)
    inputs['post_ln_b'] = nrm((DEPTH, 2, d), 0.02)
    inputs['mix_w_in'] = nrm((N_EVEN, d, IN_TOTAL), d ** -0.5)
    inputs['ssd_conv_w'] = nrm((N_EVEN, SSD_CONV, SSD_XBC), SSD_CONV ** -0.5)
    inputs['ssd_conv_b'] = nrm((N_EVEN, SSD_XBC), 0.02)
    dt0 = jnp.exp(unif((N_EVEN, 2, SSD_HEADS), math.log(1e-3), math.log(1e-1)))
    inputs['ssd_dt_bias'] = dt0 + jnp.log(-jnp.expm1(-dt0))
    inputs['ssd_a_log'] = jnp.log(unif((N_EVEN, 2, SSD_HEADS), 1.0, 16.0))
    inputs['ssd_d'] = 1.0 + nrm((N_EVEN, SSD_HEADS), 0.02)
    inputs['ssd_norm_w'] = 1.0 + nrm((N_EVEN, SSD_INNER), 0.02)
    inputs['hg_lb_raw'] = nrm((N_EVEN, HG_INNER_K), 0.5)
    inputs['hg_norm_w'] = 1.0 + nrm((N_EVEN, HG_INNER_V), 0.02)
    inputs['mix_w_out'] = nrm((N_EVEN, MIX_OUT, d), MIX_OUT ** -0.5 * BETA)
    inputs['conf_w1'] = nrm((N_ODD, d, 2 * d), d ** -0.5)
    inputs['conf_b1'] = nrm((N_ODD, 2 * d), 0.02)
    inputs['conf_dw_w'] = nrm((N_ODD, CONF_KERNEL, d), CONF_KERNEL ** -0.5)
    inputs['conf_dw_b'] = nrm((N_ODD, d), 0.02)
    inputs['conf_ln_g'] = 1.0 + nrm((N_ODD, d), 0.02)
    inputs['conf_ln_b'] = nrm((N_ODD, d), 0.02)
    inputs['conf_w2'] = nrm((N_ODD, d, d), d ** -0.5 * BETA)
    inputs['conf_b2'] = nrm((N_ODD, d), 0.02)
    inputs['ffn_w_up'] = nrm((DEPTH, d, 2 * D_FF), d ** -0.5)
    inputs['ffn_conv_w'] = nrm((DEPTH, FFN_CONV, FFN_CONV, D_FF), 1.0 / FFN_CONV)
    inputs['ffn_conv_b'] = nrm((DEPTH, D_FF), 0.02)
    inputs['ffn_w_down'] = nrm((DEPTH, D_FF, d), D_FF ** -0.5 * BETA)
    return inputs

def first_block(x, c, ctx, c_ctx, ada_w, ada_b, post_ln_g, post_ln_b, mix_w_in, ssd_conv_w, ssd_conv_b,
              ssd_dt_bias, ssd_a_log, ssd_d, ssd_norm_w, hg_lb_raw, hg_norm_w, mix_w_out,
              conf_w1, conf_b1, conf_dw_w, conf_dw_b, conf_ln_g, conf_ln_b, conf_w2, conf_b2,
              ffn_w_up, ffn_conv_w, ffn_conv_b, ffn_w_down):
    rows = x.shape[1] // GRID_W
    lb_p = jax.nn.softmax(hg_lb_raw.astype(F32), axis=0)
    lb_all = jnp.cumsum(lb_p, axis=0) - lb_p[0]
    s_c = jax.nn.silu(c)
    s_ctx = jax.nn.silu(c_ctx)
    xc = ctx
    for l in range(DEPTH):
        m = (s_c @ ada_w[l] + ada_b[l]).reshape(-1, 6, 1, D_MODEL)
        mc = (s_ctx @ ada_w[l] + ada_b[l]).reshape(6, D_MODEL)
        ctx_next = any(j % 2 == 0 for j in range(l + 1, DEPTH))
        h = modulate(x, m[:, 0], m[:, 1])
        if l % 2 == 0:
            e = l // 2
            hc = modulate(xc, mc[0], mc[1])
            y, yc = even_mixer(h, hc, mix_w_in[e], ssd_conv_w[e], ssd_conv_b[e], ssd_dt_bias[e], ssd_a_log[e],
                               ssd_d[e], ssd_norm_w[e], lb_all[e], e == 0, hg_norm_w[e], mix_w_out[e], ctx_next)
        else:
            o = l // 2
            conf = (conf_w1[o], conf_b1[o], conf_dw_w[o], conf_dw_b[o], conf_ln_g[o], conf_ln_b[o],
                    conf_w2[o], conf_b2[o])
            y = conformer_conv(h, *conf)
            yc = conformer_conv(modulate(xc, mc[0], mc[1]), *conf) if ctx_next else None
        ffn = (ffn_w_up[l], ffn_conv_w[l], ffn_conv_b[l], ffn_w_down[l])
        x = layer_norm(ALPHA * x + m[:, 2] * y, post_ln_g[l, 0], post_ln_b[l, 0])
        x = layer_norm(ALPHA * x + m[:, 5] * conv_glu_ffn(modulate(x, m[:, 3], m[:, 4]), *ffn, rows, GRID_W),
                       post_ln_g[l, 1], post_ln_b[l, 1])
        if ctx_next:
            xc = layer_norm(ALPHA * xc + mc[2] * yc, post_ln_g[l, 0], post_ln_b[l, 0])
            xc = layer_norm(ALPHA * xc + mc[5] * conv_glu_ffn(modulate(xc, mc[3], mc[4]), *ffn, 1, xc.shape[1]),
                            post_ln_g[l, 1], post_ln_b[l, 1])
    return x


_first_inputs = first_inputs


def first_inputs(seed=0):
    import zlib

    import numpy as np

    out = dict(_first_inputs(seed))
    spreads = {}
    factors = {'ctx': 8.0,
     'c_ctx': 5.035,
     'ada_b': 3.002,
     'ssd_conv_b': 8.0,
     'ssd_d': 8.0,
     'ssd_norm_w': 8.0,
     'hg_norm_w': 8.0,
     'conf_b1': 8.0,
     'conf_dw_b': 8.0,
     'conf_ln_g': 8.0,
     'conf_ln_b': 8.0,
     'conf_b2': 6.819,
     'ffn_conv_b': 8.0}
    for name, (base, spread) in spreads.items():
        noise = np.random.default_rng([zlib.crc32(name.encode()), seed]).standard_normal(out[name].shape)
        drawn = base * np.exp(spread * noise) if base else spread * noise
        out[name] = jnp.asarray(drawn.astype(out[name].dtype))
    for name, factor in factors.items():
        out[name] = (out[name] * factor).astype(out[name].dtype)
    return out


_narrow_inputs = first_inputs


def first_inputs(seed=0):
    out = dict(_narrow_inputs(seed))
    wider = {'ssd_conv_b': 4.89,
     'ssd_d': 12.0,
     'ssd_norm_w': 4.44,
     'hg_norm_w': 6.12,
     'conf_ln_g': 4.0,
     'conf_ln_b': 4.11}
    for name, times in wider.items():
        mean = out[name].mean()
        out[name] = (mean + times * (out[name] - mean)).astype(out[name].dtype)
    return out


DEPTH_2 = 1

HEAD_DIM = 64
NSA_HEADS = 6
NSA_KV_HEADS = 2
NSA_GROUP = NSA_HEADS // NSA_KV_HEADS
RWKV_HEADS = 4
MOBA_HEADS = 6
D_NSA = NSA_HEADS * HEAD_DIM
D_NSA_KV = NSA_KV_HEADS * HEAD_DIM
D_RWKV = RWKV_HEADS * HEAD_DIM
D_MOBA = MOBA_HEADS * HEAD_DIM
D_MIX = D_NSA + D_RWKV + D_MOBA

CMP_LEN = 32
CMP_STRIDE = 16
CMP_HIDDEN = 256
SLC_BLOCK = 64
SLC_TOPK = 16
WINDOW = 512
N_BRANCH = 3
RW_DECAY_LORA = 32
RW_AAA_LORA = 32
RW_GATE_LORA = 64
RW_DECAY_SCALE = 0.606531
RW_LN_EPS = 64e-5
MOBA_BLOCK = 256
MOBA_TOPK = 3
CONV_WIDTH = 3
Q_CHUNK = 128
NORM_EPS = 1e-6
BIG = 1e9

N_IN_NSA = D_NSA + 6 * D_NSA_KV + NSA_HEADS * N_BRANCH
N_IN_RWKV = 3 * D_RWKV + RW_DECAY_LORA + RW_AAA_LORA + RW_GATE_LORA
N_IN_MOBA = 3 * D_MOBA
N_IN = N_IN_NSA + N_IN_RWKV + N_IN_MOBA


def _rmsnorm(x, g):
    xf = x.astype(jnp.float32)
    y = xf * lax.rsqrt(jnp.mean(xf * xf, axis=-1, keepdims=True) + NORM_EPS)
    return (y * g.astype(jnp.float32)).astype(x.dtype)

def _head_rmsnorm(o, g):
    b, s, d = o.shape
    oh = o.reshape(b, s, d // HEAD_DIM, HEAD_DIM)
    return _rmsnorm(oh, g.reshape(d // HEAD_DIM, HEAD_DIM)).reshape(b, s, d)

def _masked_softmax(s, mask):
    s = jnp.where(mask, s.astype(jnp.float32), -jnp.inf)
    m = jnp.max(s, axis=-1, keepdims=True)
    m = jnp.where(jnp.isfinite(m), m, 0.0)
    p = jnp.exp(s - m)
    return p / jnp.maximum(jnp.sum(p, axis=-1, keepdims=True), 1e-30)

def _split_2(a, sizes):
    return jnp.split(a, [int(i) for i in np.cumsum(sizes)[:-1]], axis=-1)

def _nsa_compress(kv, pos, w1, w2):
    b, s, g, d = kv.shape
    n_cmp = (s - CMP_LEN) // CMP_STRIDE + 1
    idx = np.arange(n_cmp)[:, None] * CMP_STRIDE + np.arange(CMP_LEN)[None, :]
    blk = kv[:, idx] + pos[:, None, :]
    blk = jnp.transpose(blk, (0, 3, 1, 2, 4)).reshape(b, g, n_cmp, CMP_LEN * d)
    return jax.nn.gelu(blk @ w1) @ w2

def _cmp_to_slc(n_cmp, n_slc):
    r = SLC_BLOCK // CMP_STRIDE
    c = CMP_LEN // CMP_STRIDE
    i = (r * np.arange(n_slc)[:, None, None] - np.arange(r)[None, :, None] - np.arange(c)[None, None, :]).reshape(n_slc, -1)
    m = (i[:, :, None] == np.arange(n_cmp)[None, None, :]).sum(1)
    return jnp.asarray(m.T, jnp.float32)

def _nsa_mixer(p, cmp_pos, cmp_w1, cmp_w2):
    b, s, _ = p.shape
    q, kc, vc, ks, vs, kw, vw, gt = _split_2(p, [D_NSA] + [D_NSA_KV] * 6 + [NSA_HEADS * N_BRANCH])
    kvh = lambda t: t.reshape(b, s, NSA_KV_HEADS, HEAD_DIM)
    hf = lambda t: jnp.transpose(kvh(t), (0, 2, 1, 3))
    q = jnp.transpose(q.reshape(b, s, NSA_KV_HEADS, NSA_GROUP, HEAD_DIM), (0, 2, 3, 1, 4))
    gt = jnp.transpose(jax.nn.sigmoid(gt.reshape(b, s, NSA_KV_HEADS, NSA_GROUP, N_BRANCH)), (0, 2, 3, 1, 4))
    kc = _nsa_compress(kvh(kc), cmp_pos[0], cmp_w1[0], cmp_w2[0])
    vc = _nsa_compress(kvh(vc), cmp_pos[1], cmp_w1[1], cmp_w2[1])
    n_cmp = kc.shape[2]
    n_slc = s // SLC_BLOCK
    k_slc = min(SLC_TOPK, n_slc)
    ks = hf(ks).reshape(b, NSA_KV_HEADS, n_slc, SLC_BLOCK, HEAD_DIM)
    vs = hf(vs).reshape(b, NSA_KV_HEADS, n_slc, SLC_BLOCK, HEAD_DIM)
    kw = jnp.pad(hf(kw), ((0, 0), (0, 0), (WINDOW, 0), (0, 0)))
    vw = jnp.pad(hf(vw), ((0, 0), (0, 0), (WINDOW, 0), (0, 0)))
    cmp_map = _cmp_to_slc(n_cmp, n_slc)
    cmp_end = jnp.asarray(np.arange(n_cmp) * CMP_STRIDE + CMP_LEN - 1)
    blk_id = jnp.arange(n_slc)
    bi = jnp.arange(b)[:, None, None, None]
    gi = jnp.arange(NSA_KV_HEADS)[None, :, None, None]
    scale = HEAD_DIM ** -0.5

    def chunk(c):
        t0 = c * Q_CHUNK
        tpos = t0 + jnp.arange(Q_CHUNK)
        qc = lax.dynamic_slice_in_dim(q, t0, Q_CHUNK, axis=3)
        gc = lax.dynamic_slice_in_dim(gt, t0, Q_CHUNK, axis=3)
        pc = _masked_softmax(jnp.einsum('bgrqd,bgnd->bgrqn', qc, kc) * scale, cmp_end[None, :] <= tpos[:, None])
        oc = jnp.einsum('bgrqn,bgnd->bgrqd', pc.astype(vc.dtype), vc)
        imp = jnp.einsum('bgrqn,nj->bgqj', pc, cmp_map)
        cur = tpos // SLC_BLOCK
        forced = (blk_id[None, :] == 0) | (blk_id[None, :] == cur[:, None]) | (blk_id[None, :] == cur[:, None] - 1)
        causal = blk_id[None, :] * SLC_BLOCK <= tpos[:, None]
        imp = jnp.where(forced, BIG, jnp.where(causal, imp, -BIG))
        _, sel = lax.top_k(imp, k_slc)
        kg = ks[bi, gi, sel].reshape(b, NSA_KV_HEADS, Q_CHUNK, k_slc * SLC_BLOCK, HEAD_DIM)
        vg = vs[bi, gi, sel].reshape(b, NSA_KV_HEADS, Q_CHUNK, k_slc * SLC_BLOCK, HEAD_DIM)
        kpos = (sel[..., None] * SLC_BLOCK + jnp.arange(SLC_BLOCK)).reshape(b, NSA_KV_HEADS, Q_CHUNK, k_slc * SLC_BLOCK)
        ps = _masked_softmax(jnp.einsum('bgrqd,bgqkd->bgrqk', qc, kg) * scale, (kpos <= tpos[:, None])[:, :, None])
        osl = jnp.einsum('bgrqk,bgqkd->bgrqd', ps.astype(vg.dtype), vg)
        kwc = lax.dynamic_slice_in_dim(kw, t0, Q_CHUNK + WINDOW, axis=2)
        vwc = lax.dynamic_slice_in_dim(vw, t0, Q_CHUNK + WINDOW, axis=2)
        wpos = t0 - WINDOW + jnp.arange(Q_CHUNK + WINDOW)
        dist = tpos[:, None] - wpos[None, :]
        mw = (dist >= 0) & (dist < WINDOW) & (wpos[None, :] >= 0)
        pw = _masked_softmax(jnp.einsum('bgrqd,bgkd->bgrqk', qc, kwc) * scale, mw)
        ow = jnp.einsum('bgrqk,bgkd->bgrqd', pw.astype(vwc.dtype), vwc)
        return gc[..., 0:1] * oc + gc[..., 1:2] * osl + gc[..., 2:3] * ow

    o = lax.map(chunk, jnp.arange(s // Q_CHUNK))
    return jnp.transpose(o, (1, 0, 4, 2, 3, 5)).reshape(b, s, D_NSA)

def _rwkv7_mixer(p, mu, w0, w2, a0, a2, g2, k_k, k_a, r_k, lnx_w, lnx_b):
    b, s, _ = p.shape
    f32 = jnp.float32
    p_prev = jnp.pad(p, ((0, 0), (1, 0), (0, 0)))[:, :-1]
    p = p + (p_prev - p) * mu
    r, k, v, xw, xa, xg = _split_2(p, [D_RWKV] * 3 + [RW_DECAY_LORA, RW_AAA_LORA, RW_GATE_LORA])
    w = jnp.exp(-RW_DECAY_SCALE * jax.nn.sigmoid((w0 + jnp.tanh(xw) @ w2).astype(f32)))
    a = jax.nn.sigmoid(a0 + xa @ a2)
    g = jax.nn.sigmoid(xg) @ g2
    heads = lambda t: t.reshape(b, s, RWKV_HEADS, HEAD_DIM).astype(f32)
    kk = heads(k * k_k)
    kk = kk / jnp.maximum(jnp.sqrt(jnp.sum(kk * kk, axis=-1, keepdims=True)), 1e-12)
    k = k * (1.0 + (a - 1.0) * k_a)
    r_h, w_h, k_h, v_h, a_h = heads(r), heads(w), heads(k), heads(v), heads(a)

    def step(state, inp):
        r_t, w_t, k_t, v_t, kk_t, a_t = inp
        sa = jnp.einsum('bhvk,bhk->bhv', state, -kk_t)
        state = state * w_t[:, :, None, :] + sa[..., None] * (kk_t * a_t)[:, :, None, :] + v_t[..., None] * k_t[:, :, None, :]
        return state, jnp.einsum('bhvk,bhk->bhv', state, r_t)

    xs = tuple(jnp.moveaxis(t, 1, 0) for t in (r_h, w_h, k_h, v_h, kk, a_h))
    _, out = lax.scan(step, jnp.zeros((b, RWKV_HEADS, HEAD_DIM, HEAD_DIM), f32), xs)
    out = jnp.moveaxis(out, 0, 1)
    mean = jnp.mean(out, axis=-1, keepdims=True)
    var = jnp.mean(jnp.square(out - mean), axis=-1, keepdims=True)
    out = ((out - mean) * lax.rsqrt(var + RW_LN_EPS)).reshape(b, s, D_RWKV) * lnx_w + lnx_b
    bonus = jnp.sum(r_h * k_h * r_k, axis=-1, keepdims=True) * v_h
    out = (out + bonus.reshape(b, s, D_RWKV)) * g
    return out.astype(p.dtype)

def _moba_mixer(p):
    b, s, _ = p.shape
    q, k, v = [jnp.transpose(t.reshape(b, s, MOBA_HEADS, HEAD_DIM), (0, 2, 1, 3)) for t in _split_2(p, [D_MOBA] * 3)]
    n_blk = -(-s // MOBA_BLOCK)
    pad = n_blk * MOBA_BLOCK - s
    k = jnp.pad(k, ((0, 0), (0, 0), (0, pad), (0, 0)))
    v = jnp.pad(v, ((0, 0), (0, 0), (0, pad), (0, 0)))
    kb = k.reshape(b, MOBA_HEADS, n_blk, MOBA_BLOCK, HEAD_DIM)
    vb = v.reshape(b, MOBA_HEADS, n_blk, MOBA_BLOCK, HEAD_DIM)
    kmean = jnp.mean(kb.astype(jnp.float32), axis=3)
    n_sel = min(MOBA_TOPK, max(n_blk - 1, 1))
    n_g = n_sel * MOBA_BLOCK
    blk_id = jnp.arange(n_blk)
    bi = jnp.arange(b)[:, None, None, None]
    hi = jnp.arange(MOBA_HEADS)[None, :, None, None]
    scale = HEAD_DIM ** -0.5

    def chunk(c):
        t0 = c * Q_CHUNK
        tpos = t0 + jnp.arange(Q_CHUNK)
        cur = t0 // MOBA_BLOCK
        qc = lax.dynamic_slice_in_dim(q, t0, Q_CHUNK, axis=2)
        gate = jnp.einsum('bhqd,bhnd->bhqn', qc.astype(jnp.float32), kmean)
        gate = jnp.where(blk_id < cur, gate, -jnp.inf)
        _, sel = lax.top_k(gate, n_sel)
        kg = kb[bi, hi, sel].reshape(b, MOBA_HEADS, Q_CHUNK, n_g, HEAD_DIM)
        vg = vb[bi, hi, sel].reshape(b, MOBA_HEADS, Q_CHUNK, n_g, HEAD_DIM)
        mg = jnp.repeat(sel < cur, MOBA_BLOCK, axis=-1)
        ko = lax.dynamic_slice_in_dim(k, cur * MOBA_BLOCK, MOBA_BLOCK, axis=2)
        vo = lax.dynamic_slice_in_dim(v, cur * MOBA_BLOCK, MOBA_BLOCK, axis=2)
        mo = (cur * MOBA_BLOCK + jnp.arange(MOBA_BLOCK))[None, :] <= tpos[:, None]
        s_g = jnp.einsum('bhqd,bhqkd->bhqk', qc, kg)
        s_o = jnp.einsum('bhqd,bhkd->bhqk', qc, ko)
        mask = jnp.concatenate([mg, jnp.broadcast_to(mo, s_o.shape)], axis=-1)
        prob = _masked_softmax(jnp.concatenate([s_g, s_o], axis=-1) * scale, mask).astype(v.dtype)
        return jnp.einsum('bhqk,bhqkd->bhqd', prob[..., :n_g], vg) + jnp.einsum('bhqk,bhkd->bhqd', prob[..., n_g:], vo)

    o = lax.map(chunk, jnp.arange(s // Q_CHUNK))
    return jnp.transpose(o, (1, 0, 3, 2, 4)).reshape(b, s, D_MOBA)

def _conv_glu(h, w_in, conv_w, conv_b, w_out):
    u, gt = jnp.split(h @ w_in, 2, axis=-1)
    gt = lax.conv_general_dilated(gt, conv_w[:, None, :], window_strides=(1,), padding=[(CONV_WIDTH - 1, 0)], dimension_numbers=('NWC', 'WIO', 'NWC'), feature_group_count=D_FF) + conv_b
    return (jax.nn.silu(gt) * u) @ w_out

def second_inputs(seed: int = 0) -> dict:
    key = jax.random.key(seed)
    ks = iter(jax.random.split(key, 32))
    nrm = lambda shape, sc: jax.random.normal(next(ks), shape, jnp.float32) * sc
    gain = lambda shape: 1.0 + nrm(shape, 0.02)
    L = DEPTH_2
    resid = (2 * DEPTH_2) ** -0.5
    return {
        'x': nrm((BATCH, SEQ, D_MODEL), 1.0),
        'attn_norm': gain((L, D_MODEL)),
        'w_in': nrm((L, D_MODEL, N_IN), D_MODEL ** -0.5),
        'nsa_cmp_pos': nrm((L, 2, CMP_LEN, HEAD_DIM), 0.1),
        'nsa_cmp_w1': nrm((L, 2, CMP_LEN * HEAD_DIM, CMP_HIDDEN), (CMP_LEN * HEAD_DIM) ** -0.5),
        'nsa_cmp_w2': nrm((L, 2, CMP_HIDDEN, HEAD_DIM), CMP_HIDDEN ** -0.5),
        'nsa_out_gain': gain((L, D_NSA)),
        'rw_mu': jax.random.uniform(next(ks), (L, N_IN_RWKV), jnp.float32),
        'rw_w0': nrm((L, D_RWKV), 0.5),
        'rw_w2': nrm((L, RW_DECAY_LORA, D_RWKV), 0.5 * RW_DECAY_LORA ** -0.5),
        'rw_a0': nrm((L, D_RWKV), 0.5),
        'rw_a2': nrm((L, RW_AAA_LORA, D_RWKV), 0.5 * RW_AAA_LORA ** -0.5),
        'rw_g2': nrm((L, RW_GATE_LORA, D_RWKV), RW_GATE_LORA ** -0.5),
        'rw_k_k': 1.0 + nrm((L, D_RWKV), 0.1),
        'rw_k_a': 1.0 + nrm((L, D_RWKV), 0.1),
        'rw_r_k': nrm((L, RWKV_HEADS, HEAD_DIM), 0.1),
        'rw_lnx_w': gain((L, D_RWKV)),
        'rw_lnx_b': nrm((L, D_RWKV), 0.01),
        'moba_out_gain': gain((L, D_MOBA)),
        'w_out': nrm((L, D_MIX, D_MODEL), D_MIX ** -0.5 * resid),
        'ffn_norm': gain((L, D_MODEL)),
        'ffn_w_in': nrm((L, D_MODEL, 2 * D_FF), D_MODEL ** -0.5),
        'ffn_conv_w': nrm((L, CONV_WIDTH, D_FF), CONV_WIDTH ** -0.5),
        'ffn_conv_b': nrm((L, D_FF), 0.01),
        'ffn_w_out': nrm((L, D_FF, D_MODEL), D_FF ** -0.5 * resid),
        'final_norm': gain((D_MODEL,)),
    }

def second_block(x, attn_norm, w_in, nsa_cmp_pos, nsa_cmp_w1, nsa_cmp_w2, nsa_out_gain, rw_mu, rw_w0, rw_w2, rw_a0, rw_a2, rw_g2, rw_k_k, rw_k_a, rw_r_k, rw_lnx_w, rw_lnx_b, moba_out_gain, w_out, ffn_norm, ffn_w_in, ffn_conv_w, ffn_conv_b, ffn_w_out, final_norm):
    for l in range(DEPTH_2):
        h = _rmsnorm(x, attn_norm[l])
        proj = h @ w_in[l]
        p_nsa, p_rw, p_moba = _split_2(proj, [N_IN_NSA, N_IN_RWKV, N_IN_MOBA])
        o_nsa = _head_rmsnorm(_nsa_mixer(p_nsa, nsa_cmp_pos[l], nsa_cmp_w1[l], nsa_cmp_w2[l]), nsa_out_gain[l])
        o_rw = _rwkv7_mixer(p_rw, rw_mu[l], rw_w0[l], rw_w2[l], rw_a0[l], rw_a2[l], rw_g2[l], rw_k_k[l], rw_k_a[l], rw_r_k[l], rw_lnx_w[l], rw_lnx_b[l])
        o_moba = _head_rmsnorm(_moba_mixer(p_moba), moba_out_gain[l])
        x = x + jnp.concatenate([o_nsa, o_rw, o_moba], axis=-1) @ w_out[l]
        x = x + _conv_glu(_rmsnorm(x, ffn_norm[l]), ffn_w_in[l], ffn_conv_w[l], ffn_conv_b[l], ffn_w_out[l])
    return _rmsnorm(x, final_norm)


_first_inputs_2 = second_inputs


def second_inputs(seed=0):
    import zlib

    import numpy as np

    out = dict(_first_inputs_2(seed))
    spreads = {}
    factors = {'attn_norm': 2.959,
     'nsa_out_gain': 6.578,
     'rw_w2': 5.598,
     'rw_k_k': 8.0,
     'rw_k_a': 2.879,
     'rw_lnx_w': 8.0,
     'rw_lnx_b': 8.0,
     'moba_out_gain': 7.339,
     'ffn_norm': 6.102,
     'ffn_conv_b': 8.0,
     'final_norm': 2.808}
    for name, (base, spread) in spreads.items():
        noise = np.random.default_rng([zlib.crc32(name.encode()), seed]).standard_normal(out[name].shape)
        drawn = base * np.exp(spread * noise) if base else spread * noise
        out[name] = __import__('jax').numpy.asarray(drawn.astype(out[name].dtype))
    for name, factor in factors.items():
        out[name] = (out[name] * factor).astype(out[name].dtype)
    return out


_narrow_inputs_2 = second_inputs


def second_inputs(seed=0):

    out = dict(_narrow_inputs_2(seed))
    wider = {'nsa_out_gain': 3.66,
     'rw_k_k': 6.58,
     'rw_lnx_w': 7.02,
     'rw_lnx_b': 12.0,
     'moba_out_gain': 3.67,
     'ffn_conv_b': 5.07,
     'final_norm': 3.15}
    for name, times in wider.items():
        mean = out[name].mean()
        out[name] = (mean + times * (out[name] - mean)).astype(out[name].dtype)
    return out


def setup_inputs(seed=0):
    out = dict(first_inputs(seed))
    for name, value in second_inputs(seed + 1).items():
        if name != "x":
            out[name + "_2"] = value
    return out


def reference(
    x, c, ctx, c_ctx, ada_w, ada_b, post_ln_g, post_ln_b, mix_w_in, ssd_conv_w, ssd_conv_b,
    ssd_dt_bias, ssd_a_log, ssd_d, ssd_norm_w, hg_lb_raw, hg_norm_w, mix_w_out, conf_w1,
    conf_b1, conf_dw_w, conf_dw_b, conf_ln_g, conf_ln_b, conf_w2, conf_b2, ffn_w_up, ffn_conv_w,
    ffn_conv_b, ffn_w_down, attn_norm_2, w_in_2, nsa_cmp_pos_2, nsa_cmp_w1_2, nsa_cmp_w2_2,
    nsa_out_gain_2, rw_mu_2, rw_w0_2, rw_w2_2, rw_a0_2, rw_a2_2, rw_g2_2, rw_k_k_2, rw_k_a_2,
    rw_r_k_2, rw_lnx_w_2, rw_lnx_b_2, moba_out_gain_2, w_out_2, ffn_norm_2, ffn_w_in_2,
    ffn_conv_w_2, ffn_conv_b_2, ffn_w_out_2, final_norm_2,
):
    x = first_block(
        x, c, ctx, c_ctx, ada_w, ada_b, post_ln_g, post_ln_b, mix_w_in, ssd_conv_w, ssd_conv_b,
        ssd_dt_bias, ssd_a_log, ssd_d, ssd_norm_w, hg_lb_raw, hg_norm_w, mix_w_out, conf_w1,
        conf_b1, conf_dw_w, conf_dw_b, conf_ln_g, conf_ln_b, conf_w2, conf_b2, ffn_w_up,
        ffn_conv_w, ffn_conv_b, ffn_w_down,
    )
    return second_block(
        x, attn_norm_2, w_in_2, nsa_cmp_pos_2, nsa_cmp_w1_2, nsa_cmp_w2_2, nsa_out_gain_2,
        rw_mu_2, rw_w0_2, rw_w2_2, rw_a0_2, rw_a2_2, rw_g2_2, rw_k_k_2, rw_k_a_2, rw_r_k_2,
        rw_lnx_w_2, rw_lnx_b_2, moba_out_gain_2, w_out_2, ffn_norm_2, ffn_w_in_2, ffn_conv_w_2,
        ffn_conv_b_2, ffn_w_out_2, final_norm_2,
    )


_drawn_inputs = setup_inputs


def setup_inputs(seed=0):
    import zlib

    import numpy as np

    out = dict(_drawn_inputs(seed))
    spreads = {}
    factors = {'ssd_d': 8.0, 'nsa_cmp_pos_2': 2.858}
    for name, (base, spread) in spreads.items():
        noise = np.random.default_rng([zlib.crc32(name.encode()), seed]).standard_normal(out[name].shape)
        drawn = base * np.exp(spread * noise) if base else spread * noise
        out[name] = jnp.asarray(drawn.astype(out[name].dtype))
    for name, factor in factors.items():
        out[name] = (out[name] * factor).astype(out[name].dtype)
    return out
```

```python
from contextlib import ExitStack, contextmanager


import numpy as np

import concourse.bass as bass
from concourse import mybir

F32 = mybir.dt.float32
U32 = mybir.dt.uint32
ALU = mybir.AluOpType
ACT = mybir.ActivationFunctionType
AX_X = mybir.AxisListType.X

P = 128
D = 1024
DT = D // P
SEQ = 512
CTX = 256
TOK = SEQ + CTX
DEPTH = 2
ALPHA = (2 * DEPTH) ** 0.25
EPS = 1e-5
D_FF = 2816
FT = D_FF // P
GRID_W = 64
ROWS = SEQ // GRID_W

SSD_HEADS = 16
SSD_P = 64
SSD_IN = SSD_HEADS * SSD_P
SSD_G = 2
SSD_N = 128
SSD_XBC = SSD_IN + 2 * SSD_G * SSD_N
SSD_K = 5
HG_HEADS = 8
MIX_AT = {}
at = 0
for part, size in (("z", SSD_IN), ("xbc", SSD_XBC), ("dt", 2 * SSD_HEADS), ("q", D), ("f", 2 * D), ("v", D), ("g", D)):
    MIX_AT[part] = at
    at += size
CONF_K = 31
CHUNK = 128
NEG = -1e30

HD = 64
NSA_H, KV_H, RW_H, MOBA_H = 6, 2, 4, 6
NORM_EPS = 1e-6
RW_C = 64
RW_DECAY = 0.606531
RW_LN_EPS = 64e-5
CMP_LEN, CMP_STRIDE, CMP_HID = 32, 16, 256
N_CMP = (SEQ - CMP_LEN) // CMP_STRIDE + 1
TT = SEQ // P
AT2 = {}
at = 0
for part, size in (("q", 384), ("kc", 128), ("vc", 128), ("ks", 128), ("vs", 128), ("kw", 128), ("vw", 128), ("gt", 18),
                   ("rw", 896), ("mq", 384), ("mk", 384), ("mv", 384)):
    AT2[part] = at
    at += size

LEVELS = [CHUNK >> (n + 1) for n in range(7)]
CONST = ["ident", "ones", "head_ones", "until", "since", "neg_until", "neg_since"]
CONST += [f"left_right_{m}" for m in LEVELS] + [f"right_left_{m}" for m in LEVELS]
CONST += ["rw_masks", "rw_level_1_2", "rw_level_4_8", "rw_level_16_32", "rw_levelT_1_2", "rw_levelT_4_8",
          "rw_levelT_16_32", "cmp_mask", "cmp_valid", "rw_eye"]
CONST_AT = {name: n for n, name in enumerate(CONST)}

COLS = {
    "ada_b0": (1, 6 * D), "ada_b1": (1, 6 * D), "post_ln_g": (4, D), "post_ln_b": (4, D), "ssd_conv_w": (SSD_K, SSD_XBC), "ssd_conv_b": (1, SSD_XBC),
    "ssd_norm_w": (1, D), "hg_norm_w": (1, D), "conf_b1": (2, D), "conf_dw_w": (CONF_K, D), "conf_dw_b": (1, D),
    "conf_ln_g": (1, D), "conf_ln_b": (1, D), "conf_b2": (1, D), "ffn_conv_w0": (9, D_FF), "ffn_conv_w1": (9, D_FF),
    "ffn_conv_b": (2, D_FF), "attn_norm": (1, D), "ffn_norm": (1, D), "final_norm": (1, D), "ffn2_conv_w": (3, D_FF),
    "ffn2_conv_b": (1, D_FF), "rw_mu": (1, 896), "rw_w0": (1, 256), "rw_a0": (1, 256), "rw_k_k": (1, 256),
    "rw_k_a": (1, 256), "rw_r_k": (1, 256), "rw_lnx_w": (1, 256), "rw_lnx_b": (1, 256), "nsa_gain": (1, 384),
    "moba_gain": (1, 384), "c": (2, D),
}
COL_AT = {}
at = 0
for name, (rows, length) in COLS.items():
    COL_AT[name] = at
    at += rows * length // P
N_COLS = at


def constants():
    s, t = np.meshgrid(np.arange(P), np.arange(P), indexing="ij")
    out = {
        "ident": s == t, "ones": s >= 0, "head_ones": s // HD == t // HD, "until": s <= t, "since": s >= t,
        "neg_until": np.where(s <= t, 0, NEG), "neg_since": np.where(s >= t, 0, NEG),
    }
    for m in LEVELS:
        lr = (s // (2 * m) == t // (2 * m)) & (s % (2 * m) < m) & (t % (2 * m) >= m)
        out[f"left_right_{m}"], out[f"right_left_{m}"] = lr, lr.T
    s, t = np.meshgrid(np.arange(P) % RW_C, np.arange(RW_C), indexing="ij")
    out["rw_masks"] = np.concatenate([s < t, s <= t], axis=1)

    def below(m, a, b):
        return (a // (2 * m) == b // (2 * m)) & (a % (2 * m) >= m) & (b % (2 * m) < m)

    for m in (1, 4, 16):
        out[f"rw_level_{m}_{2 * m}"] = np.concatenate([below(m, s, t), below(2 * m, s, t)], axis=1)
        out[f"rw_levelT_{m}_{2 * m}"] = np.concatenate([below(m, t, s), below(2 * m, t, s)], axis=1)
    out["rw_eye"] = np.concatenate([s == t, s > t], axis=1)
    tok = np.arange(P)[:, None, None] + P * np.arange(TT)[None, :, None]
    seen = CMP_STRIDE * np.arange(N_CMP + 1)[None, None, :] + CMP_LEN - 1 <= tok
    seen[:, :, N_CMP:] = False
    out["cmp_mask"] = np.where(seen, 0, NEG).reshape(P, P)
    out["cmp_valid"] = np.broadcast_to(seen.any(axis=2, keepdims=True), seen.shape).reshape(P, P)
    return np.stack([out[n].astype(np.float32) for n in CONST], axis=1)


def columns(arrays):
    out = []
    for name, (rows, length) in COLS.items():
        a = np.reshape(arrays[name], (rows, length // P, P))
        out.append(np.transpose(a, (2, 1, 0)).reshape(P, -1))
    return np.ascontiguousarray(np.concatenate(out, axis=1))


class Core:

    def __init__(self, nc, ctx):
        self.nc = nc
        self.stages = self.rooms = 0
        self.banks = [ctx.enter_context(nc.psum_tensor(f"bank{i}", [P, SEQ], F32)) for i in range(8)]
        self.const_sb = ctx.enter_context(nc.sbuf_tensor("const_sb", [P, len(CONST), P], F32))
        self.cols_sb = ctx.enter_context(nc.sbuf_tensor("cols_sb", [P, N_COLS], F32))

    def const(self, name):
        return self.const_sb[:, CONST_AT[name], :]

    def col(self, name, tile, row=0):
        start = COL_AT[name] + tile * COLS[name][0] + row
        return self.cols_sb[:, bass.ds(start, 1)]

    @contextmanager
    def room(self, **shapes):
        self.rooms += 1
        n = self.rooms
        with ExitStack() as ctx:
            yield [ctx.enter_context(self.nc.sbuf_tensor(f"{name}_{n}", shape, F32)) for name, shape in shapes.items()]

    @contextmanager
    def stage(self, *names):
        self.stages += 1
        with self.nc.cleanup_on_exit():
            sems = [self.nc.alloc_semaphore(f"{n}_{self.stages}") for n in names]
            with self.nc.Block() as block:
                yield [block, *sems]


def gemm(core, name, weights, acts, spans, out, tiles, unroll, bias=None, func=ACT.Identity):
    kt = weights.shape[0] // P
    w = weights.rearrange("(k p) f -> p k f", p=P)
    steps = tiles // unroll
    assert steps * unroll == tiles and unroll * len(spans) <= 8
    names = [f"slab_in{u}" for u in range(unroll)] + ["tile_done", "banks_free", "slots_refilled"]
    with core.room(**{f"{name}_ring": [P, unroll, kt, P]}) as (ring,), core.stage(*names) as (block, *sems):
        slab_in, (tile_done, banks_free, slots_refilled) = sems[:unroll], sems[unroll:]

        def bank(u, n):
            return core.banks[u * len(spans) + n][:, 0:spans[n][1]]

        @block.sync
        def _(sp):
            for u in range(unroll):
                sp.dma_start(ring[:, u], w[:, :, u * P:(u + 1) * P]).then_inc(slab_in[u], 16)
            if steps > 1:
                with sp.Fori(1, steps) as i:
                    for u in range(unroll):
                        feature = sp.snap((i * unroll + u) * P)
                        sp.wait_ge(tile_done, (i - 1) * unroll + u + 1)
                        sp.sem_inc(slots_refilled, 1)
                        sp.dma_start(ring[:, u], w[:, :, bass.ds(feature, P)]).then_inc(slab_in[u], 16)

        @block.tensor
        def _(pe):
            with pe.Fori(0, steps) as i:
                for u in range(unroll):
                    pe.wait_ge(slab_in[u], (i + 1) * 16)
                    pe.wait_ge(banks_free, i * unroll + u + 1)
                    for n, (start, size) in enumerate(spans):
                        for k in range(kt):
                            mm = pe.matmul(bank(u, n), ring[:, u, k, :], acts[:, k, start:start + size],
                                           start=(k == 0), stop=(k == kt - 1))
                    mm.then_inc(tile_done, 1)

        @block.scalar
        def _(act):
            act.sem_inc(banks_free, unroll)
            with act.Fori(0, steps) as i:
                for u in range(unroll):
                    act.wait_ge(tile_done, i * unroll + u + 1)
                    tile = i * unroll + u
                    for n in range(len(spans)):
                        b = bias(tile) if bias else 0.0
                        done = act.activation(out(tile, n), bank(u, n), func, bias=b)
                    done.then_inc(banks_free, 1)


def gemm_tokens(core, name, weights, acts, tiles, out, width, bias=None):
    kt = weights.shape[0] // P
    w = weights.rearrange("(k p) f -> p k f", p=P)
    slabs = weights.shape[1] // width
    with core.room(**{f"{name}_ring": [P, min(slabs, 2), kt, width]}) as (ring,), \
            core.stage("slab_in0", "slab_in1", "tile_done", "banks_free") as (block, slab_in0, slab_in1, tile_done, banks_free):
        slab_in = [slab_in0, slab_in1]

        @block.sync
        def _(sp):
            for s in range(slabs):
                if s >= 2:
                    sp.wait_ge(tile_done, (s - 1) * tiles)
                sp.dma_start(ring[:, s % 2], w[:, :, s * width:(s + 1) * width]).then_inc(slab_in[s % 2], 16)

        @block.tensor
        def _(pe):
            for s in range(slabs):
                pe.wait_ge(slab_in[s % 2], 16 * (s // 2 + 1))
                for t in range(tiles):
                    n = s * tiles + t
                    if n >= 8:
                        pe.wait_ge(banks_free, n - 7)
                    for k in range(kt):
                        mm = pe.matmul(core.banks[n % 8][:, 0:width], acts[:, k, t * P:(t + 1) * P], ring[:, s % 2, k, :],
                                       start=(k == 0), stop=(k == kt - 1))
                    mm.then_inc(tile_done, 1)

        @block.scalar
        def _(act):
            for n in range(slabs * tiles):
                act.wait_ge(tile_done, n + 1)
                act.activation(out(n % tiles, n // tiles), core.banks[n % 8][:, 0:width], ACT.Identity)\
                   .then_inc(banks_free, 1)


def modulate(core, x, shift, scale1, out):
    with core.stage("modulated") as (block, modulated):
        @block.vector
        def _(dve):
            for k in range(DT):
                dve.tensor_scalar(out[:, k, :], x[:, k, :], scale1(k), shift(k), ALU.mult, ALU.add).then_inc(modulated, 1)


def residual(core, x, y, gate):
    with core.stage("scaled") as (block, scaled):
        if gate is None:
            @block.vector
            def _(dve):
                for k in range(DT):
                    dve.tensor_tensor(x[:, k, :], x[:, k, :], y[:, k, :], ALU.add)
            return

        @block.scalar
        def _(act):
            for k in range(DT):
                act.activation(x[:, k, :], x[:, k, :], ACT.Identity, scale=ALPHA).then_inc(scaled, 1)

        @block.vector
        def _(dve):
            for k in range(DT):
                dve.wait_ge(scaled, k + 1)
                dve.scalar_tensor_tensor(out=x[:, k, :], in0=y[:, k, :], scalar=gate(k), in1=x[:, k, :],
                                         op0=ALU.mult, op1=ALU.add)


def norm(core, name, src, out, gain, bias=None, eps=EPS, center=True, func=ACT.Identity):
    total, squares = core.banks[0], core.banks[1]
    ones = core.const("ones")
    with core.room(**{f"{name}_sq": [P, DT, SEQ], f"{name}_mean": [P, SEQ], f"{name}_rstd": [P, SEQ]}) as (sq, mean, rstd), \
            core.stage("summed", "mean_done", "centered", "squared", "sq_summed", "var_done", "root_done", "inverse_done",
                       "scaled") as (block, summed, mean_done, centered, squared, sq_summed, var_done, root_done,
                                     inverse_done, scaled):
        @block.tensor
        def _(pe):
            if center:
                for k in range(DT):
                    mm = pe.matmul(total[:, :], ones, src[:, k, :], start=(k == 0), stop=(k == DT - 1))
                mm.then_inc(summed, 1)
            for k in range(DT):
                pe.wait_ge(squared, k + 1)
                mm = pe.matmul(squares[:, :], ones, sq[:, k, :], start=(k == 0), stop=(k == DT - 1))
            mm.then_inc(sq_summed, 1)

        @block.vector
        def _(dve):
            if center:
                dve.wait_ge(summed, 1)
                dve.tensor_scalar(mean[:, :], total[:, :], 1.0 / D, None, ALU.mult).then_inc(mean_done, 1)
                dve.wait_ge(mean_done, 1)
                for k in range(DT):
                    dve.tensor_tensor(out[:, k, :], src[:, k, :], mean[:, :], ALU.subtract).then_inc(centered, 1)
            dve.wait_ge(sq_summed, 1)
            dve.tensor_scalar(rstd[:, :], squares[:, :], 1.0 / D, eps, ALU.mult, ALU.add).then_inc(var_done, 1)
            dve.wait_ge(root_done, 1)
            dve.reciprocal(rstd[:, :], rstd[:, :]).then_inc(inverse_done, 1)
            dve.wait_ge(inverse_done, 1)
            for k in range(DT):
                dve.scalar_tensor_tensor(out=out[:, k, :], in0=(out if center else src)[:, k, :], scalar=gain(k),
                                         in1=rstd[:, :], op0=ALU.mult, op1=ALU.mult).then_inc(scaled, 1)

        @block.scalar
        def _(act):
            for k in range(DT):
                if center:
                    act.wait_ge(centered, k + 1)
                act.activation(sq[:, k, :], (out if center else src)[:, k, :], ACT.Square).then_inc(squared, 1)
            act.wait_ge(var_done, 1)
            act.activation(rstd[:, :], rstd[:, :], ACT.Sqrt).then_inc(root_done, 1)
            if bias is not None:
                for k in range(DT):
                    act.wait_ge(scaled, k + 1)
                    act.activation(out[:, k, :], out[:, k, :], func, bias=bias(k))


def glu_ffn(core, name, w_up, gate_at, value_at, w_down, x, y, width, interior, taps, conv_w, conv_b, func):
    with core.room(**{f"{name}_h": [P, FT, SEQ]}) as (h,):
        w = w_up.rearrange("(k p) f -> p k f", p=P)
        with core.room(**{f"{name}_ring": [P, 4, DT, P], f"{name}_pad": [P, 2, width], f"{name}_acc": [P, 2, SEQ],
                          f"{name}_val": [P, 2, SEQ]}) as (ring, pad, acc, val), \
                core.stage("slab_in0", "slab_in1", "slab_in2", "slab_in3", "tile_done", "banks_free",
                           "tapped0", "tapped1", "active", "values_free", "slots_refilled") as (
                    block, slab_in0, slab_in1, slab_in2, slab_in3, tile_done, banks_free, tapped0,
                    tapped1, active, values_free, slots_refilled):
            slab_in = [slab_in0, slab_in1, slab_in2, slab_in3]
            tapped = [tapped0, tapped1]
            steps = FT // 2

            def slab_at(i, u):
                return (2 * i + u // 2) * P + (gate_at, value_at)[u % 2]

            @block.sync
            def _(sp):
                for u in range(4):
                    sp.dma_start(ring[:, u], w[:, :, bass.ds(slab_at(0, u), P)]).then_inc(slab_in[u], 16)
                with sp.Fori(1, steps) as i:
                    for u in range(4):
                        feature = sp.snap(slab_at(i, u))
                        sp.wait_ge(tile_done, 4 * (i - 1) + u + 1)
                        sp.sem_inc(slots_refilled, 1)
                        sp.dma_start(ring[:, u], w[:, :, bass.ds(feature, P)]).then_inc(slab_in[u], 16)

            @block.tensor
            def _(pe):
                with pe.Fori(0, steps) as i:
                    for u in range(4):
                        pe.wait_ge(slab_in[u], 16 * (i + 1))
                        pe.wait_ge(banks_free, 4 * i + u + 1)
                        for k in range(DT):
                            mm = pe.matmul(core.banks[u][:, :], ring[:, u, k, :], x[:, k, :],
                                           start=(k == 0), stop=(k == DT - 1))
                        mm.then_inc(tile_done, 1)

            @block.scalar
            def _(act):
                act.sem_inc(banks_free, 4)
                with act.Fori(0, steps) as i:
                    for j in range(2):
                        act.wait_ge(tile_done, 4 * i + 2 * j + 1)
                        act.wait_ge(tapped[j], len(taps) * i + 1)
                        src, dst = core.banks[2 * j][:, :], interior(pad[:, j, :])
                        if len(dst.shape) == 3:
                            src = src.rearrange("p (a b) -> p a b", b=dst.shape[2])
                        act.activation(dst, src, ACT.Identity).then_inc(banks_free, 1)
                        act.wait_ge(tile_done, 4 * i + 2 * j + 2)
                        act.wait_ge(values_free, 2 * i + j + 1)
                        act.activation(val[:, j, :], core.banks[2 * j + 1][:, :], ACT.Identity).then_inc(banks_free, 1)
                    for j in range(2):
                        act.wait_ge(tapped[j], len(taps) * (i + 1) + 1)
                        act.activation(acc[:, j, :], acc[:, j, :], func, bias=conv_b(2 * i + j)).then_inc(active, 1)

            @block.vector
            def _(dve):
                for j in range(2):
                    dve.memset(pad[:, j, :], 0.0).then_inc(tapped[j], 1)
                dve.sem_inc(values_free, 2)
                with dve.Fori(0, steps) as i:
                    for n, tap in enumerate(taps):
                        for j in range(2):
                            if n == 0:
                                dve.wait_ge(banks_free, 4 + 4 * i + 2 * j + 1)
                                dve.wait_ge(values_free, 2 * i + j + 1)
                            src = tap(pad[:, j, :])
                            dst = acc[:, j, :]
                            if len(src.shape) == 3:
                                dst = dst.rearrange("p (a b) -> p a b", b=src.shape[2])
                            dve.wait_ge(tapped[j], len(taps) * i + n + 1)
                            if n == 0:
                                dve.tensor_scalar(dst, src, conv_w(2 * i + j, n), None, ALU.mult).then_inc(tapped[j], 1)
                            else:
                                dve.scalar_tensor_tensor(out=dst, in0=src, scalar=conv_w(2 * i + j, n), in1=dst,
                                                         op0=ALU.mult, op1=ALU.add).then_inc(tapped[j], 1)
                    for j in range(2):
                        dve.wait_ge(active, 2 * i + j + 1)
                        dve.wait_ge(banks_free, 4 + 4 * i + 2 * j + 2)
                        dve.tensor_tensor(h[:, bass.ds(2 * i + j, 1), :], acc[:, j:j + 1, :], val[:, j:j + 1, :], ALU.mult)\
                           .then_inc(values_free, 1)

        gemm(core, f"{name}_down", w_down, h, [(0, SEQ)], lambda tile, n: y[:, bass.ds(tile, 1), :], DT, 4)


GRID_PAD = (ROWS + 2) * (GRID_W + 2)


def grid_window(r, c):
    return lambda b: b.rearrange("p (a b) -> p a b", b=GRID_W + 2)[:, r:r + ROWS, c:c + GRID_W]


GRID_TAPS = [grid_window(r, c) for r in range(3) for c in range(3)]


def conformer(core, w1, w2, x, y):
    half = CONF_K // 2
    w = w1.rearrange("(k p) f -> p k f", p=P)
    with core.room(conf_pad=[P, DT, SEQ + 2 * half], conf_u=[P, DT, SEQ]) as (pad, conv):
        with core.room(conf_ring=[P, 4, DT, P], conf_sig=[P, 2, SEQ]) as (ring, sig), \
                core.stage("slab_in0", "slab_in1", "slab_in2", "slab_in3", "tile_done", "sig_done", "tile_used",
                           "border", "slots_refilled") as (block, slab_in0, slab_in1, slab_in2, slab_in3, tile_done,
                                                           sig_done, tile_used, border, slots_refilled):
            slab_in = [slab_in0, slab_in1, slab_in2, slab_in3]

            def slab_at(i, u):
                return (2 * i + u // 2) * P + (D, 0)[u % 2]

            @block.sync
            def _(sp):
                for u in range(4):
                    sp.dma_start(ring[:, u], w[:, :, bass.ds(slab_at(0, u), P)]).then_inc(slab_in[u], 16)
                with sp.Fori(1, DT // 2) as i:
                    for u in range(4):
                        feature = sp.snap(slab_at(i, u))
                        sp.wait_ge(tile_done, 4 * (i - 1) + u + 1)
                        sp.sem_inc(slots_refilled, 1)
                        sp.dma_start(ring[:, u], w[:, :, bass.ds(feature, P)]).then_inc(slab_in[u], 16)

            @block.tensor
            def _(pe):
                with pe.Fori(0, DT // 2) as i:
                    for u in range(4):
                        pe.wait_ge(slab_in[u], 16 * (i + 1))
                        pe.wait_ge(tile_used, 2 * i + u // 2 + 1)
                        for k in range(DT):
                            mm = pe.matmul(core.banks[u][:, :], ring[:, u, k, :], x[:, k, :],
                                           start=(k == 0), stop=(k == DT - 1))
                        mm.then_inc(tile_done, 1)

            @block.scalar
            def _(act):
                with act.Fori(0, DT // 2) as i:
                    for j in range(2):
                        act.wait_ge(tile_done, 4 * i + 2 * j + 1)
                        act.wait_ge(tile_used, 2 * i + j + 1)
                        act.activation(sig[:, j, :], core.banks[2 * j][:, :], ACT.Sigmoid,
                                       bias=core.col("conf_b1", 2 * i + j, 1)).then_inc(sig_done, 1)

            @block.vector
            def _(dve):
                for k in range(DT):
                    dve.memset(pad[:, k, :], 0.0).then_inc(border, 1)
                dve.sem_inc(tile_used, 2)
                dve.wait_ge(border, DT)
                with dve.Fori(0, DT // 2) as i:
                    for j in range(2):
                        dve.wait_ge(tile_done, 4 * i + 2 * j + 2)
                        dve.wait_ge(sig_done, 2 * i + j + 1)
                        dve.scalar_tensor_tensor(
                            out=pad[:, bass.ds(2 * i + j, 1), half:half + SEQ],
                            in0=core.banks[2 * j + 1][:, :].rearrange("p (a n) -> p a n", a=1),
                            scalar=core.col("conf_b1", 2 * i + j, 0), in1=sig[:, j:j + 1, :],
                            op0=ALU.add, op1=ALU.mult).then_inc(tile_used, 1)

        with core.stage("tapped0", "tapped1") as (block, tapped0, tapped1):
            tapped = [tapped0, tapped1]

            @block.vector
            def _(dve):
                with dve.Fori(0, DT // 2) as i:
                    for n in range(CONF_K):
                        for j in range(2):
                            tile = bass.ds(2 * i + j, 1)
                            src, dst = pad[:, tile, n:n + SEQ], conv[:, tile, :]
                            if n == 0:
                                dve.tensor_scalar(dst, src, core.col("conf_dw_w", 2 * i + j, n),
                                                  core.col("conf_dw_b", 2 * i + j), ALU.mult, ALU.add)\
                                   .then_inc(tapped[j], 1)
                            else:
                                dve.wait_ge(tapped[j], CONF_K * i + n)
                                dve.scalar_tensor_tensor(out=dst, in0=src, scalar=core.col("conf_dw_w", 2 * i + j, n),
                                                         in1=dst, op0=ALU.mult, op1=ALU.add).then_inc(tapped[j], 1)
        norm(core, "conf_ln", conv, conv, lambda k: core.col("conf_ln_g", k), lambda k: core.col("conf_ln_b", k),
             func=ACT.Silu)
        gemm(core, "conf_out", w2, conv, [(0, SEQ)], lambda tile, n: y[:, bass.ds(tile, 1), :], DT, 4,
             bias=lambda tile: core.col("conf_b2", tile))


def spread(ap, axis, count):
    ap = ap.unsqueeze(axis)
    shape = list(ap.shape)
    shape[axis] = count
    return ap.broadcast_to(shape)


LAT_PAD = SEQ + SSD_K - 1
CTX_PAD = CTX + SSD_K - 1
SPANS = [(0, SEQ), (SEQ, CTX)]
XS_T, B_T, C_T = 0, SSD_IN // P, SSD_IN // P + SSD_G
XBC_T = SSD_XBC // P


def ssd_inputs(core, w_in, h, xbc):
    half = SSD_K // 2
    with core.room(xbc_pad=[P, XBC_T, LAT_PAD + CTX_PAD]) as (pad,):
        def inner(tile, n):
            at, size = ((half, SEQ), (LAT_PAD + half, CTX))[n]
            return pad[:, bass.ds(tile, 1), at:at + size]

        with core.stage("border") as (block, border):
            @block.gpsimd
            def _(pool):
                for at, size in ((0, half), (LAT_PAD - half, 2 * half), (LAT_PAD + CTX_PAD - half, half)):
                    pool.memset(pad[:, :, at:at + size], 0.0).then_inc(border, 1)
        gemm(core, "xbc", w_in[:, MIX_AT["xbc"]:MIX_AT["dt"]], h, SPANS, inner, XBC_T, 4)
        with core.stage("lat_tapped", "ctx_tapped") as (block, lat_tapped, ctx_tapped):
            @block.vector
            def _(dve):
                with dve.Fori(0, XBC_T) as i:
                    for n in range(SSD_K):
                        for tapped, at, start, size in ((lat_tapped, 0, 0, SEQ), (ctx_tapped, LAT_PAD, SEQ, CTX)):
                            src = pad[:, bass.ds(i, 1), at + n:at + n + size]
                            dst = xbc[:, bass.ds(i, 1), start:start + size]
                            tap = core.col("ssd_conv_w", i, n)
                            if n == 0:
                                dve.tensor_scalar(dst, src, tap, None, ALU.mult).then_inc(tapped, 1)
                            else:
                                dve.wait_ge(tapped, SSD_K * i + n)
                                dve.scalar_tensor_tensor(out=dst, in0=src, scalar=tap, in1=dst, op0=ALU.mult,
                                                         op1=ALU.add).then_inc(tapped, 1)

            @block.scalar
            def _(act):
                with act.Fori(0, XBC_T) as i:
                    act.wait_ge(lat_tapped, SSD_K * (i + 1))
                    act.wait_ge(ctx_tapped, SSD_K * (i + 1))
                    act.activation(xbc[:, bass.ds(i, 1), :], xbc[:, bass.ds(i, 1), :], ACT.Silu,
                                   bias=core.col("ssd_conv_b", i))


def ssd_tokens(core, xbc, x_tok, b_tok):
    with core.stage("turned", "taken") as (block, turned, taken):
        jobs = [(t, j, x_tok[:, t, j * P:(j + 4) * P], range(j, j + 4)) for t in range(TOK // P) for j in (0, 4)]
        jobs += [(t, B_T, b_tok[:, t, :], range(B_T, B_T + 2)) for t in range(TOK // P)]

        @block.tensor
        def _(pe):
            for n, (t, _, _, tiles) in enumerate(jobs):
                if n >= 8:
                    pe.wait_ge(taken, n - 7)
                for m, j in enumerate(tiles):
                    mm = pe.transpose(core.banks[n % 8][:, m * P:(m + 1) * P], xbc[:, j, t * P:(t + 1) * P],
                                      core.const("ident"))
                mm.then_inc(turned, 1)

        @block.scalar
        def _(act):
            for n, (_, _, out, tiles) in enumerate(jobs):
                act.wait_ge(turned, n + 1)
                act.activation(out, core.banks[n % 8][:, 0:len(tiles) * P], ACT.Copy).then_inc(taken, 1)


def step_sizes(core, dt, a, rows):
    tiles = TOK // P
    with core.room(dt_soft=[P, tiles, 32], a_exp=[P, 32]) as (soft, a_exp), \
            core.stage("biased", "folded", "exp_done", "soft_done", "dt_done", "a_exp_done") as (
                block, biased, folded, exp_done, soft_done, dt_done, a_exp_done):
        @block.vector
        def _(dve):
            dve.tensor_tensor(dt[:], dt[:], spread(rows[:, 0:32], 1, tiles), ALU.add).then_inc(biased, 1)
            dve.wait_ge(biased, 1)
            dve.scalar_tensor_tensor(out=soft[:], in0=dt[:], scalar=-1.0, in1=dt[:], op0=ALU.mult, op1=ALU.min)\
               .then_inc(folded, 1)
            dve.wait_ge(soft_done, 1)
            dve.scalar_tensor_tensor(out=dt[:], in0=dt[:], scalar=0.0, in1=soft[:], op0=ALU.max, op1=ALU.add)\
               .then_inc(dt_done, 1)
            dve.wait_ge(dt_done, 1)
            dve.wait_ge(a_exp_done, 1)
            dve.scalar_tensor_tensor(out=a[:], in0=dt[:], scalar=-1.0, in1=spread(a_exp[:, :], 1, tiles),
                                     op0=ALU.mult, op1=ALU.mult)

        @block.scalar
        def _(act):
            act.activation(a_exp[:, :], rows[:, 32:64], ACT.Exp).then_inc(a_exp_done, 1)
            act.wait_ge(folded, 1)
            act.activation(soft[:], soft[:], ACT.Exp).then_inc(exp_done, 1)
            act.wait_ge(exp_done, 1)
            act.activation(soft[:], soft[:], ACT.Ln, bias=1.0).then_inc(soft_done, 1)


def ssd_chunk(core, d, token, tile, output, xbc, x_tok, b_tok, dt, a, state, y, buf):
    b_st, c_st, bt_st, a_st, xdt, xdtd, acum, left, decay, cb, diff, m_buf, ce_buf = buf
    banks = core.banks
    until, neg = (core.const("until"), core.const("neg_until")) if d == 0 else (core.const("since"), core.const("neg_since"))
    heads = slice(d * SSD_HEADS, (d + 1) * SSD_HEADS)
    here = bass.ds(token, CHUNK)
    quads = SSD_HEADS // 4
    names = ["b_staged", "a_staged", "x_scaled", "cols_done", "acum_done", "left_done", "decay_done", "x_decayed", "cb_done",
             "cb_taken", "acum_rows", "diff_done", "m_exp", "ce_exp", "m_done", "ce_done", "y_done", "y_added",
             "states_made", "state_faded"]
    with core.stage(*names) as (block, b_staged, a_staged, x_scaled, cols_done, acum_done, left_done, decay_done, x_decayed,
                                cb_done, cb_taken, acum_rows, diff_done, m_exp, ce_exp, m_done, ce_done, y_done, y_added,
                                states_made, state_faded):
        @block.gpsimd
        def _(pool):
            x3 = x_tok[:, bass.ds(tile, 1), :].rearrange("p a (h x) -> p (a h) x", x=SSD_P)
            dt_here = dt[:, bass.ds(tile, 1), heads].rearrange("p a h -> p (a h)")
            pool.tensor_tensor(xdt[:], x3, spread(dt_here, 2, SSD_P), ALU.mult).then_inc(x_scaled, 1)
            pool.wait_ge(x_scaled, 1)
            pool.wait_ge(decay_done, 1)
            pool.tensor_tensor(xdtd[:], xdt[:], spread(decay[:, 0:16], 2, SSD_P), ALU.mult).then_inc(x_decayed, 1)
            if output:
                for q in range(quads):
                    pool.wait_ge(ce_exp, q + 1)
                    if q == 0:
                        pool.wait_ge(b_staged, 3)
                    pool.tensor_tensor(ce_buf[:, q % 2], ce_buf[:, q % 2], spread(c_st[:, q // 2, :], 1, 4), ALU.mult)\
                        .then_inc(ce_done, 1)

        @block.tensor
        def _(pe):
            pe.wait_ge(a_staged, 1)
            pe.matmul(banks[0][:, 0:16], until, a_st[:, :], start=True, stop=True)
            pe.matmul(banks[0][:, 16:32], core.const("ones"), a_st[:, :], start=True, stop=True).then_inc(cols_done, 1)
            if output:
                pe.wait_ge(b_staged, 3)
                for g in range(SSD_G):
                    mm = pe.matmul(banks[1][:, g * P:(g + 1) * P], b_st[:, g, :], c_st[:, g, :], start=True, stop=True)
                mm.then_inc(cb_done, 1)

                def rows(q):
                    if q >= 2:
                        pe.wait_ge(diff_done, 4 * (q - 1))
                        pe.wait_ge(ce_exp, q - 1)
                    for n in range(4):
                        h = 4 * q + n
                        mm = pe.matmul(banks[2 + q % 2][:, n * P:(n + 1) * P], a_st[:, h:h + 1].broadcast_to([P, P]),
                                       until, start=True, stop=True)
                    mm.then_inc(acum_rows, 1)

                rows(0)
                rows(1)
                for q in range(quads):
                    if q == 0:
                        pe.wait_ge(x_scaled, 1)
                    pe.wait_ge(m_done, q + 1)
                    pe.wait_ge(ce_done, q + 1)
                    if q >= 2:
                        pe.wait_ge(y_added, q - 1)
                    for n in range(4):
                        h = 4 * q + n
                        out = banks[4 + q % 2][64 * (n % 2):64 * (n % 2) + 64, (n // 2) * P:(n // 2 + 1) * P]
                        pe.matmul(out, xdt[:, h, :], m_buf[:, q % 2, n, :], start=True, stop=False)
                        mm = pe.matmul(out, state[:, h, :], ce_buf[:, q % 2, n, :], start=False, stop=True)
                    mm.then_inc(y_done, 1)
                    if q + 2 < quads:
                        rows(q + 2)
            pe.wait_ge(x_decayed, 1)
            pe.wait_ge(b_staged, 3)
            for g in range(SSD_G):
                mm = pe.matmul(banks[6 + g][:, :], bt_st[:, g * P:(g + 1) * P],
                               xdtd[:, 8 * g:8 * g + 8, :].rearrange("p h x -> p (h x)"), start=True, stop=True)
            mm.then_inc(states_made, 1)

        @block.scalar
        def _(act):
            act.activation(b_st[:], xbc[:, B_T:B_T + 2, here], ACT.Identity).then_inc(b_staged, 1)
            act.activation(c_st[:], xbc[:, C_T:C_T + 2, here], ACT.Identity).then_inc(b_staged, 1)
            act.activation(bt_st[:].rearrange("p (a n) -> p a n", a=1), b_tok[:, bass.ds(tile, 1), :], ACT.Identity)\
               .then_inc(b_staged, 1)
            act.wait_ge(left_done, 1)
            act.activation(decay[:, :], left[:, :], ACT.Exp).then_inc(decay_done, 1)
            if output:
                for q in range(quads):
                    act.wait_ge(diff_done, 4 * (q + 1))
                    if q >= 2:
                        act.wait_ge(y_done, q - 1)
                    act.activation(m_buf[:, q % 2], diff[:, q % 2], ACT.Exp).then_inc(m_exp, 1)
                    act.activation(ce_buf[:, q % 2].rearrange("p n t -> p (n t)"), banks[2 + q % 2][:, :], ACT.Exp)\
                       .then_inc(ce_exp, 1)

        @block.vector
        def _(dve):
            dve.tensor_copy(a_st[:, :].unsqueeze(1), a[:, bass.ds(tile, 1), heads]).then_inc(a_staged, 1)
            dve.wait_ge(cols_done, 1)
            dve.tensor_copy(acum[:, :], banks[0][:, 0:16]).then_inc(acum_done, 1)
            dve.tensor_copy(left[:, 16:32], banks[0][:, 16:32]).then_inc(acum_done, 1)
            dve.wait_ge(acum_done, 2)
            dve.tensor_tensor(left[:, 0:16], left[:, 16:32], acum[:, :], ALU.subtract).then_inc(left_done, 1)
            if output:
                dve.wait_ge(cb_done, 1)
                dve.tensor_copy(cb[:].rearrange("p g t -> p (g t)"), banks[1][:, 0:2 * P]).then_inc(cb_taken, 1)

                def add_y(q):
                    dve.wait_ge(y_done, q + 1)
                    out = y[:, 2 * q:2 * q + 2, here]
                    dve.tensor_tensor(out, out, banks[4 + q % 2][:, 0:2 * P].rearrange("p (j t) -> p j t", j=2), ALU.add)\
                       .then_inc(y_added, 1)

                def differences(q):
                    dve.wait_ge(acum_rows, q + 1)
                    if q >= 2:
                        dve.wait_ge(m_exp, q - 1)
                    for n in range(4):
                        h = 4 * q + n
                        dve.scalar_tensor_tensor(out=diff[:, q % 2, n, :], in0=banks[2 + q % 2][:, n * P:(n + 1) * P],
                                                 scalar=acum[:, h:h + 1], in1=neg, op0=ALU.subtract, op1=ALU.add)\
                           .then_inc(diff_done, 1)

                differences(0)
                for q in range(quads):
                    if q + 1 < quads:
                        differences(q + 1)
                    dve.wait_ge(m_exp, q + 1)
                    if q == 0:
                        dve.wait_ge(cb_taken, 1)
                    dve.tensor_tensor(m_buf[:, q % 2], m_buf[:, q % 2], spread(cb[:, q // 2, :], 1, 4), ALU.mult)\
                       .then_inc(m_done, 1)
                    if q >= 1:
                        add_y(q - 1)
                add_y(quads - 1)
            dve.wait_ge(decay_done, 1)
            dve.wait_ge(states_made, 1)
            dve.tensor_tensor(state[:], state[:], spread(decay[:, 16:32], 2, SSD_P), ALU.mult).then_inc(state_faded, 1)
            dve.wait_ge(state_faded, 1)
            for g in range(SSD_G):
                dve.tensor_tensor(state[:, 8 * g:8 * g + 8, :].rearrange("p h x -> p (h x)"),
                                  state[:, 8 * g:8 * g + 8, :].rearrange("p h x -> p (h x)"), banks[6 + g][:, :], ALU.add)


def chunks_of(core, d, body):
    for first, count, output in ((SEQ // CHUNK, CTX // CHUNK, False), (0, SEQ // CHUNK, True)):
        with core.nc.Fori(0, count) as i:
            tile = i + first if d == 0 else i * -1 + (first + count - 1)
            body(tile * CHUNK, tile, output)


def ssd(core, w_in, h, y, rows):
    tiles = TOK // P
    with core.room(xbc=[P, XBC_T, TOK]) as (xbc,):
        ssd_inputs(core, w_in, h, xbc)
        with core.room(x_tok=[P, tiles, SSD_IN], b_tok=[P, tiles, SSD_G * SSD_N], dt=[P, tiles, 32], a=[P, tiles, 32],
                       state=[P, SSD_HEADS, SSD_P], b_st=[P, SSD_G, P], c_st=[P, SSD_G, P], bt_st=[P, SSD_G * P],
                       a_st=[P, 16], xdt=[P, SSD_HEADS, SSD_P], xdtd=[P, SSD_HEADS, SSD_P], acum=[P, 16], left=[P, 32],
                       decay=[P, 32], cb=[P, SSD_G, P], diff=[P, 2, 4, P], m_buf=[P, 2, 4, P], ce_buf=[P, 2, 4, P]) as (
                x_tok, b_tok, dt, a, state, *buf):
            ssd_tokens(core, xbc, x_tok, b_tok)
            gemm_tokens(core, "dt", w_in[:, MIX_AT["dt"]:MIX_AT["q"]], h, tiles, lambda t, s: dt[:, t, :], 32)
            step_sizes(core, dt, a, rows)
            with core.stage("skipped") as (block, skipped):
                @block.vector
                def _(dve):
                    for j in range(DT):
                        dve.tensor_scalar(y[:, j, :], xbc[:, j, 0:SEQ], rows[:, 64 + j:65 + j], None, ALU.mult)
            for d in range(2):
                with core.stage("cleared") as (block, cleared):
                    @block.vector
                    def _(dve):
                        dve.memset(state[:], 0.0)
                chunks_of(core, d, lambda token, tile, output: ssd_chunk(
                    core, d, token, tile, output, xbc, x_tok, b_tok, dt, a, state, y, buf))


def gla_chunk(core, d, token, tile, output, q, f, v, state, o, reset, buf):
    key, acum, q_st, v_st, q_in, k_out, att, mix0, mix1, fade = buf
    t1, lf, kt = mix0, mix1, mix0
    mix = [mix0, mix1]
    banks = core.banks
    flat = lambda b: b[:].rearrange("p h t -> p (h t)")
    end = CHUNK - 1 if d == 0 else 0
    here = bass.ds(token, CHUNK)
    fh = f[:, :, here]
    names = ["folded", "exp_done", "ln_done", "lf_done", "key_arg", "key_done", "summed", "q_staged", "v_staged", "q_exp",
             "q_in_done", "left_done", "left_exp", "k_out_done", "fade_done"]
    with core.stage(*names) as (block, folded, exp_done, ln_done, lf_done, key_arg, key_done, summed, q_staged, v_staged,
                                q_exp, q_in_done, left_done, left_exp, k_out_done, fade_done):
        @block.vector
        def _(dve):
            dve.scalar_tensor_tensor(out=t1[:], in0=fh, scalar=-1.0, in1=fh, op0=ALU.mult, op1=ALU.min).then_inc(folded, 1)
            dve.wait_ge(ln_done, 1)
            dve.scalar_tensor_tensor(out=lf[:], in0=fh, scalar=0.0, in1=t1[:], op0=ALU.min, op1=ALU.subtract)\
               .then_inc(lf_done, 1)
            dve.wait_ge(lf_done, 1)
            dve.tensor_tensor(key[:], lf[:], fh, ALU.subtract).then_inc(key_arg, 1)
            step = 1 if d == 0 else -1
            dve.tensor_tensor_scan(flat(acum)[:, ::step], reset[:, :], flat(lf)[:, ::step], 0.0, ALU.mult, ALU.add)\
               .then_inc(summed, 1)
            dve.wait_ge(summed, 1)
            dve.tensor_tensor(k_out[:], spread(acum[:, :, end], 2, CHUNK), acum[:], ALU.subtract).then_inc(left_done, 1)
            dve.wait_ge(left_exp, 1)
            dve.wait_ge(key_done, 1)
            dve.tensor_tensor(k_out[:], k_out[:], key[:], ALU.mult).then_inc(k_out_done, 1)
            if output:
                dve.wait_ge(q_exp, 1)
                dve.wait_ge(q_staged, 1)
                dve.tensor_tensor(q_in[:], q_in[:], q_st[:], ALU.mult).then_inc(q_in_done, 1)

        @block.scalar
        def _(act):
            act.wait_ge(folded, 1)
            act.activation(t1[:], t1[:], ACT.Exp).then_inc(exp_done, 1)
            act.wait_ge(exp_done, 1)
            act.activation(t1[:], t1[:], ACT.Ln, bias=1.0).then_inc(ln_done, 1)
            act.wait_ge(key_arg, 1)
            act.activation(key[:], key[:], ACT.Exp).then_inc(key_done, 1)
            act.wait_ge(summed, 1)
            act.activation(fade[:, :], acum[:, :, end], ACT.Exp).then_inc(fade_done, 1)
            act.wait_ge(left_done, 1)
            act.activation(k_out[:], k_out[:], ACT.Exp).then_inc(left_exp, 1)
            if output:
                act.activation(q_in[:], acum[:], ACT.Exp).then_inc(q_exp, 1)

        @block.gpsimd
        def _(pool):
            if output:
                pool.tensor_copy(q_st[:], q[:, :, here]).then_inc(q_staged, 1)
            pool.tensor_copy(flat(v_st).unsqueeze(1), v[:, bass.ds(tile, 1), :]).then_inc(v_staged, 1)

    def half(b, m, side):
        return flat(b).rearrange("p (b t) -> p b t", t=2 * m)[:, :, side * m:(side + 1) * m]

    if output:
        names = ["diff_done", "exp_done", "mixed", "products", "merged", "diagonal", "att_done", "o_done", "o_added"]
        with core.stage(*names) as (block, diff_done, exp_done, mixed, products, merged, diagonal, att_done, o_done, o_added):
            levels = list(enumerate(LEVELS))

            @block.gpsimd
            def _(pool):
                for n, m in levels:
                    if n >= 2:
                        pool.wait_ge(products, n - 1)
                    left, right = half(acum, m, 0), half(acum, m, 1)
                    middle = left[:, :, m - 1] if d == 0 else right[:, :, 0]
                    middle = spread(middle, 2, m)
                    a, b = (left, right) if d == 0 else (right, left)
                    out_a, out_b = half(mix[n % 2], m, d), half(mix[n % 2], m, 1 - d)
                    pool.tensor_tensor(out_a, middle, a, ALU.subtract).then_inc(diff_done, 1)
                    pool.tensor_tensor(out_b, b, middle, ALU.subtract).then_inc(diff_done, 1)

            @block.scalar
            def _(act):
                for n, m in levels:
                    act.wait_ge(diff_done, 2 * n + 2)
                    act.activation(mix[n % 2][:], mix[n % 2][:], ACT.Exp).then_inc(exp_done, 1)

            @block.tensor
            def _(pe):
                for h in range(HG_HEADS):
                    mm = pe.matmul(banks[4 + h // 4][:, (h % 4) * P:(h % 4 + 1) * P], key[:, h, :], q_st[:, h, :],
                                   start=True, stop=True)
                mm.then_inc(diagonal, 1)
                for n, m in levels:
                    pe.wait_ge(mixed, 2 * n + 2)
                    if n >= 2:
                        pe.wait_ge(merged, 2 * (n - 1))
                    for h in range(HG_HEADS):
                        mm = pe.matmul(banks[2 * (n % 2) + h // 4][:, (h % 4) * P:(h % 4 + 1) * P], mix[n % 2][:, h, :],
                                       mix[n % 2][:, h, :], start=True, stop=True)
                    mm.then_inc(products, 1)
                pe.wait_ge(merged, 2 * len(levels))
                for h in range(HG_HEADS):
                    out = banks[6 + h // 4][:, (h % 4) * P:(h % 4 + 1) * P]
                    pe.matmul(out, v_st[:, h, :], att[:, h, :], start=True, stop=False)
                    mm = pe.matmul(out, state[:, h, :], q_in[:, h, :], start=False, stop=True)
                mm.then_inc(o_done, 1)

            @block.vector
            def _(dve):
                def mix_level(n, m):
                    dve.wait_ge(exp_done, n + 1)
                    for side in range(2):
                        src = key if side == d else q_st
                        dve.tensor_tensor(half(mix[n % 2], m, side), half(mix[n % 2], m, side), half(src, m, side), ALU.mult)\
                           .then_inc(mixed, 1)

                mix_level(*levels[0])
                dve.wait_ge(diagonal, 1)
                for b in range(2):
                    four = slice(4 * b, 4 * b + 4)
                    dve.tensor_tensor(att[:, four, :], banks[4 + b][:, :].rearrange("p (h t) -> p h t", h=4),
                                      spread(core.const("ident"), 1, 4), ALU.mult).then_inc(att_done, 1)
                for n, m in levels:
                    if n + 1 < len(levels):
                        mix_level(*levels[n + 1])
                    side = "left_right" if d == 0 else "right_left"
                    mask = core.const(f"{side}_{m}").bitcast(U32)
                    dve.wait_ge(products, n + 1)
                    for b in range(2):
                        four = slice(4 * b, 4 * b + 4)
                        if n == 0:
                            dve.wait_ge(att_done, 2)
                        else:
                            dve.wait_ge(merged, 2 * n)
                        dve.copy_predicated(att[:, four, :], spread(mask, 1, 4),
                                            banks[2 * (n % 2) + b][:, :].rearrange("p (h t) -> p h t", h=4))\
                           .then_inc(merged, 1)
                dve.wait_ge(o_done, 1)
                for b in range(2):
                    out = o[:, 4 * b:4 * b + 4, here]
                    dve.tensor_tensor(out, out, banks[6 + b][:, :].rearrange("p (h t) -> p h t", h=4), ALU.add)\
                       .then_inc(o_added, 1)

    with core.stage("turned", "taken", "states_made", "faded") as (block, turned, taken, states_made, faded):
        @block.tensor
        def _(pe):
            for h in range(HG_HEADS):
                mm = pe.transpose(banks[h // 4][:, (h % 4) * P:(h % 4 + 1) * P], k_out[:, h, :], core.const("ident"))
                if h % 4 == 3:
                    mm.then_inc(turned, 1)
            for h in range(HG_HEADS):
                pe.wait_ge(taken, h // 4 + 1)
                mm = pe.matmul(banks[2 + h // 4][:, (h % 4) * P:(h % 4 + 1) * P], kt[:, h, :], v_st[:, h, :],
                               start=True, stop=True)
                if h % 4 == 3:
                    mm.then_inc(states_made, 1)

        @block.scalar
        def _(act):
            for b in range(2):
                act.wait_ge(turned, b + 1)
                act.activation(kt[:, 4 * b:4 * b + 4, :].rearrange("p h t -> p (h t)"), banks[b][:, :], ACT.Copy)\
                   .then_inc(taken, 1)

        @block.vector
        def _(dve):
            for h in range(HG_HEADS):
                dve.wait_ge(states_made, h // 4 + 1)
                dve.scalar_tensor_tensor(out=state[:, h, :], in0=state[:, h, :], scalar=fade[:, h:h + 1],
                                         in1=banks[2 + h // 4][:, (h % 4) * P:(h % 4 + 1) * P], op0=ALU.mult, op1=ALU.add)


def gla(core, w_in, h, o):
    tiles = TOK // P
    wide = [P, HG_HEADS, CHUNK]
    with core.room(v=[P, tiles, D], q=[P, HG_HEADS, SEQ]) as (v, q):
        gemm_tokens(core, "v", w_in[:, MIX_AT["v"]:MIX_AT["g"]], h, tiles,
                    lambda t, s: v[:, t, s * 256:(s + 1) * 256], 256)
        gemm(core, "q", w_in[:, MIX_AT["q"]:MIX_AT["f"]], h, [(0, SEQ)], lambda tile, n: q[:, bass.ds(tile, 1), :], DT, 4,
             func=ACT.Silu)
        with core.room(f=[P, HG_HEADS, TOK], hg_state=[P, HG_HEADS, P], reset=[P, HG_HEADS * CHUNK]) as (f, state, reset):
            with core.stage("ones_in", "cleared") as (block, ones_in, cleared):
                @block.vector
                def _(dve):
                    dve.memset(reset[:, :], 1.0).then_inc(ones_in, 1)
                    dve.wait_ge(ones_in, 1)
                    dve.memset(reset[:, ::CHUNK], 0.0)

                @block.gpsimd
                def _(pool):
                    pool.memset(o[:], 0.0).then_inc(cleared, 1)
            for d in range(2):
                at = MIX_AT["f"] + d * D
                gemm(core, f"f{d}", w_in[:, at:at + D], h, SPANS,
                     lambda tile, n: f[:, bass.ds(tile, 1), SPANS[n][0]:SPANS[n][0] + SPANS[n][1]], HG_HEADS, 4)
                with core.stage("cleared") as (block, cleared):
                    @block.vector
                    def _(dve):
                        dve.memset(state[:], 0.0)
                names = ["key", "acum", "q_st", "v_st", "q_in", "k_out", "att", "mix0", "mix1"]
                with core.room(**{f"{n}_{d}": wide for n in names}, **{f"fade_{d}": [P, HG_HEADS]}) as buf:
                    chunks_of(core, d, lambda token, tile, output: gla_chunk(
                        core, d, token, tile, output, q, f, v, state, o, reset, buf))


def group_norm_gate(core, name, y, w_gate, x, groups, gain, gate_first):
    size = DT // groups
    width = size * P
    with core.room(**{f"{name}_gate": [P, DT, SEQ], f"{name}_sq": [P, DT, SEQ], f"{name}_rstd": [P, 2, SEQ]}) as (
            gate, sq, rstd):
        gemm(core, f"{name}_g", w_gate, x, [(0, SEQ)], lambda tile, n: gate[:, bass.ds(tile, 1), :], DT, 4, func=ACT.Silu)
        with core.stage("gated", "squared", "sq_summed", "var_done", "root_done", "inverse_done", "scaled") as (
                block, gated, squared, sq_summed, var_done, root_done, inverse_done, scaled):
            @block.vector
            def _(dve):
                if gate_first:
                    for k in range(DT):
                        dve.tensor_tensor(y[:, k, :], y[:, k, :], gate[:, k, :], ALU.mult).then_inc(gated, 1)
                for g in range(groups):
                    dve.wait_ge(sq_summed, g + 1)
                    if g >= 2:
                        dve.wait_ge(scaled, (g - 1) * size)
                    dve.tensor_scalar(rstd[:, g % 2, :], core.banks[g % 8][:, :], 1.0 / width, EPS, ALU.mult, ALU.add)\
                       .then_inc(var_done, 1)
                    dve.wait_ge(root_done, g + 1)
                    dve.reciprocal(rstd[:, g % 2, :], rstd[:, g % 2, :]).then_inc(inverse_done, 1)
                    dve.wait_ge(inverse_done, g + 1)
                    for k in range(g * size, (g + 1) * size):
                        dve.scalar_tensor_tensor(out=y[:, k, :], in0=y[:, k, :], scalar=gain(k), in1=rstd[:, g % 2, :],
                                                 op0=ALU.mult, op1=ALU.mult).then_inc(scaled, 1)
                if not gate_first:
                    for k in range(DT):
                        dve.wait_ge(scaled, k + 1)
                        dve.tensor_tensor(y[:, k, :], y[:, k, :], gate[:, k, :], ALU.mult).then_inc(gated, 1)

            @block.scalar
            def _(act):
                for k in range(DT):
                    if gate_first:
                        act.wait_ge(gated, k + 1)
                    act.activation(sq[:, k, :], y[:, k, :], ACT.Square).then_inc(squared, 1)
                for g in range(groups):
                    act.wait_ge(var_done, g + 1)
                    act.activation(rstd[:, g % 2, :], rstd[:, g % 2, :], ACT.Sqrt).then_inc(root_done, 1)

            @block.tensor
            def _(pe):
                for g in range(groups):
                    for k in range(g * size, (g + 1) * size):
                        pe.wait_ge(squared, k + 1)
                        mm = pe.matmul(core.banks[g % 8][:, :], core.const("ones"), sq[:, k, :], start=(k % size == 0),
                                       stop=(k % size == size - 1))
                    mm.then_inc(sq_summed, 1)


def even_mixer(core, w_in, w_out, h, y_out, rows):
    with core.room(y_ssd=[P, 2 * DT, SEQ]) as (merged,):
        y, o = merged[:, 0:DT, :], merged[:, DT:2 * DT, :]
        ssd(core, w_in, h, y, rows)
        gla(core, w_in, h, o)
        group_norm_gate(core, "ssd", y, w_in[:, MIX_AT["z"]:MIX_AT["xbc"]], h, SSD_G,
                        lambda k: core.col("ssd_norm_w", k), True)
        group_norm_gate(core, "hg", o, w_in[:, MIX_AT["g"]:], h, HG_HEADS, lambda k: core.col("hg_norm_w", k), False)
        gemm(core, "mix_out", w_out, merged, [(0, SEQ)], lambda tile, n: y_out[:, bass.ds(tile, 1), :], DT, 4)

HEAD_SCALE = HD ** -0.5
PAIRS = NSA_H // 2
UNITS = 2 * TT
NC = SEQ // RW_C
RU = 2 * NC


def causal_attention(core, name, q, k, v, out, gates):
    banks = core.banks
    with core.room(**{f"{name}_q": [P, SEQ], f"{name}_k": [P, SEQ], f"{name}_v": [P, TT, 2 * HD], f"{name}_p": [P, 2, SEQ],
                      f"{name}_pt": [P, 2, SEQ], f"{name}_top": [P, UNITS], f"{name}_bias": [P, UNITS],
                      f"{name}_sum": [P, UNITS]}) as (q_st, k_st, v_st, prob, prob_t, top, bias, total), \
            core.nc.Fori(0, PAIRS) as j, \
            core.stage("staged", "scored", "masked", "top_done", "bias_done", "exp_done", "turned", "taken", "summed",
                       "guarded", "inverted", "weighed", "added") as (
                block, staged, scored, masked, top_done, bias_done, exp_done, turned, taken, summed, guarded, inverted,
                weighed, added):
        @block.gpsimd
        def _(pool):
            pool.tensor_copy(q_st[:, :].unsqueeze(1), q[:, bass.ds(j, 1), :]).then_inc(staged, 1)
            pool.tensor_copy(k_st[:, :].unsqueeze(1), k[:, bass.ds(j, 1), :]).then_inc(staged, 1)
            pool.tensor_copy(v_st[:], v[:, :, bass.ds(j * (2 * HD), 2 * HD)]).then_inc(staged, 1)

        @block.tensor
        def _(pe):
            def scores(u):
                e, t = u // TT, u % TT
                if u >= 2:
                    pe.wait_ge(exp_done, u - 1)
                pe.matmul(banks[u % 2][:, 0:(t + 1) * P], q_st[HD * e:HD * e + HD, t * P:(t + 1) * P],
                          k_st[HD * e:HD * e + HD, 0:(t + 1) * P], start=True, stop=True).then_inc(scored, 1)

            def turn(u):
                t = u % TT
                pe.wait_ge(exp_done, u + 1)
                if u >= 2:
                    pe.wait_ge(taken, u - 1)
                for n in range(t + 1):
                    mm = pe.transpose(banks[2 + u % 2][:, n * P:(n + 1) * P], prob[:, u % 2, n * P:(n + 1) * P],
                                      core.const("ident"))
                mm.then_inc(turned, 1)

            def values(u):
                e, t = u // TT, u % TT
                pe.wait_ge(taken, u + 1)
                if u >= 2:
                    pe.wait_ge(added, u - 1)
                for n in range(t + 1):
                    mm = pe.matmul(banks[4 + u % 2][:, 0:HD], prob_t[:, u % 2, n * P:(n + 1) * P],
                                   v_st[:, n, HD * e:HD * e + HD], start=(n == 0), stop=(n == t))
                mm.then_inc(summed, 1)

            pe.wait_ge(staged, 3)
            scores(0)
            scores(1)
            for u in range(UNITS):
                turn(u)
                if u + 2 < UNITS:
                    scores(u + 2)
                values(u)

        @block.scalar
        def _(act):
            for u in range(UNITS):
                n = (u % TT + 1) * P
                act.wait_ge(bias_done, u + 1)
                if u >= 2:
                    act.wait_ge(turned, u - 1)
                act.activation(prob[:, u % 2, 0:n], banks[u % 2][:, 0:n], ACT.Exp, bias=bias[:, u:u + 1],
                               scale=HEAD_SCALE, accum_out=total[:, u:u + 1]).then_inc(exp_done, 1)
                act.wait_ge(turned, u + 1)
                if u >= 2:
                    act.wait_ge(summed, u - 1)
                act.activation(prob_t[:, u % 2, 0:n], banks[2 + u % 2][:, 0:n], ACT.Copy).then_inc(taken, 1)

        @block.vector
        def _(dve):
            def finish(u):
                e, t = u // TT, u % TT
                dve.wait_ge(exp_done, u + 1)
                dve.tensor_scalar(total[:, u:u + 1], total[:, u:u + 1], 1e-30, None, ALU.max).then_inc(guarded, 1)
                dve.wait_ge(guarded, u + 1)
                dve.reciprocal(total[:, u:u + 1], total[:, u:u + 1]).then_inc(inverted, 1)
                dve.wait_ge(inverted, u + 1)
                dst = out[:, t, bass.ds(j * (2 * HD) + HD * e, HD)]
                if gates is None:
                    dve.wait_ge(summed, u + 1)
                    dve.tensor_scalar(dst, banks[4 + u % 2][:, 0:HD], total[:, u:u + 1], None, ALU.mult)\
                       .then_inc(added, 1)
                else:
                    dve.tensor_tensor(total[:, u:u + 1], total[:, u:u + 1], gates(j, e, t), ALU.mult).then_inc(weighed, 1)
                    dve.wait_ge(weighed, u + 1)
                    dve.wait_ge(summed, u + 1)
                    dve.scalar_tensor_tensor(out=dst, in0=banks[4 + u % 2][:, 0:HD], scalar=total[:, u:u + 1],
                                             in1=dst, op0=ALU.mult, op1=ALU.add).then_inc(added, 1)

            for u in range(UNITS):
                t = u % TT
                dve.wait_ge(scored, u + 1)
                last = banks[u % 2][:, t * P:(t + 1) * P]
                dve.tensor_tensor(last, last, core.const("neg_since"), ALU.add).then_inc(masked, 1)
                dve.wait_ge(masked, u + 1)
                dve.tensor_reduce(top[:, u:u + 1], banks[u % 2][:, 0:(t + 1) * P], AX_X, ALU.max).then_inc(top_done, 1)
                dve.wait_ge(top_done, u + 1)
                dve.tensor_scalar(bias[:, u:u + 1], top[:, u:u + 1], -HEAD_SCALE, None, ALU.mult).then_inc(bias_done, 1)
                if u >= 1:
                    finish(u - 1)
            finish(UNITS - 1)


def compress(core, n, kv, pos, w1, w2, k_out, v_out):
    half = SEQ // 2
    step = CMP_STRIDE // 2
    pairs = CMP_LEN // 2
    g_n = KV_H * N_CMP
    with core.room(**{f"cmp_even_odd{n}": [P, 2, half], f"cmp_pairs{n}": [P, KV_H, half],
                      f"cmp_x{n}": [P, pairs, KV_H, N_CMP], f"cmp_w1{n}": [P, pairs, CMP_HID], f"cmp_w2{n}": [P, 2, HD],
                      f"cmp_pos{n}": [P, pairs], f"cmp_hid{n}": [P, 2, g_n]}) as (
            even_odd, both, x, w1_sb, w2_sb, pos_sb, hid), \
            core.stage("w_in", "split", "moved", "placed", "hid_done", "active", "out_done", "out_taken", "cleared") as (
                block, w_in, split, moved, placed, hid_done, active, out_done, out_taken, cleared):
        @block.sync
        def _(sp):
            sp.dma_start(w1_sb[:], w1.rearrange("(k p) m -> p k m", p=P)).then_inc(w_in, 16)
            sp.dma_start(w2_sb[:], w2.rearrange("(k p) m -> p k m", p=P)).then_inc(w_in, 16)
            sp.dma_start(pos_sb[:], pos).then_inc(w_in, 16)
            sp.wait_ge(split, 1)
            for g in range(KV_H):
                for parity in range(2):
                    sp.dma_start(both[HD * parity:HD * parity + HD, g, :], even_odd[HD * g:HD * g + HD, parity, :])\
                      .then_inc(moved, 16)
            sp.wait_ge(moved, 64)

        @block.vector
        def _(dve):
            dve.tensor_copy(even_odd[:], kv.rearrange("p (t a) -> p a t", a=2)).then_inc(split, 1)
            if v_out is not None:
                dve.memset(v_out[:], 0.0).then_inc(cleared, 1)
            else:
                dve.memset(k_out[:], 0.0).then_inc(cleared, 1)
            dve.wait_ge(w_in, 48)
            dve.wait_ge(moved, 64)
            for g in range(KV_H):
                for a in range(pairs // step):
                    src = both[:, g, step * a:step * (a + N_CMP)].rearrange("p (i b) -> p i b", b=step)
                    dst = x[:, step * a:step * (a + 1), g, :].rearrange("p b i -> p i b")
                    dve.tensor_tensor(dst, src, spread(pos_sb[:, step * a:step * (a + 1)], 1, N_CMP), ALU.add)\
                       .then_inc(placed, 1)
            dve.wait_ge(out_done, 1)
            dve.wait_ge(cleared, 1)
            if v_out is not None:
                dve.tensor_copy(v_out[0:N_CMP, :], core.banks[2][0:N_CMP, 0:KV_H * HD]).then_inc(out_taken, 1)
            else:
                for j in range(PAIRS):
                    for e in range(2):
                        g = (2 * j + e) // (NSA_H // KV_H)
                        rows = slice(HD * e, HD * e + HD)
                        dve.tensor_copy(k_out[rows, j, 0:N_CMP], core.banks[2][rows, g * N_CMP:(g + 1) * N_CMP])\
                           .then_inc(out_taken, 1)

        @block.tensor
        def _(pe):
            pe.wait_ge(w_in, 48)
            pe.wait_ge(placed, 2 * KV_H)
            for m in range(2):
                for i in range(pairs):
                    mm = pe.matmul(core.banks[m][:, 0:g_n], w1_sb[:, i, m * P:(m + 1) * P],
                                   x[:, i, :, :].rearrange("p g i -> p (g i)"), start=(i == 0), stop=(i == pairs - 1))
                mm.then_inc(hid_done, 1)
            pe.wait_ge(active, 2)
            for e in range(2):
                for m in range(2):
                    if v_out is not None:
                        mm = pe.matmul(core.banks[2][0:N_CMP, HD * e:HD * e + HD], hid[:, m, N_CMP * e:N_CMP * (e + 1)],
                                       w2_sb[:, m, :], start=(m == 0), stop=(m == 1))
                    else:
                        mm = pe.matmul(core.banks[2][HD * e:HD * e + HD, 0:g_n], w2_sb[:, m, :], hid[:, m, :],
                                       start=(m == 0), stop=(m == 1))
            mm.then_inc(out_done, 1)

        @block.scalar
        def _(act):
            for m in range(2):
                act.wait_ge(hid_done, m + 1)
                act.activation(hid[:, m, :], core.banks[m][:, 0:g_n], ACT.Gelu_apprx_tanh).then_inc(active, 1)


def compressed_attention(core, q, k, v, out, gates):
    n_u = NSA_H * TT
    keys = N_CMP + 1
    banks = core.banks
    per_bank = 4
    with core.room(cs=[P, NSA_H, TT, keys], cs_top=[P, n_u], cs_sum=[P, n_u], cs_t=[keys, n_u, P]) as (cs, top, total, cs_t), \
            core.stage("scored", "masked", "top_done", "shifted", "exp_done", "kept", "total_done", "guarded", "inverted",
                       "weighed", "prob_done", "turned", "taken", "summed", "written") as (
                block, scored, masked, top_done, shifted, exp_done, kept, total_done, guarded, inverted, weighed,
                prob_done, turned, taken, summed, written):
        flat = cs[:].rearrange("p h t k -> p (h t) k")

        @block.tensor
        def _(pe):
            for h in range(NSA_H):
                rows = slice(HD * (h % 2), HD * (h % 2) + HD)
                for t in range(TT):
                    mm = pe.matmul(banks[h % 2][:, ((h // 2) * TT + t) * keys:((h // 2) * TT + t + 1) * keys],
                                   q[rows, h // 2, t * P:(t + 1) * P], k[rows, h // 2, :], start=True, stop=True)
                mm.then_inc(scored, 1)
            pe.wait_ge(prob_done, 1)
            for u in range(n_u):
                mm = pe.transpose(banks[2 + u // 4][0:keys, (u % 4) * P:(u % 4 + 1) * P], flat[:, u, :], core.const("ident"))
                if u % 4 == 3:
                    mm.then_inc(turned, 1)
            for u in range(n_u):
                g = (u // TT) // (NSA_H // KV_H)
                if u % 4 == 0:
                    pe.wait_ge(taken, u // 4 + 1)
                bank = banks[(0, 1, 2)[u // 8]]
                if u == 16:
                    pe.wait_ge(taken, 6)
                mm = pe.matmul(bank[:, (u % 8) * HD:(u % 8 + 1) * HD], cs_t[:, u, :], v[:, g * HD:(g + 1) * HD],
                               start=True, stop=True)
                if u % 8 == 7:
                    mm.then_inc(summed, 1)

        @block.vector
        def _(dve):
            mask = core.const("cmp_mask").rearrange("p (t k) -> p t k", t=TT)
            valid = core.const("cmp_valid").rearrange("p (t k) -> p t k", t=TT)
            dve.wait_ge(scored, NSA_H)
            for h in range(NSA_H):
                src = banks[h % 2][:, (h // 2) * P:(h // 2 + 1) * P].rearrange("p (t k) -> p t k", t=TT)
                dve.tensor_tensor(cs[:, h], src, mask, ALU.add).then_inc(masked, 1)
            dve.wait_ge(masked, NSA_H)
            dve.tensor_reduce(top[:, :], flat, AX_X, ALU.max).then_inc(top_done, 1)
            dve.wait_ge(top_done, 1)
            dve.tensor_tensor(flat, flat, spread(top[:, :], 2, keys), ALU.subtract).then_inc(shifted, 1)
            dve.wait_ge(exp_done, 1)
            for h in range(NSA_H):
                dve.tensor_tensor(cs[:, h], cs[:, h], valid, ALU.mult).then_inc(kept, 1)
            dve.wait_ge(kept, NSA_H)
            dve.tensor_reduce(total[:, :], flat, AX_X, ALU.add).then_inc(total_done, 1)
            dve.wait_ge(total_done, 1)
            dve.tensor_scalar(total[:, :], total[:, :], 1e-30, None, ALU.max).then_inc(guarded, 1)
            dve.wait_ge(guarded, 1)
            dve.reciprocal(total[:, :], total[:, :]).then_inc(inverted, 1)
            dve.wait_ge(inverted, 1)
            dve.tensor_tensor(total[:].rearrange("p (h t) -> p h t", t=TT), total[:].rearrange("p (h t) -> p h t", t=TT),
                              gates, ALU.mult).then_inc(weighed, 1)
            dve.wait_ge(weighed, 1)
            dve.tensor_tensor(flat, flat, spread(total[:, :], 2, keys), ALU.mult).then_inc(prob_done, 1)
            for n in range(3):
                dve.wait_ge(summed, n + 1)
                src = banks[n][:, :].rearrange("p (h t d) -> p t h d", h=2, t=TT)
                dst = out[:, :, 2 * n * HD:2 * (n + 1) * HD].rearrange("p t (h d) -> p t h d", h=2)
                dve.tensor_copy(dst, src).then_inc(written, 1)

        @block.scalar
        def _(act):
            act.wait_ge(shifted, 1)
            act.activation(cs[:], cs[:], ACT.Exp, scale=HEAD_SCALE).then_inc(exp_done, 1)
            for n in range(n_u // 4):
                act.wait_ge(turned, n + 1)
                act.activation(cs_t[:, 4 * n:4 * n + 4, :].rearrange("k u t -> k (u t)"), banks[2 + n][0:keys, :],
                               ACT.Copy).then_inc(taken, 1)


def head_norm(core, name, o, mix, first, gain):
    heads = o.shape[2] // HD
    n = TT * heads
    with core.room(**{f"{name}_sq": [P, TT, heads * HD], f"{name}_rs": [P, n]}) as (sq, rs), \
            core.stage("squared", "summed", "var_done", "root_done", "inverted", "scaled", "turned", "taken") as (
                block, squared, summed, var_done, root_done, inverted, scaled, turned, taken):
        @block.scalar
        def _(act):
            act.activation(sq[:], o[:], ACT.Square).then_inc(squared, 1)
            act.wait_ge(var_done, 1)
            act.activation(rs[:, :], rs[:, :], ACT.Sqrt).then_inc(root_done, 1)
            for j in range(heads // 2):
                act.wait_ge(turned, j + 1)
                act.activation(mix[:, first + j, :], core.banks[j][:, :], ACT.Identity, scale=gain(j)).then_inc(taken, 1)

        @block.vector
        def _(dve):
            dve.wait_ge(squared, 1)
            dve.tensor_reduce(rs[:, :], sq[:].rearrange("p t (h d) -> p (t h) d", d=HD), AX_X, ALU.add).then_inc(summed, 1)
            dve.wait_ge(summed, 1)
            dve.tensor_scalar(rs[:, :], rs[:, :], 1.0 / HD, NORM_EPS, ALU.mult, ALU.add).then_inc(var_done, 1)
            dve.wait_ge(root_done, 1)
            dve.reciprocal(rs[:, :], rs[:, :]).then_inc(inverted, 1)
            dve.wait_ge(inverted, 1)
            o3 = o[:].rearrange("p t (h d) -> p (t h) d", d=HD)
            dve.tensor_tensor(o3, o3, spread(rs[:, :], 2, HD), ALU.mult).then_inc(scaled, 1)

        @block.tensor
        def _(pe):
            pe.wait_ge(scaled, 1)
            for j in range(heads // 2):
                for t in range(TT):
                    mm = pe.transpose(core.banks[j][:, t * P:(t + 1) * P], o[:, t, j * P:(j + 1) * P], core.const("ident"))
                mm.then_inc(turned, 1)


def load(core, pairs):
    with core.stage("loaded") as (block, loaded):
        @block.sync
        def _(sp):
            for dst, src in pairs:
                sp.dma_start(dst, src).then_inc(loaded, 16)
            sp.wait_ge(loaded, 16 * len(pairs))


def key_pairs(k, out):
    top, low = slice(0, HD), slice(HD, P)
    return [(out[top, 0, :], k[top, :]), (out[low, 0, :], k[top, :]), (out[:, 1, :], k[:, :]),
            (out[top, 2, :], k[low, :]), (out[low, 2, :], k[low, :])]


def repeat_values(core, pairs):
    with core.stage("repeated") as (block, repeated):
        @block.vector
        def _(dve):
            for dst, src in pairs:
                for t in range(TT):
                    dve.tensor_copy(dst[:, t, :].rearrange("p (g r d) -> p g r d", g=KV_H, d=HD),
                                    spread(src[:, t, :].rearrange("p (g d) -> p g d", g=KV_H), 2, NSA_H // KV_H))\
                       .then_inc(repeated, 1)


def nsa(core, w, h, cmp, mix):
    with core.room(nsa_o=[P, TT, NSA_H * HD], nsa_q=[P, 6, SEQ], nsa_g=[P, TT, 146], nsa_kx=[P, PAIRS, SEQ],
                   nsa_vx=[P, TT, NSA_H * HD], kc=[P, PAIRS, N_CMP + 1], vc=[N_CMP + 1, KV_H * HD]) as (
            o, qk, vg, kx, vx, kc, vc):
        gemm(core, "nsa_qk", w[:, 0:768], h, [(0, SEQ)], lambda tile, n: qk[:, bass.ds(tile, 1), :], 6, 6)
        q = qk[:, 0:3, :]
        gemm_tokens(core, "nsa_vw", w[:, AT2["vw"]:AT2["rw"]], h, TT, lambda t, s: vg[:, t, :], 146)
        with core.stage("gated") as (block, gated):
            @block.scalar
            def _(act):
                act.activation(vg[:, :, 128:146], vg[:, :, 128:146], ACT.Sigmoid).then_inc(gated, 1)
        compress(core, 0, qk[:, 3, :], cmp["pos"][0], cmp["w1"][0, 0], cmp["w2"][0, 0], kc, None)
        compress(core, 1, qk[:, 4, :], cmp["pos"][1], cmp["w1"][0, 1], cmp["w2"][0, 1], None, vc)
        all_gates = vg[:, :, 128:146].rearrange("p t (h b) -> p h t b", b=3)
        compressed_attention(core, q, kc, vc, o, all_gates[:, :, :, 0])

        def gates(branch):
            return lambda j, e, t: vg[:, t, bass.ds(j * 6 + (128 + 3 * e + branch), 1)]

        load(core, key_pairs(qk[:, 5, :], kx))
        with core.room(vs=[P, TT, KV_H * HD]) as (vs,):
            gemm_tokens(core, "nsa_vs", w[:, AT2["vs"]:AT2["kw"]], h, TT, lambda t, s: vs[:, t, :], 128)
            repeat_values(core, [(vx, vs)])
        causal_attention(core, "slc", q, kx, vx, o, gates(1))
        gemm(core, "nsa_kw", w[:, AT2["kw"]:AT2["vw"]], h, [(0, SEQ)], lambda tile, n: qk[:, bass.ds(tile + 5, 1), :], 1, 1)
        load(core, key_pairs(qk[:, 5, :], kx))
        repeat_values(core, [(vx, vg[:, :, 0:128])])
        causal_attention(core, "win", q, kx, vx, o, gates(2))
        head_norm(core, "nsa", o, mix, 0, lambda j: core.col("nsa_gain", j))


def moba(core, w, h, mix):
    with core.room(moba_o=[P, TT, MOBA_H * HD], moba_qk=[P, 6, SEQ], moba_v=[P, TT, MOBA_H * HD]) as (o, qk, v):
        gemm(core, "moba_qk", w[:, AT2["mq"]:AT2["mv"]], h, [(0, SEQ)], lambda tile, n: qk[:, bass.ds(tile, 1), :], 6, 6)
        gemm_tokens(core, "moba_v", w[:, AT2["mv"]:], h, TT, lambda t, s: v[:, t, :], MOBA_H * HD)
        causal_attention(core, "moba_a", qk[:, 0:3, :], qk[:, 3:6, :], v, o, None)
        head_norm(core, "moba_n", o, mix, 5, lambda j: core.col("moba_gain", j))


def rwkv_inputs(core, w, h, lora, r, v, gate, bonus, a_in, b_out, k_out, r_in, fade):
    with core.room(rw_p=[P, 7, SEQ + 1], rw_m=[P, 7, SEQ], rw_log=[P, 2, SEQ], rw_cum=[P, 2, SEQ], rw_a=[P, 2, SEQ],
                   rw_kk=[P, 2, SEQ], rw_t=[P, 2, SEQ], rw_t2=[P, 2, SEQ], rw_reset=[P, 2 * SEQ], rw_lora=[P, 256]) as (
            p, m, log_w, cum, a, kk, t1, t2, reset, lora_sb):
        with core.stage("first", "ones_in", "lora_in") as (block, first, ones_in, lora_in):
            @block.sync
            def _(sp):
                sp.dma_start(lora_sb[:], lora).then_inc(lora_in, 16)
                sp.wait_ge(lora_in, 16)

            @block.vector
            def _(dve):
                dve.memset(p[:, :, 0:1], 0.0).then_inc(first, 1)
                dve.memset(reset[:, :], 1.0).then_inc(ones_in, 1)
                dve.wait_ge(ones_in, 1)
                dve.memset(reset[:, ::RW_C], 0.0)
        gemm(core, "rw", w[:, AT2["rw"]:AT2["mq"]], h, [(0, SEQ)], lambda tile, n: p[:, bass.ds(tile, 1), 1:SEQ + 1], 7, 7)
        k = m[:, 2:4, :]
        with core.stage("step", "mixed", "squashed", "low_rank", "w_done", "a_done", "g_done", "kk_raw", "kk_sq", "kk_sum",
                        "kk_root", "rkr", "rkr_sum", "cum_done", "cum_exp", "cum_neg_exp", "before_exp", "before") as (
                block, step, mixed, squashed, low_rank, w_done, a_done, g_done, kk_raw, kk_sq, kk_sum, kk_root, rkr,
                rkr_sum, cum_done, cum_exp, cum_neg_exp, before_exp, before):
            banks = core.banks

            @block.vector
            def _(dve):
                steps = 0
                for n in range(7):
                    dve.tensor_tensor(m[:, n, :], p[:, n, 0:SEQ], p[:, n, 1:SEQ + 1], ALU.subtract).then_inc(step, 1)
                for n in (6, 0, 1, 2, 3, 4, 5):
                    dve.wait_ge(step, 7)
                    dve.scalar_tensor_tensor(out=m[:, n, :], in0=m[:, n, :], scalar=core.col("rw_mu", n),
                                             in1=p[:, n, 1:SEQ + 1], op0=ALU.mult, op1=ALU.add).then_inc(mixed, 1)
                dve.wait_ge(mixed, 7)
                for j in range(2):
                    dve.tensor_scalar(kk[:, j, :], k[:, j, :], core.col("rw_k_k", j), None, ALU.mult).then_inc(kk_raw, 1)
                dve.wait_ge(w_done, 2)
                dve.tensor_scalar(log_w[:], log_w[:], -RW_DECAY, None, ALU.mult).then_inc(step, 1)
                dve.wait_ge(step, 8)
                dve.tensor_tensor_scan(cum[:].rearrange("p j t -> p (j t)"), reset[:, :],
                                       log_w[:].rearrange("p j t -> p (j t)"), 0.0, ALU.mult, ALU.add).then_inc(cum_done, 1)
                dve.wait_ge(cum_done, 1)
                dve.tensor_tensor(t1[:], cum[:], log_w[:], ALU.subtract).then_inc(before, 1)
                dve.wait_ge(a_done, 2)
                for j in range(2):
                    dve.tensor_scalar(t2[:, j, :], a[:, j, :], -1.0, core.col("rw_k_a", j), ALU.add, ALU.mult)\
                       .then_inc(step, 1)
                dve.wait_ge(step, 10)
                dve.wait_ge(kk_raw, 2)
                dve.scalar_tensor_tensor(out=k, in0=t2[:], scalar=1.0, in1=k, op0=ALU.add, op1=ALU.mult).then_inc(step, 1)
                dve.wait_ge(step, 11)
                for j in range(2):
                    dve.scalar_tensor_tensor(out=t2[:, j, :], in0=m[:, j, :], scalar=core.col("rw_r_k", j), in1=k[:, j, :],
                                             op0=ALU.mult, op1=ALU.mult).then_inc(rkr, 1)
                dve.tensor_copy(v[:], m[:, 4:6, :]).then_inc(step, 1)
                dve.wait_ge(rkr_sum, 1)
                dve.wait_ge(step, 12)
                for j in range(2):
                    dve.tensor_tensor(bonus[:, j, :], banks[6 + j][:, :], v[:, j, :], ALU.mult).then_inc(step, 1)
                dve.wait_ge(kk_root, 2)
                dve.tensor_scalar(t2[:], t2[:], 1e-12, None, ALU.max).then_inc(step, 1)
                dve.wait_ge(step, 15)
                dve.reciprocal(t2[:], t2[:]).then_inc(step, 1)
                dve.wait_ge(step, 16)
                dve.tensor_tensor(kk[:], kk[:], t2[:], ALU.mult).then_inc(step, 1)
                dve.wait_ge(step, 17)
                dve.wait_ge(before_exp, 1)
                dve.scalar_tensor_tensor(out=a_in[:], in0=kk[:], scalar=-1.0, in1=t1[:], op0=ALU.mult, op1=ALU.mult)\
                   .then_inc(step, 1)
                dve.tensor_tensor(a[:], a[:], kk[:], ALU.mult).then_inc(step, 1)
                dve.wait_ge(step, 19)
                dve.wait_ge(cum_neg_exp, 1)
                dve.tensor_tensor(b_out[:], a[:], log_w[:], ALU.mult).then_inc(step, 1)
                dve.tensor_tensor(k_out[:], k, log_w[:], ALU.mult).then_inc(step, 1)
                dve.wait_ge(cum_exp, 1)
                dve.tensor_tensor(r_in[:], m[:, 0:2, :], cum[:], ALU.mult).then_inc(step, 1)
                dve.tensor_copy(fade[:], cum[:, :, RW_C - 1::RW_C]).then_inc(step, 1)
                del steps

            @block.scalar
            def _(act):
                act.wait_ge(mixed, 1)
                act.activation(m[0:32, 6, :], m[0:32, 6, :], ACT.Tanh).then_inc(squashed, 1)
                act.activation(m[64:128, 6, :], m[64:128, 6, :], ACT.Sigmoid).then_inc(squashed, 1)
                for j in range(2):
                    act.wait_ge(low_rank, j + 1)
                    act.activation(log_w[:, j, :], banks[j][:, :], ACT.Sigmoid, bias=core.col("rw_w0", j)).then_inc(w_done, 1)
                    act.activation(a[:, j, :], banks[2 + j][:, :], ACT.Sigmoid, bias=core.col("rw_a0", j)).then_inc(a_done, 1)
                    act.activation(gate[:, j, :], banks[4 + j][:, :], ACT.Copy).then_inc(g_done, 1)
                act.wait_ge(kk_raw, 2)
                act.wait_ge(mixed, 7)
                act.activation(r[:], kk[:], ACT.Square).then_inc(kk_sq, 1)
                act.wait_ge(rkr_sum, 1)
                for j in range(2):
                    act.wait_ge(kk_sum, 1)
                    act.activation(t2[:, j, :], banks[j][:, :], ACT.Sqrt).then_inc(kk_root, 1)
                act.wait_ge(before, 1)
                act.activation(t1[:], t1[:], ACT.Exp).then_inc(before_exp, 1)
                act.activation(log_w[:], cum[:], ACT.Exp, scale=-1.0).then_inc(cum_neg_exp, 1)
                act.wait_ge(cum_neg_exp, 1)
                act.activation(cum[:], cum[:], ACT.Exp).then_inc(cum_exp, 1)

            @block.tensor
            def _(pe):
                pe.wait_ge(squashed, 2)
                for j in range(2):
                    cols = slice(j * P, (j + 1) * P)
                    pe.matmul(banks[j][:, :], lora_sb[0:32, cols], m[0:32, 6, :], start=True, stop=True)
                    pe.matmul(banks[2 + j][:, :], lora_sb[32:64, cols], m[32:64, 6, :], start=True, stop=True)
                    pe.matmul(banks[4 + j][:, :], lora_sb[64:128, cols], m[64:128, 6, :], start=True, stop=True)\
                      .then_inc(low_rank, 1)
                pe.wait_ge(rkr, 2)
                for j in range(2):
                    mm = pe.matmul(banks[6 + j][:, :], core.const("head_ones"), t2[:, j, :], start=True, stop=True)
                mm.then_inc(rkr_sum, 1)
                pe.wait_ge(kk_sq, 1)
                pe.wait_ge(w_done, 2)
                for j in range(2):
                    mm = pe.matmul(banks[j][:, :], core.const("head_ones"), r[:, j, :], start=True, stop=True)
                mm.then_inc(kk_sum, 1)


def unit(u):
    return slice(u * RW_C, (u + 1) * RW_C)


def each_head(pe, bank, lhs, rhs, start=True, stop=True):
    for e in range(2):
        rows = slice(HD * e, HD * e + HD)
        mm = pe.matmul(bank[rows], lhs(rows, e), rhs(rows, e), start=start, stop=stop)
    return mm


def rwkv_products(core, name, jobs):
    banks = core.banks
    with core.stage("made", "taken") as (block, made, taken):
        @block.tensor
        def _(pe):
            for n, (lhs, rhs, _, _) in enumerate(jobs):
                for j in range(2):
                    k = 2 * n + j
                    if k >= 8:
                        pe.wait_ge(taken, k - 7)
                    for c in range(NC):
                        tok = unit(c)
                        mm = each_head(pe, banks[k % 8][:, tok], lambda r, e: lhs[r, j, tok],
                                       lambda r, e: rhs[r, j, tok] if rhs is not None
                                       else core.const("ident")[r, HD * e:HD * e + HD])
                    mm.then_inc(made, 1)

        @block.vector
        def _(dve):
            for n, (_, _, mask, out) in enumerate(jobs):
                for j in range(2):
                    dve.wait_ge(made, 2 * n + j + 1)
                    dst = out[:, NC * j:NC * (j + 1), :]
                    src = banks[(2 * n + j) % 8][:, :].rearrange("p (c t) -> p c t", c=NC)
                    if mask is None:
                        dve.tensor_copy(dst, src).then_inc(taken, 1)
                    else:
                        dve.tensor_tensor(dst, src, spread(mask, 1, NC), ALU.mult).then_inc(taken, 1)


def rwkv_inverse(core, lab, lab_t, t_inv, tt_inv, level, y):
    banks = core.banks

    def level_mask(m, turned):
        pair = {1: (1, 0), 2: (1, 1), 4: (4, 0), 8: (4, 1), 16: (16, 0), 32: (16, 1)}[m]
        name = f"rw_level{'T' if turned else ''}_{pair[0]}_{2 * pair[0]}"
        return spread(core.const(name)[:, RW_C * pair[1]:RW_C * (pair[1] + 1)], 1, RU)

    with core.stage("masked", "t_done", "y_done", "y_taken", "z_done", "zt_done") as (
            block, masked, t_done, y_done, y_taken, z_done, zt_done):
        sizes = [2, 4, 8, 16, 32]

        @block.vector
        def _(dve):
            eye = spread(core.const("rw_eye")[:, 0:RW_C], 1, RU)
            dve.tensor_tensor(t_inv[:], lab[:], level_mask(1, False), ALU.mult).then_inc(masked, 1)
            dve.tensor_tensor(tt_inv[:], lab_t[:], level_mask(1, True), ALU.mult).then_inc(masked, 1)
            dve.wait_ge(masked, 2)
            dve.tensor_tensor(t_inv[:], t_inv[:], eye, ALU.add).then_inc(t_done, 1)
            dve.tensor_tensor(tt_inv[:], tt_inv[:], eye, ALU.add).then_inc(t_done, 1)
            for n, m in enumerate(sizes):
                if n:
                    dve.wait_ge(y_done, 2 * n)
                dve.tensor_tensor(level[:], lab_t[:], level_mask(m, True), ALU.mult).then_inc(masked, 1)
                for j in range(2):
                    units = slice(NC * j, NC * (j + 1))
                    dve.wait_ge(z_done, 2 * n + j + 1)
                    dve.wait_ge(t_done, 2 + 4 * n)
                    dve.tensor_tensor(t_inv[:, units, :], t_inv[:, units, :],
                                      banks[2 + j][:, :].rearrange("p (c t) -> p c t", c=NC), ALU.add).then_inc(t_done, 1)
                    dve.wait_ge(zt_done, 2 * n + 2)
                    dve.tensor_tensor(tt_inv[:, units, :], tt_inv[:, units, :],
                                      banks[4 + j][:, :].rearrange("p (c t) -> p c t", c=NC), ALU.add).then_inc(t_done, 1)

        @block.scalar
        def _(act):
            for n in range(len(sizes)):
                for j in range(2):
                    act.wait_ge(y_done, 2 * n + j + 1)
                    if n:
                        act.wait_ge(zt_done, 2 * n)
                    act.activation(y[:, NC * j:NC * (j + 1), :], banks[j][:, :].rearrange("p (c t) -> p c t", c=NC),
                                   ACT.Copy).then_inc(y_taken, 1)

        @block.tensor
        def _(pe):
            for n in range(len(sizes)):
                pe.wait_ge(masked, 3 + n)
                pe.wait_ge(t_done, 2 + 4 * n)
                for j in range(2):
                    for c in range(NC):
                        u = NC * j + c
                        mm = each_head(pe, banks[j][:, unit(c)], lambda r, e: level[r, u, :], lambda r, e: t_inv[r, u, :])
                    mm.then_inc(y_done, 1)
                for j in range(2):
                    pe.wait_ge(y_taken, 2 * n + j + 1)
                    for c in range(NC):
                        u = NC * j + c
                        mm = each_head(pe, banks[2 + j][:, unit(c)], lambda r, e: tt_inv[r, u, :], lambda r, e: y[r, u, :])
                    mm.then_inc(z_done, 1)
                    for c in range(NC):
                        u = NC * j + c
                        mm = each_head(pe, banks[4 + j][:, unit(c)], lambda r, e: y[r, u, :], lambda r, e: tt_inv[r, u, :])
                    mm.then_inc(zt_done, 1)


def rwkv_scan(core, a_in, r_in, lak_t, lrb_t, lrk_t, tt_inv, b_tok, k_tok, v_tok, fade, state, x, sa, o):
    banks = core.banks
    with core.stage("x_made", "x_taken", "sa_made", "sa_taken", "o_made", "o_taken", "s_made", "s_added", "s_faded",
                    "cleared") as (block, x_made, x_taken, sa_made, sa_taken, o_made, o_taken, s_made, s_added, s_faded,
                                   cleared):
        @block.tensor
        def _(pe):
            pe.wait_ge(cleared, 1)
            for c in range(NC):
                tok = unit(c)
                if c:
                    pe.wait_ge(s_faded, 2 * c)
                for j in range(2):
                    u = NC * j + c
                    each_head(pe, banks[0][:, unit(j)], lambda r, e: lak_t[r, u, :], lambda r, e: v_tok[r, u, :], stop=False)
                    mm = each_head(pe, banks[0][:, unit(j)], lambda r, e: a_in[r, j, tok], lambda r, e: state[r, j, :],
                                   start=False)
                mm.then_inc(x_made, 1)
                pe.wait_ge(x_taken, c + 1)
                for j in range(2):
                    u = NC * j + c
                    mm = each_head(pe, banks[1][:, unit(j)], lambda r, e: tt_inv[r, u, :], lambda r, e: x[r, j, :])
                mm.then_inc(sa_made, 1)
                pe.wait_ge(sa_taken, c + 1)
                if c:
                    pe.wait_ge(o_taken, c)
                for j in range(2):
                    u = NC * j + c
                    each_head(pe, banks[3][:, unit(j)], lambda r, e: b_tok[r, u, :], lambda r, e: sa[r, j, :], stop=False)
                    mm = each_head(pe, banks[3][:, unit(j)], lambda r, e: k_tok[r, u, :], lambda r, e: v_tok[r, u, :],
                                   start=False)
                mm.then_inc(s_made, 1)
                for j in range(2):
                    u = NC * j + c
                    each_head(pe, banks[2][:, unit(j)], lambda r, e: state[r, j, :], lambda r, e: r_in[r, j, tok], stop=False)
                    each_head(pe, banks[2][:, unit(j)], lambda r, e: sa[r, j, :], lambda r, e: lrb_t[r, u, :],
                              start=False, stop=False)
                    mm = each_head(pe, banks[2][:, unit(j)], lambda r, e: v_tok[r, u, :], lambda r, e: lrk_t[r, u, :],
                                   start=False)
                mm.then_inc(o_made, 1)

        @block.vector
        def _(dve):
            dve.memset(state[:], 0.0).then_inc(cleared, 1)
            for c in range(NC):
                dve.wait_ge(x_made, c + 1)
                dve.tensor_copy(x[:], banks[0][:, 0:P].rearrange("p (j t) -> p j t", j=2)).then_inc(x_taken, 1)
                dve.wait_ge(sa_made, c + 1)
                if c:
                    dve.wait_ge(o_made, c)
                dve.tensor_copy(sa[:], banks[1][:, 0:P].rearrange("p (j t) -> p j t", j=2)).then_inc(sa_taken, 1)
                dve.wait_ge(s_made, c + 1)
                dve.wait_ge(o_made, c + 1)
                dve.tensor_tensor(state[:], state[:], banks[3][:, 0:P].rearrange("p (j t) -> p j t", j=2), ALU.add)\
                   .then_inc(s_added, 1)
                dve.wait_ge(s_added, c + 1)
                for j in range(2):
                    dve.tensor_scalar(state[:, j, :], state[:, j, :], fade[:, j, c:c + 1], None, ALU.mult)\
                       .then_inc(s_faded, 1)

        @block.scalar
        def _(act):
            for c in range(NC):
                act.wait_ge(o_made, c + 1)
                act.activation(o[:, :, unit(c)], banks[2][:, 0:P].rearrange("p (j t) -> p j t", j=2), ACT.Copy)\
                   .then_inc(o_taken, 1)


def rwkv_output(core, o, bonus, gate, mix):
    banks = core.banks
    with core.room(rw_sq=[P, 2, SEQ], rw_rstd=[P, 2, SEQ]) as (sq, rstd), \
            core.stage("summed", "centered", "squared", "sq_summed", "var_done", "root_done", "inverted", "scaled",
                       "shifted", "bonused") as (block, summed, centered, squared, sq_summed, var_done, root_done,
                                                 inverted, scaled, shifted, bonused):
        @block.tensor
        def _(pe):
            for j in range(2):
                mm = pe.matmul(banks[j][:, :], core.const("head_ones"), o[:, j, :], start=True, stop=True)
            mm.then_inc(summed, 1)
            for j in range(2):
                pe.wait_ge(squared, j + 1)
                mm = pe.matmul(banks[2 + j][:, :], core.const("head_ones"), sq[:, j, :], start=True, stop=True)
                mm.then_inc(sq_summed, 1)

        @block.vector
        def _(dve):
            dve.wait_ge(summed, 1)
            for j in range(2):
                dve.scalar_tensor_tensor(out=o[:, j, :], in0=banks[j][:, :], scalar=-1.0 / HD, in1=o[:, j, :],
                                         op0=ALU.mult, op1=ALU.add).then_inc(centered, 1)
            for j in range(2):
                dve.wait_ge(sq_summed, j + 1)
                dve.tensor_scalar(rstd[:, j, :], banks[2 + j][:, :], 1.0 / HD, RW_LN_EPS, ALU.mult, ALU.add)\
                   .then_inc(var_done, 1)
            for j in range(2):
                dve.wait_ge(root_done, j + 1)
                dve.reciprocal(rstd[:, j, :], rstd[:, j, :]).then_inc(inverted, 1)
            for j in range(2):
                dve.wait_ge(inverted, j + 1)
                dve.scalar_tensor_tensor(out=o[:, j, :], in0=o[:, j, :], scalar=core.col("rw_lnx_w", j), in1=rstd[:, j, :],
                                         op0=ALU.mult, op1=ALU.mult).then_inc(scaled, 1)
            for j in range(2):
                dve.wait_ge(scaled, j + 1)
                dve.scalar_tensor_tensor(out=o[:, j, :], in0=o[:, j, :], scalar=core.col("rw_lnx_b", j), in1=bonus[:, j, :],
                                         op0=ALU.add, op1=ALU.add).then_inc(shifted, 1)
            for j in range(2):
                dve.wait_ge(shifted, j + 1)
                dve.tensor_tensor(mix[:, 3 + j, :], o[:, j, :], gate[:, j, :], ALU.mult).then_inc(bonused, 1)

        @block.scalar
        def _(act):
            for j in range(2):
                act.wait_ge(centered, j + 1)
                act.activation(sq[:, j, :], o[:, j, :], ACT.Square).then_inc(squared, 1)
            for j in range(2):
                act.wait_ge(var_done, j + 1)
                act.activation(rstd[:, j, :], rstd[:, j, :], ACT.Sqrt).then_inc(root_done, 1)


def rwkv(core, w, h, lora, mix):
    two, by_unit = [P, 2, SEQ], [P, RU, RW_C]
    with core.room(rw_v=two, rw_gate=two, rw_bonus=two, rw_a_in=two, rw_b_out=two, rw_k_out=two, rw_r_in=two, rw_o=two,
                   rw_fade=[P, 2, NC]) as (v, gate, bonus, a_in, b_out, k_out, r_in, o, fade):
        rwkv_inputs(core, w, h, lora, o, v, gate, bonus, a_in, b_out, k_out, r_in, fade)
        with core.room(lab=by_unit, lab_t=by_unit, lak_t=by_unit, lrb_t=by_unit, lrk_t=by_unit, b_tok=by_unit,
                       k_tok=by_unit, v_tok=by_unit, t_inv=by_unit, tt_inv=by_unit, level=by_unit, rw_y=by_unit,
                       rw_state=[P, 2, HD], rw_x=[P, 2, HD], rw_sa=[P, 2, HD]) as (
                lab, lab_t, lak_t, lrb_t, lrk_t, b_tok, k_tok, v_tok, t_inv, tt_inv, level, y, state, x, sa):
            before = core.const("rw_masks")[:, 0:RW_C]
            until = core.const("rw_masks")[:, RW_C:2 * RW_C]
            after = core.const("rw_eye")[:, RW_C:2 * RW_C]
            rwkv_products(core, "rw", [
                (b_out, a_in, before, lab_t), (a_in, b_out, after, lab), (k_out, a_in, before, lak_t),
                (b_out, r_in, until, lrb_t), (k_out, r_in, until, lrk_t),
                (b_out, None, None, b_tok), (k_out, None, None, k_tok), (v, None, None, v_tok)])
            rwkv_inverse(core, lab, lab_t, t_inv, tt_inv, level, y)
            rwkv_scan(core, a_in, r_in, lak_t, lrb_t, lrk_t, tt_inv, b_tok, k_tok, v_tok, fade, state, x, sa, o)
        rwkv_output(core, o, bonus, gate, mix)


def causal_tap(n):
    return lambda b: b[:, n:n + SEQ]


def second_block(core, x, w):
    with core.room(h2=[P, DT, SEQ], mix2=[P, DT, SEQ]) as (h, mix):
        norm(core, "attn_norm", x, h, lambda k: core.col("attn_norm", k), eps=NORM_EPS, center=False)
        nsa(core, w["w_in_2"], h, w["cmp"], mix)
        moba(core, w["w_in_2"], h, mix)
        rwkv(core, w["w_in_2"], h, w["lora"], mix)
        gemm(core, "out2", w["w_out_2"], mix, [(0, SEQ)], lambda tile, n: h[:, bass.ds(tile, 1), :], DT, 4)
        residual(core, x, h, None)
    with core.room(h3=[P, DT, SEQ], y3=[P, DT, SEQ]) as (h, y):
        norm(core, "ffn_norm", x, h, lambda k: core.col("ffn_norm", k), eps=NORM_EPS, center=False)
        glu_ffn(core, "ffn2", w["ffn_w_in_2"], D_FF, 0, w["ffn_w_out_2"], h, y, SEQ + 2, lambda b: b[:, 2:SEQ + 2],
                [causal_tap(n) for n in range(3)], lambda t, n: core.col("ffn2_conv_w", t, n),
                lambda t: core.col("ffn2_conv_b", t), ACT.Silu)
        residual(core, x, y, None)
    norm(core, "final_norm", x, x, lambda k: core.col("final_norm", k), eps=NORM_EPS, center=False)


def conditioning(core, ada_w, mods):
    with core.room(cond=[P, DT, 2]) as (cond,):
        with core.stage("cond_done") as (block, cond_done):
            @block.scalar
            def _(act):
                at = COL_AT["c"]
                act.activation(cond[:].rearrange("p k w -> p (k w)"), core.cols_sb[:, at:at + 2 * DT], ACT.Silu)\
                   .then_inc(cond_done, 1)
        for layer in range(DEPTH):
            gemm(core, f"ada{layer}", ada_w[layer], cond, [(0, 2)],
                 lambda tile, n: mods[layer][:, bass.ds(tile, 1), :].rearrange("p a w -> p (a w)"), 6 * DT, 8,
                 bias=lambda tile: core.col(f"ada_b{layer}", tile))
    with core.stage("raised") as (block, raised):
        @block.vector
        def _(dve):
            for layer in range(DEPTH):
                for part in (1, 4):
                    scale = mods[layer][:, part * DT:(part + 1) * DT, :]
                    dve.tensor_scalar(scale, scale, 1.0, None, ALU.add).then_inc(raised, 1)


def model(nc, x, ctx, const, cols, rows, lora, pos, ada_w, mix_w_in, mix_w_out, conf_w1, conf_w2, ffn_w_up, ffn_w_down,
          w_in_2, cmp_w1, cmp_w2, w_out_2, ffn_w_in_2, ffn_w_out_2, out):
    features = lambda a: a.rearrange("(k p) t -> p k t", p=P)
    with ExitStack() as stack:
        core = Core(nc, stack)
        mods = [stack.enter_context(nc.sbuf_tensor(f"mods{layer}", [P, 6 * DT, 2], F32)) for layer in range(DEPTH)]
        load(core, [(core.const_sb[:], const), (core.cols_sb[:], cols)])
        conditioning(core, ada_w, mods)

        def mod(layer, part, who=0):
            return lambda k: mods[layer][:, part * DT + k, who:who + 1]

        def finish_half(name, layer, n, x_sb, y_sb):
            residual(core, x_sb, y_sb, mod(layer, 3 * n + 2))
            norm(core, name, x_sb, x_sb, lambda k: core.col("post_ln_g", k, 2 * layer + n),
                 lambda k: core.col("post_ln_b", k, 2 * layer + n))

        def ffn(layer, x_sb):
            with core.room(**{f"ffn_x{layer}": [P, DT, SEQ], f"ffn_y{layer}": [P, DT, SEQ]}) as (h, y):
                modulate(core, x_sb, mod(layer, 3), mod(layer, 4), h)
                glu_ffn(core, f"ffn{layer}", ffn_w_up[layer], D_FF, 0, ffn_w_down[layer], h, y, GRID_PAD,
                        grid_window(1, 1), GRID_TAPS, lambda t, n: core.col(f"ffn_conv_w{layer}", t, n),
                        lambda t: core.col("ffn_conv_b", t, layer), ACT.Gelu)
                finish_half(f"ln_ffn{layer}", layer, 1, x_sb, y)

        with core.room(x_sb=[P, DT, SEQ]) as (x_sb,):
            with core.room(h0=[P, DT, TOK], rows_sb=[P, 72]) as (h, rows_sb):
                load(core, [(h[:, :, 0:SEQ], features(x)), (h[:, :, SEQ:TOK], features(ctx)), (rows_sb[:], rows)])
                modulate(core, h[:, :, 0:SEQ], mod(0, 0), mod(0, 1), h[:, :, 0:SEQ])
                modulate(core, h[:, :, SEQ:TOK], mod(0, 0, 1), mod(0, 1, 1), h[:, :, SEQ:TOK])
                even_mixer(core, mix_w_in[0], mix_w_out[0], h, x_sb, rows_sb)
            with core.room(x_again=[P, DT, SEQ]) as (x_again,):
                load(core, [(x_again[:], features(x))])
                with core.stage("scaled", "added") as (block, scaled, added):
                    @block.scalar
                    def _(act):
                        for k in range(DT):
                            act.activation(x_again[:, k, :], x_again[:, k, :], ACT.Identity, scale=ALPHA)\
                               .then_inc(scaled, 1)

                    @block.vector
                    def _(dve):
                        for k in range(DT):
                            dve.wait_ge(scaled, k + 1)
                            dve.scalar_tensor_tensor(out=x_sb[:, k, :], in0=x_sb[:, k, :], scalar=mod(0, 2)(k),
                                                     in1=x_again[:, k, :], op0=ALU.mult, op1=ALU.add).then_inc(added, 1)
            norm(core, "ln_mix0", x_sb, x_sb, lambda k: core.col("post_ln_g", k), lambda k: core.col("post_ln_b", k))
            ffn(0, x_sb)
            with core.room(h1=[P, DT, SEQ], y1=[P, DT, SEQ]) as (h, y):
                modulate(core, x_sb, mod(1, 0), mod(1, 1), h)
                conformer(core, conf_w1[0], conf_w2[0], h, y)
                finish_half("ln_mix1", 1, 0, x_sb, y)
            ffn(1, x_sb)
            second_block(core, x_sb, {"w_in_2": w_in_2[0], "cmp": {"pos": pos, "w1": cmp_w1, "w2": cmp_w2}, "lora": lora,
                                      "w_out_2": w_out_2[0], "ffn_w_in_2": ffn_w_in_2[0], "ffn_w_out_2": ffn_w_out_2[0]})
            with core.stage("stored") as (block, stored):
                @block.sync
                def _(sp):
                    sp.dma_start(features(out), x_sb[:]).then_inc(stored, 16)
                    sp.wait_ge(stored, 16)


WEIGHTS = {
    "ada_w": "ada_w", "mix_w_in": "mix_w_in", "mix_w_out": "mix_w_out", "conf_w1": "conf_w1", "conf_w2": "conf_w2",
    "ffn_w_up": "ffn_w_up", "ffn_w_down": "ffn_w_down", "w_in_2": "w_in_2", "cmp_w1": "nsa_cmp_w1_2",
    "cmp_w2": "nsa_cmp_w2_2", "w_out_2": "w_out_2", "ffn_w_in_2": "ffn_w_in_2", "ffn_w_out_2": "ffn_w_out_2",
}


def laid_out(inputs):
    vectors = {name: inputs[name] for name in COLS if name in inputs}
    vectors["c"] = np.concatenate([inputs["c"], inputs["c_ctx"][None]])
    for layer in range(DEPTH):
        vectors[f"ada_b{layer}"] = inputs["ada_b"][layer]
        vectors[f"ffn_conv_w{layer}"] = inputs["ffn_conv_w"][layer]
    for name, source in (("attn_norm", "attn_norm_2"), ("ffn_norm", "ffn_norm_2"), ("final_norm", "final_norm_2"),
                         ("ffn2_conv_w", "ffn_conv_w_2"), ("ffn2_conv_b", "ffn_conv_b_2"), ("nsa_gain", "nsa_out_gain_2"),
                         ("moba_gain", "moba_out_gain_2")):
        vectors[name] = inputs[source]
    for name in ("mu", "w0", "a0", "k_k", "k_a", "r_k", "lnx_w", "lnx_b"):
        vectors[f"rw_{name}"] = inputs[f"rw_{name}_2"]
    arrays = {
        "x": np.ascontiguousarray(np.transpose(inputs["x"][0])),
        "ctx": np.ascontiguousarray(np.transpose(inputs["ctx"][0])),
        "const": constants(),
        "cols": columns(vectors),
        "rows": np.ascontiguousarray(np.concatenate([
            np.broadcast_to(np.reshape(inputs["ssd_dt_bias"], (1, 32)), (P, 32)),
            np.broadcast_to(np.reshape(inputs["ssd_a_log"], (1, 32)), (P, 32)),
            np.transpose(np.repeat(np.reshape(inputs["ssd_d"], (DT, 2)), SSD_P, axis=1))], axis=1)),
        "lora": np.ascontiguousarray(np.concatenate([inputs["rw_w2_2"][0], inputs["rw_a2_2"][0], inputs["rw_g2_2"][0]])),
        "pos": np.ascontiguousarray(np.transpose(np.reshape(inputs["nsa_cmp_pos_2"], (2, CMP_LEN // 2, P)), (0, 2, 1))),
    }
    for name, source in WEIGHTS.items():
        arrays[name] = np.ascontiguousarray(inputs[source])
    return arrays


def kernel(**inputs):
    import concourse.bacc as bacc
    from concourse.bass_utils import run_bass_kernel_spmd

    nc = bacc.Bacc("TRN2", target_bir_lowering=False, num_devices=1)
    arrays = {f"in_{name}": a for name, a in laid_out({k: np.asarray(v) for k, v in inputs.items()}).items()}
    args = [nc.dram_tensor(name, a.shape, mybir.dt.from_np(a.dtype), kind="ExternalInput").ap()
            for name, a in arrays.items()]
    out = nc.dram_tensor("out", (D, SEQ), F32, kind="ExternalOutput").ap()
    model(nc, *args, out)
    result = run_bass_kernel_spmd(nc, [arrays], core_ids=[0])
    return np.ascontiguousarray(np.transpose(result.results[0]["out"]))[None]
```

```python
from contextlib import ExitStack, contextmanager


import numpy as np

import concourse.bass as bass
from concourse import mybir

F32 = mybir.dt.float32
F32R = mybir.dt.float32r
U32 = mybir.dt.uint32
ALU = mybir.AluOpType
ACT = mybir.ActivationFunctionType
AX_X = mybir.AxisListType.X

P = 128
D = 1024
DT = D // P
SEQ = 512
CTX = 256
TOK = SEQ + CTX
DEPTH = 2
ALPHA = (2 * DEPTH) ** 0.25
EPS = 1e-5
D_FF = 2816
FT = D_FF // P
GRID_W = 64
ROWS = SEQ // GRID_W

SSD_HEADS = 16
SSD_P = 64
SSD_IN = SSD_HEADS * SSD_P
SSD_G = 2
SSD_N = 128
SSD_XBC = SSD_IN + 2 * SSD_G * SSD_N
SSD_K = 5
HG_HEADS = 8
MIX_AT = {}
at = 0
for part, size in (("z", SSD_IN), ("xbc", SSD_XBC), ("dt", 2 * SSD_HEADS), ("q", D), ("f", 2 * D), ("v", D), ("g", D)):
    MIX_AT[part] = at
    at += size
CONF_K = 31
CHUNK = 128
NEG = -1e30

HD = 64
NSA_H, KV_H, RW_H, MOBA_H = 6, 2, 4, 6
NORM_EPS = 1e-6
RW_C = 64
RW_DECAY = 0.606531
RW_LN_EPS = 64e-5
CMP_LEN, CMP_STRIDE, CMP_HID = 32, 16, 256
N_CMP = (SEQ - CMP_LEN) // CMP_STRIDE + 1
TT = SEQ // P
AT2 = {}
at = 0
for part, size in (("q", 384), ("kc", 128), ("vc", 128), ("ks", 128), ("vs", 128), ("kw", 128), ("vw", 128), ("gt", 18),
                   ("rw", 896), ("mq", 384), ("mk", 384), ("mv", 384)):
    AT2[part] = at
    at += size

LEVELS = [CHUNK >> (n + 1) for n in range(7)]
CONST = ["ident", "ones", "head_ones", "until", "since", "neg_until", "neg_since"]
ALWAYS = len(CONST)
MIXER_CONST = [f"left_right_{m}" for m in LEVELS] + [f"right_left_{m}" for m in LEVELS]
ODD_CONST = ["rw_masks", "rw_level_1_2", "rw_level_4_8", "rw_level_16_32", "rw_levelT_1_2", "rw_levelT_4_8",
          "rw_levelT_16_32", "cmp_mask", "cmp_valid", "rw_eye"]
CONST += MIXER_CONST + ODD_CONST
CONST_AT = {name: n for n, name in enumerate(CONST)}

COLS = {
    "ada_b0": (1, 6 * D), "ada_b1": (1, 6 * D), "post_ln_g": (4, D), "post_ln_b": (4, D), "ssd_conv_w": (SSD_K, SSD_XBC), "ssd_conv_b": (1, SSD_XBC),
    "ssd_norm_w": (1, D), "hg_norm_w": (1, D), "conf_b1": (2, D), "conf_dw_w": (CONF_K, D), "conf_dw_b": (1, D),
    "conf_ln_g": (1, D), "conf_ln_b": (1, D), "conf_b2": (1, D), "ffn_conv_w0": (9, D_FF), "ffn_conv_w1": (9, D_FF),
    "ffn_conv_b": (2, D_FF), "attn_norm": (1, D), "ffn_norm": (1, D), "final_norm": (1, D), "ffn2_conv_w": (3, D_FF),
    "ffn2_conv_b": (1, D_FF), "rw_mu": (1, 896), "rw_w0": (1, 256), "rw_a0": (1, 256), "rw_k_k": (1, 256),
    "rw_k_a": (1, 256), "rw_r_k": (1, 256), "rw_lnx_w": (1, 256), "rw_lnx_b": (1, 256), "nsa_gain": (1, 384),
    "moba_gain": (1, 384), "c": (2, D),
}
COL_AT = {}
at = 0
for name, (rows, length) in COLS.items():
    COL_AT[name] = at
    at += rows * length // P
N_COLS = at


def constants():
    s, t = np.meshgrid(np.arange(P), np.arange(P), indexing="ij")
    out = {
        "ident": s == t, "ones": s >= 0, "head_ones": s // HD == t // HD, "until": s <= t, "since": s >= t,
        "neg_until": np.where(s <= t, 0, NEG), "neg_since": np.where(s >= t, 0, NEG),
    }
    for m in LEVELS:
        lr = (s // (2 * m) == t // (2 * m)) & (s % (2 * m) < m) & (t % (2 * m) >= m)
        out[f"left_right_{m}"], out[f"right_left_{m}"] = lr, lr.T
    s, t = np.meshgrid(np.arange(P) % RW_C, np.arange(RW_C), indexing="ij")
    out["rw_masks"] = np.concatenate([s < t, s <= t], axis=1)

    def below(m, a, b):
        return (a // (2 * m) == b // (2 * m)) & (a % (2 * m) >= m) & (b % (2 * m) < m)

    for m in (1, 4, 16):
        out[f"rw_level_{m}_{2 * m}"] = np.concatenate([below(m, s, t), below(2 * m, s, t)], axis=1)
        out[f"rw_levelT_{m}_{2 * m}"] = np.concatenate([below(m, t, s), below(2 * m, t, s)], axis=1)
    out["rw_eye"] = np.concatenate([s == t, s > t], axis=1)
    tok = np.arange(P)[:, None, None] + P * np.arange(TT)[None, :, None]
    seen = CMP_STRIDE * np.arange(N_CMP + 1)[None, None, :] + CMP_LEN - 1 <= tok
    seen[:, :, N_CMP:] = False
    out["cmp_mask"] = np.where(seen, 0, NEG).reshape(P, P)
    out["cmp_valid"] = np.broadcast_to(seen.any(axis=2, keepdims=True), seen.shape).reshape(P, P)
    return np.stack([out[n].astype(np.float32) for n in CONST], axis=1)


def columns(arrays):
    out = []
    for name, (rows, length) in COLS.items():
        a = np.reshape(arrays[name], (rows, length // P, P))
        out.append(np.transpose(a, (2, 1, 0)).reshape(P, -1))
    return np.ascontiguousarray(np.concatenate(out, axis=1))


class Core:

    def __init__(self, nc, ctx):
        self.nc = nc
        self.stages = self.rooms = 0
        self.banks = [ctx.enter_context(nc.psum_tensor(f"bank{i}", [P, SEQ], F32)) for i in range(8)]
        self.const_sb = ctx.enter_context(nc.sbuf_tensor("const_sb", [P, ALWAYS, P], F32))
        self.some = {}
        self.cols_sb = ctx.enter_context(nc.sbuf_tensor("cols_sb", [P, N_COLS], F32))

    def const(self, name):
        return self.const_sb[:, CONST_AT[name], :] if CONST_AT[name] < ALWAYS else self.some[name]

    @contextmanager
    def more_constants(self, names, source):
        first = CONST_AT[names[0]]
        with self.room(**{f"const_{names[0]}": [P, len(names), P]}) as (buf,):
            load(self, [(buf[:], source[:, first:first + len(names), :])])
            self.some = {name: buf[:, n, :] for n, name in enumerate(names)}
            yield

    def col(self, name, tile, row=0):
        start = COL_AT[name] + tile * COLS[name][0] + row
        return self.cols_sb[:, bass.ds(start, 1)]

    @contextmanager
    def room(self, **shapes):
        self.rooms += 1
        n = self.rooms
        with ExitStack() as ctx:
            yield [ctx.enter_context(self.nc.sbuf_tensor(f"{name}_{n}", shape, F32)) for name, shape in shapes.items()]

    @contextmanager
    def split_room(self, **shapes):
        self.rooms += 1
        n = self.rooms
        with ExitStack() as ctx:
            yield [tuple(ctx.enter_context(self.nc.sbuf_tensor(f"{name}_{part}_{n}", shape, F32R))
                         for part in ("high", "low")) for name, shape in shapes.items()]

    @contextmanager
    def stage(self, *names):
        self.stages += 1
        with self.nc.cleanup_on_exit():
            sems = [self.nc.alloc_semaphore(f"{n}_{self.stages}") for n in names]
            with self.nc.Block() as block:
                yield [block, *sems]


def three_passes(pe, bank, weights, acts, start, stop):
    pe.matmul(bank, weights[0], acts[0], start=start, stop=False)
    pe.matmul(bank, weights[0], acts[1], start=False, stop=False)
    return pe.matmul(bank, weights[1], acts[0], start=False, stop=stop)


def gemm(core, name, weights, acts, spans, out, tiles, unroll, bias=None, func=ACT.Identity, more=None):
    kt = weights.shape[0] // P
    w = weights.rearrange("(k p) f -> p k f", p=P)
    steps = tiles // unroll
    slots = 2 if unroll % 2 == 0 or steps == 1 else unroll
    rings = min(unroll, 4) if steps == 1 else unroll
    assert steps * unroll == tiles and unroll * len(spans) <= 8
    names = [f"slab_in{u}" for u in range(rings)] + ["high_done", "low_done", "tile_done", "banks_free", "slots_refilled"]
    with core.room(**{f"{name}_ring": [P, rings, kt, P]}) as (ring,), \
            core.split_room(**{f"{name}_w": [P, slots, kt, P]}) as ((high, low),), core.stage(*names) as (block, *sems):
        slab_in, (high_done, low_done, tile_done, banks_free, slots_refilled) = sems[:rings], sems[rings:]

        def bank(u, n):
            return core.banks[u * len(spans) + n][:, 0:spans[n][1]]

        def taken(k, start, size):
            source, at = (more, k - DT) if more and k >= DT else (acts, k)
            return [part[:, at, start:start + size] for part in source]

        @block.sync
        def _(sp):
            for u in range(unroll):
                if u >= rings:
                    sp.wait_ge(low_done, u - rings + 1)
                sp.dma_start(ring[:, u % rings], w[:, :, u * P:(u + 1) * P]).then_inc(slab_in[u % rings], 16)
            if steps > 1:
                with sp.Fori(1, steps) as i:
                    for u in range(unroll):
                        feature = sp.snap((i * unroll + u) * P)
                        sp.wait_ge(low_done, (i - 1) * unroll + u + 1)
                        sp.sem_inc(slots_refilled, 1)
                        sp.dma_start(ring[:, u], w[:, :, bass.ds(feature, P)]).then_inc(slab_in[u], 16)

        @block.vector
        def _(dve):
            with dve.Fori(0, steps) as i:
                for u in range(unroll):
                    dve.wait_ge(slab_in[u % rings], (i + 1 + u // rings) * 16)
                    dve.wait_ge(tile_done, i * unroll + u + 1)
                    dve.tensor_copy(high[:, u % slots], ring[:, u % rings]).then_inc(high_done, 1)

        @block.gpsimd
        def _(pool):
            with pool.Fori(0, steps) as i:
                for u in range(unroll):
                    pool.wait_ge(high_done, i * unroll + u + 1)
                    pool.tensor_tensor(low[:, u % slots], ring[:, u % rings], high[:, u % slots].bitcast(F32), ALU.subtract)\
                        .then_inc(low_done, 1)

        @block.tensor
        def _(pe):
            pe.sem_inc(tile_done, slots)
            with pe.Fori(0, steps) as i:
                for u in range(unroll):
                    pe.wait_ge(low_done, i * unroll + u + 1)
                    pe.wait_ge(banks_free, i * unroll + u + 1)
                    for n, (start, size) in enumerate(spans):
                        for k in range(kt):
                            mm = three_passes(pe, bank(u, n), [part[:, u % slots, k, :] for part in (high, low)],
                                              taken(k, start, size), k == 0, k == kt - 1)
                    mm.then_inc(tile_done, 1)

        @block.scalar
        def _(act):
            act.sem_inc(banks_free, unroll)
            with act.Fori(0, steps) as i:
                for u in range(unroll):
                    act.wait_ge(tile_done, i * unroll + u + 1 + slots)
                    tile = i * unroll + u
                    for n in range(len(spans)):
                        b = bias(tile) if bias else 0.0
                        done = act.activation(out(tile, n), bank(u, n), func, bias=b)
                    done.then_inc(banks_free, 1)


def gemm_tokens(core, name, weights, acts, tiles, out, width):
    kt = weights.shape[0] // P
    w = weights.rearrange("(k p) f -> p k f", p=P)
    slabs = weights.shape[1] // width
    slots = min(slabs, 2)
    with core.room(**{f"{name}_ring": [P, slots, kt, width]}) as (ring,), \
            core.split_room(**{f"{name}_w": [P, slots, kt, width]}) as ((high, low),), \
            core.stage("slab_in0", "slab_in1", "high_done", "low_done", "tile_done", "banks_free") as (
                block, slab_in0, slab_in1, high_done, low_done, tile_done, banks_free):
        slab_in = [slab_in0, slab_in1]

        @block.sync
        def _(sp):
            for s in range(slabs):
                if s >= 2:
                    sp.wait_ge(low_done, s - 1)
                sp.dma_start(ring[:, s % 2], w[:, :, s * width:(s + 1) * width]).then_inc(slab_in[s % 2], 16)

        @block.vector
        def _(dve):
            for s in range(slabs):
                dve.wait_ge(slab_in[s % 2], 16 * (s // 2 + 1))
                if s >= 2:
                    dve.wait_ge(tile_done, (s - 1) * tiles)
                dve.tensor_copy(high[:, s % 2], ring[:, s % 2]).then_inc(high_done, 1)

        @block.gpsimd
        def _(pool):
            for s in range(slabs):
                pool.wait_ge(high_done, s + 1)
                pool.tensor_tensor(low[:, s % 2], ring[:, s % 2], high[:, s % 2].bitcast(F32), ALU.subtract)\
                    .then_inc(low_done, 1)

        @block.tensor
        def _(pe):
            for s in range(slabs):
                pe.wait_ge(low_done, s + 1)
                for t in range(tiles):
                    n = s * tiles + t
                    if n >= 8:
                        pe.wait_ge(banks_free, n - 7)
                    for k in range(kt):
                        bank = core.banks[n % 8][:, 0:width]
                        pe.matmul(bank, acts[0][:, k, t * P:(t + 1) * P], high[:, s % 2, k, :], start=(k == 0), stop=False)
                        pe.matmul(bank, acts[0][:, k, t * P:(t + 1) * P], low[:, s % 2, k, :], start=False, stop=False)
                        mm = pe.matmul(bank, acts[1][:, k, t * P:(t + 1) * P], high[:, s % 2, k, :], start=False,
                                       stop=(k == kt - 1))
                    mm.then_inc(tile_done, 1)

        @block.scalar
        def _(act):
            for n in range(slabs * tiles):
                act.wait_ge(tile_done, n + 1)
                act.activation(out(n % tiles, n // tiles), core.banks[n % 8][:, 0:width], ACT.Identity)\
                   .then_inc(banks_free, 1)


def split(core, parts, modulation=None):
    with core.stage("modulated", "high_done", "low_done") as (block, modulated, high_done, low_done):
        tiles = [(src[:, k, :], high[:, k, :], low[:, k, :], k, shift_scale)
                 for (src, (high, low)), shift_scale in zip(parts, modulation or [None] * len(parts))
                 for k in range(src.shape[1])]

        @block.vector
        def _(dve):
            def take_low(n):
                src, high, low, _, _ = tiles[n]
                dve.wait_ge(high_done, n + 1)
                dve.tensor_tensor(low, src, high.bitcast(F32), ALU.subtract).then_inc(low_done, 1)

            for n, (src, _, _, k, shift_scale) in enumerate(tiles):
                if shift_scale:
                    shift, scale = shift_scale
                    dve.tensor_scalar(src, src, scale(k), shift(k), ALU.mult, ALU.add).then_inc(modulated, 1)
                if n >= 2 and n % 2 == 0:
                    take_low(n - 2)
            take_low(len(tiles) - 2)

        @block.scalar
        def _(act):
            for n, (src, high, _, _, shift_scale) in enumerate(tiles):
                if shift_scale:
                    act.wait_ge(modulated, n + 1)
                act.activation(high, src, ACT.Copy).then_inc(high_done, 1)

        @block.gpsimd
        def _(pool):
            for n, (src, high, low, _, _) in enumerate(tiles):
                if n % 2 == 1:
                    pool.wait_ge(high_done, n + 1)
                    pool.tensor_tensor(low, src, high.bitcast(F32), ALU.subtract).then_inc(low_done, 1)


def modulate(core, x, shift, scale1, out):
    with core.stage("modulated") as (block, modulated):
        @block.vector
        def _(dve):
            for k in range(DT):
                dve.tensor_scalar(out[:, k, :], x[:, k, :], scale1(k), shift(k), ALU.mult, ALU.add).then_inc(modulated, 1)


def residual(core, x, y, gate):
    with core.stage("scaled") as (block, scaled):
        if gate is None:
            @block.vector
            def _(dve):
                for k in range(DT):
                    dve.tensor_tensor(x[:, k, :], x[:, k, :], y[:, k, :], ALU.add)
            return

        @block.scalar
        def _(act):
            for k in range(DT):
                act.activation(x[:, k, :], x[:, k, :], ACT.Identity, scale=ALPHA).then_inc(scaled, 1)

        @block.vector
        def _(dve):
            for k in range(DT):
                dve.wait_ge(scaled, k + 1)
                dve.scalar_tensor_tensor(out=x[:, k, :], in0=y[:, k, :], scalar=gate(k), in1=x[:, k, :],
                                         op0=ALU.mult, op1=ALU.add)


def norm(core, name, src, out, gain, bias=None, eps=EPS, center=True, func=ACT.Identity):
    total, squares = core.banks[0], core.banks[1]
    ones = core.const("ones")
    with core.room(**{f"{name}_sq": [P, DT, SEQ], f"{name}_mean": [P, SEQ], f"{name}_rstd": [P, SEQ]}) as (sq, mean, rstd), \
            core.stage("summed", "mean_done", "centered", "squared", "sq_summed", "var_done", "root_done", "inverse_done",
                       "scaled") as (block, summed, mean_done, centered, squared, sq_summed, var_done, root_done,
                                     inverse_done, scaled):
        @block.tensor
        def _(pe):
            if center:
                for k in range(DT):
                    mm = pe.matmul(total[:, :], ones, src[:, k, :], start=(k == 0), stop=(k == DT - 1))
                mm.then_inc(summed, 1)
            for k in range(DT):
                pe.wait_ge(squared, k + 1)
                mm = pe.matmul(squares[:, :], ones, sq[:, k, :], start=(k == 0), stop=(k == DT - 1))
            mm.then_inc(sq_summed, 1)

        @block.vector
        def _(dve):
            if center:
                dve.wait_ge(summed, 1)
                dve.tensor_scalar(mean[:, :], total[:, :], 1.0 / D, None, ALU.mult).then_inc(mean_done, 1)
                dve.wait_ge(mean_done, 1)
                for k in range(DT):
                    dve.tensor_tensor(out[:, k, :], src[:, k, :], mean[:, :], ALU.subtract).then_inc(centered, 1)
            dve.wait_ge(sq_summed, 1)
            dve.tensor_scalar(rstd[:, :], squares[:, :], 1.0 / D, eps, ALU.mult, ALU.add).then_inc(var_done, 1)
            dve.wait_ge(root_done, 1)
            dve.reciprocal(rstd[:, :], rstd[:, :]).then_inc(inverse_done, 1)
            dve.wait_ge(inverse_done, 1)
            for k in range(DT):
                dve.scalar_tensor_tensor(out=out[:, k, :], in0=(out if center else src)[:, k, :], scalar=gain(k),
                                         in1=rstd[:, :], op0=ALU.mult, op1=ALU.mult).then_inc(scaled, 1)

        @block.scalar
        def _(act):
            for k in range(DT):
                if center:
                    act.wait_ge(centered, k + 1)
                act.activation(sq[:, k, :], (out if center else src)[:, k, :], ACT.Square).then_inc(squared, 1)
            act.wait_ge(var_done, 1)
            act.activation(rstd[:, :], rstd[:, :], ACT.Sqrt).then_inc(root_done, 1)
            if bias is not None:
                for k in range(DT):
                    act.wait_ge(scaled, k + 1)
                    act.activation(out[:, k, :], out[:, k, :], func, bias=bias(k))


@contextmanager
def glu_ffn(core, name, w_up, gate_at, value_at, w_down, fill_x, y_of, width, interior, taps, conv_w, conv_b, func):
    slots = 4
    with core.split_room(**{f"{name}_h": [P, FT, SEQ]}) as (h,):
        w = w_up.rearrange("(k p) f -> p k f", p=P)
        with core.split_room(**{f"{name}_x": [P, DT, SEQ]}) as (x,):
            fill_x(x)
            with core.room(**{f"{name}_ring": [P, 2, DT, P], f"{name}_pad": [P, 2, width], f"{name}_acc": [P, 2, SEQ],
                              f"{name}_val": [P, 2, SEQ]}) as (ring, pad, acc, val), \
                    core.split_room(**{f"{name}_w": [P, slots, DT, P]}) as ((high, low),), \
                    core.stage("slab_in0", "slab_in1", "high_done", "low_done", "tile_done", "banks_free", "tapped0",
                               "tapped1", "active", "products", "h_high", "h_low", "slots_refilled") as (
                        block, slab_in0, slab_in1, high_done, low_done, tile_done, banks_free, tapped0, tapped1, active,
                        products, h_high, h_low, slots_refilled):
                slab_in = [slab_in0, slab_in1]
                tapped = [tapped0, tapped1]
                steps = FT // 2

                def slab_at(i, u):
                    return (2 * i + u % 2) * P + (gate_at, value_at)[u // 2]

                @block.sync
                def _(sp):
                    for u in range(2):
                        sp.dma_start(ring[:, u], w[:, :, bass.ds(slab_at(0, u), P)]).then_inc(slab_in[u], 16)
                    for u in range(2, 4):
                        sp.wait_ge(low_done, u - 1)
                        sp.dma_start(ring[:, u % 2], w[:, :, bass.ds(slab_at(0, u), P)]).then_inc(slab_in[u % 2], 16)
                    with sp.Fori(1, steps) as i:
                        for u in range(4):
                            feature = sp.snap(slab_at(i, u))
                            sp.wait_ge(low_done, 4 * i + u - 1)
                            sp.sem_inc(slots_refilled, 1)
                            sp.dma_start(ring[:, u % 2], w[:, :, bass.ds(feature, P)]).then_inc(slab_in[u % 2], 16)

                @block.gpsimd
                def _(pool):
                    with pool.Fori(0, steps) as i:
                        for u in range(4):
                            pool.wait_ge(high_done, 4 * i + u + 1)
                            pool.tensor_tensor(low[:, u], ring[:, u % 2], high[:, u].bitcast(F32), ALU.subtract)\
                                .then_inc(low_done, 1)

                @block.tensor
                def _(pe):
                    with pe.Fori(0, steps) as i:
                        for u in range(4):
                            pe.wait_ge(low_done, 4 * i + u + 1)
                            pe.wait_ge(banks_free, 4 * i + u + 1)
                            for k in range(DT):
                                mm = three_passes(pe, core.banks[u][:, :], (high[:, u, k, :], low[:, u, k, :]),
                                                  (x[0][:, k, :], x[1][:, k, :]), k == 0, k == DT - 1)
                            mm.then_inc(tile_done, 1)

                @block.scalar
                def _(act):
                    def take_high(i, u):
                        act.wait_ge(slab_in[u % 2], 16 * (2 * i + u // 2 + 1))
                        act.activation(high[:, u], ring[:, u % 2], ACT.Copy).then_inc(high_done, 1)

                    def step(i, more):
                        for u in range(4):
                            act.wait_ge(tile_done, 4 * i + u + 1)
                            j = u % 2
                            if u < 2:
                                act.wait_ge(tapped[j], len(taps) * i + 1)
                                src, dst = core.banks[u][:, :], interior(pad[:, j, :])
                                if len(dst.shape) == 3:
                                    src = src.rearrange("p (a b) -> p a b", b=dst.shape[2])
                            else:
                                act.wait_ge(products, 2 * i + j + 1)
                                src, dst = core.banks[u][:, :], val[:, j, :]
                            act.activation(dst, src, ACT.Identity).then_inc(banks_free, 1)
                            if more:
                                take_high(i + 1, u)
                        for j in range(2):
                            act.wait_ge(tapped[j], len(taps) * (i + 1) + 1)
                            act.activation(acc[:, j, :], acc[:, j, :], func, bias=conv_b(2 * i + j)).then_inc(active, 1)
                        for j in range(2):
                            act.wait_ge(products, 2 + 2 * i + j + 1)
                            act.activation(h[0][:, bass.ds(2 * i + j, 1), :], acc[:, j:j + 1, :], ACT.Copy)\
                               .then_inc(h_high, 1)

                    act.sem_inc(banks_free, 4)
                    for u in range(4):
                        take_high(0, u)
                    with act.Fori(0, steps - 1) as i:
                        step(i, True)
                    step(steps - 1, False)

                @block.vector
                def _(dve):
                    for j in range(2):
                        dve.memset(pad[:, j, :], 0.0).then_inc(tapped[j], 1)
                    dve.sem_inc(products, 2)
                    dve.sem_inc(h_low, 2)
                    with dve.Fori(0, steps) as i:
                        for n, tap in enumerate(taps):
                            for j in range(2):
                                if n == 0:
                                    dve.wait_ge(banks_free, 4 + 4 * i + j + 1)
                                    dve.wait_ge(h_low, 2 * i + j + 1)
                                src = tap(pad[:, j, :])
                                dst = acc[:, j, :]
                                if len(src.shape) == 3:
                                    dst = dst.rearrange("p (a b) -> p a b", b=src.shape[2])
                                dve.wait_ge(tapped[j], len(taps) * i + n + 1)
                                if n == 0:
                                    dve.tensor_scalar(dst, src, conv_w(2 * i + j, n), None, ALU.mult)\
                                       .then_inc(tapped[j], 1)
                                else:
                                    dve.scalar_tensor_tensor(out=dst, in0=src, scalar=conv_w(2 * i + j, n), in1=dst,
                                                             op0=ALU.mult, op1=ALU.add).then_inc(tapped[j], 1)
                        for j in range(2):
                            dve.wait_ge(active, 2 * i + j + 1)
                            dve.wait_ge(banks_free, 4 + 4 * i + j + 3)
                            dve.tensor_tensor(acc[:, j, :], acc[:, j, :], val[:, j, :], ALU.mult).then_inc(products, 1)
                        for j in range(2):
                            dve.wait_ge(h_high, 2 * i + j + 1)
                            tile = bass.ds(2 * i + j, 1)
                            dve.tensor_tensor(h[1][:, tile, :], acc[:, j:j + 1, :], h[0][:, tile, :].bitcast(F32),
                                              ALU.subtract).then_inc(h_low, 1)

        with y_of() as (y,):
            gemm(core, f"{name}_down", w_down, h, [(0, SEQ)], lambda tile, n: y[:, bass.ds(tile, 1), :], DT, 2)
            yield y


GRID_PAD = (ROWS + 2) * (GRID_W + 2)


def grid_window(r, c):
    return lambda b: b.rearrange("p (a b) -> p a b", b=GRID_W + 2)[:, r:r + ROWS, c:c + GRID_W]


GRID_TAPS = [grid_window(r, c) for r in range(3) for c in range(3)]


def conformer(core, w1, w2, x, y):
    half = CONF_K // 2
    pe_taps = 13
    dve_taps = CONF_K - pe_taps
    with core.room(conf_pad=[P, DT, SEQ + 2 * half], conf_u=[P, DT, SEQ]) as (pad, conv):
        with core.stage("border") as (block, border):
            @block.gpsimd
            def _(pool):
                for at in (0, half + SEQ):
                    pool.memset(pad[:, :, at:at + half], 0.0).then_inc(border, 1)
        with core.room(conf_gate=[P, DT, SEQ]) as (gate,):
            gemm(core, "conf_gate", w1[:, D:], x, [(0, SEQ)], lambda tile, n: gate[:, bass.ds(tile, 1), :], DT, 4,
                 bias=lambda tile: core.col("conf_b1", tile, 1), func=ACT.Sigmoid)
            gemm(core, "conf_val", w1[:, 0:D], x, [(0, SEQ)], lambda tile, n: pad[:, bass.ds(tile, 1), half:half + SEQ],
                 DT, 4, bias=lambda tile: core.col("conf_b1", tile))
            with core.stage("gated") as (block, gated):
                @block.vector
                def _(dve):
                    for k in range(DT):
                        dve.tensor_tensor(pad[:, k, half:half + SEQ], pad[:, k, half:half + SEQ], gate[:, k, :], ALU.mult)\
                           .then_inc(gated, 1)
        with core.room(conf_diag=[P, 2, pe_taps, P]) as (diag,), \
                core.stage("tapped0", "tapped1", "diag_done", "pe_tapped", "tile_added") as (
                    block, tapped0, tapped1, diag_done, pe_tapped, tile_added):
            tapped = [tapped0, tapped1]

            @block.vector
            def _(dve):
                dve.sem_inc(tile_added, 2)
                with dve.Fori(0, DT // 2) as i:
                    for n in range(dve_taps):
                        for j in range(2):
                            tile = bass.ds(2 * i + j, 1)
                            src, dst = pad[:, tile, n:n + SEQ], conv[:, tile, :]
                            if n == 0:
                                dve.tensor_scalar(dst, src, core.col("conf_dw_w", 2 * i + j, n),
                                                  core.col("conf_dw_b", 2 * i + j), ALU.mult, ALU.add)\
                                   .then_inc(tapped[j], 1)
                            else:
                                dve.wait_ge(tapped[j], dve_taps * i + n)
                                dve.scalar_tensor_tensor(out=dst, in0=src, scalar=core.col("conf_dw_w", 2 * i + j, n),
                                                         in1=dst, op0=ALU.mult, op1=ALU.add).then_inc(tapped[j], 1)
                    for j in range(2):
                        tile = bass.ds(2 * i + j, 1)
                        dve.wait_ge(tapped[j], dve_taps * (i + 1))
                        dve.wait_ge(pe_tapped, 2 * i + j + 1)
                        dve.tensor_tensor(conv[:, tile, :], conv[:, tile, :], core.banks[j][:, :].unsqueeze(1), ALU.add)\
                           .then_inc(tile_added, 1)

            @block.scalar
            def _(act):
                with act.Fori(0, DT // 2) as i:
                    for j in range(2):
                        act.wait_ge(tile_added, 2 * i + j + 1)
                        for n in range(pe_taps):
                            done = act.activation(diag[:, j, n, :], core.const("ident"), ACT.Copy,
                                                  scale=core.col("conf_dw_w", 2 * i + j, dve_taps + n))
                        done.then_inc(diag_done, 1)

            @block.tensor
            def _(pe):
                with pe.Fori(0, DT // 2) as i:
                    for j in range(2):
                        pe.wait_ge(diag_done, 2 * i + j + 1)
                        for n in range(pe_taps):
                            at = dve_taps + n
                            mm = pe.matmul(core.banks[j][:, :], diag[:, j, n, :],
                                           pad[:, bass.ds(2 * i + j, 1), at:at + SEQ].rearrange("p a t -> p (a t)"),
                                           start=(n == 0), stop=(n == pe_taps - 1))
                        mm.then_inc(pe_tapped, 1)
        norm(core, "conf_ln", conv, conv, lambda k: core.col("conf_ln_g", k), lambda k: core.col("conf_ln_b", k),
             func=ACT.Silu)
        with core.split_room(conf_in=[P, DT, SEQ]) as (parts,):
            split(core, [(conv, parts)])
            gemm(core, "conf_out", w2, parts, [(0, SEQ)], lambda tile, n: y[:, bass.ds(tile, 1), :], DT, 4,
                 bias=lambda tile: core.col("conf_b2", tile))


def spread(ap, axis, count):
    ap = ap.unsqueeze(axis)
    shape = list(ap.shape)
    shape[axis] = count
    return ap.broadcast_to(shape)


LAT_PAD = SEQ + SSD_K - 1
CTX_PAD = CTX + SSD_K - 1
SPANS = [(0, SEQ), (SEQ, CTX)]
XS_T, B_T, C_T = 0, SSD_IN // P, SSD_IN // P + SSD_G
XBC_T = SSD_XBC // P


def ssd_inputs(core, w_in, h, xbc):
    half = SSD_K // 2
    with core.room(xbc_pad=[P, XBC_T, LAT_PAD + CTX_PAD]) as (pad,):
        def inner(tile, n):
            at, size = ((half, SEQ), (LAT_PAD + half, CTX))[n]
            return pad[:, bass.ds(tile, 1), at:at + size]

        with core.stage("border") as (block, border):
            @block.gpsimd
            def _(pool):
                for at, size in ((0, half), (LAT_PAD - half, 2 * half), (LAT_PAD + CTX_PAD - half, half)):
                    pool.memset(pad[:, :, at:at + size], 0.0).then_inc(border, 1)
        gemm(core, "xbc", w_in[:, MIX_AT["xbc"]:MIX_AT["dt"]], h, SPANS, inner, XBC_T, 4)
        with core.stage("lat_tapped", "ctx_tapped") as (block, lat_tapped, ctx_tapped):
            @block.vector
            def _(dve):
                with dve.Fori(0, XBC_T) as i:
                    for n in range(SSD_K):
                        for tapped, at, start, size in ((lat_tapped, 0, 0, SEQ), (ctx_tapped, LAT_PAD, SEQ, CTX)):
                            src = pad[:, bass.ds(i, 1), at + n:at + n + size]
                            dst = xbc[:, bass.ds(i, 1), start:start + size]
                            tap = core.col("ssd_conv_w", i, n)
                            if n == 0:
                                dve.tensor_scalar(dst, src, tap, None, ALU.mult).then_inc(tapped, 1)
                            else:
                                dve.wait_ge(tapped, SSD_K * i + n)
                                dve.scalar_tensor_tensor(out=dst, in0=src, scalar=tap, in1=dst, op0=ALU.mult,
                                                         op1=ALU.add).then_inc(tapped, 1)

            @block.scalar
            def _(act):
                with act.Fori(0, XBC_T) as i:
                    act.wait_ge(lat_tapped, SSD_K * (i + 1))
                    act.wait_ge(ctx_tapped, SSD_K * (i + 1))
                    act.activation(xbc[:, bass.ds(i, 1), :], xbc[:, bass.ds(i, 1), :], ACT.Silu,
                                   bias=core.col("ssd_conv_b", i))


def ssd_tokens(core, xbc, x_tok, b_tok):
    with core.stage("turned", "taken") as (block, turned, taken):
        jobs = [(t, j, x_tok[:, t, j * P:(j + 4) * P], range(j, j + 4)) for t in range(TOK // P) for j in (0, 4)]
        jobs += [(t, B_T, b_tok[:, t, :], range(B_T, B_T + 2)) for t in range(TOK // P)]

        @block.tensor
        def _(pe):
            for n, (t, _, _, tiles) in enumerate(jobs):
                if n >= 8:
                    pe.wait_ge(taken, n - 7)
                for m, j in enumerate(tiles):
                    mm = pe.transpose(core.banks[n % 8][:, m * P:(m + 1) * P], xbc[:, j, t * P:(t + 1) * P],
                                      core.const("ident"))
                mm.then_inc(turned, 1)

        @block.scalar
        def _(act):
            for n, (_, _, out, tiles) in enumerate(jobs):
                act.wait_ge(turned, n + 1)
                act.activation(out, core.banks[n % 8][:, 0:len(tiles) * P], ACT.Copy).then_inc(taken, 1)


def step_sizes(core, dt, a, rows):
    tiles = TOK // P
    with core.room(dt_soft=[P, tiles, 32], a_exp=[P, 32]) as (soft, a_exp), \
            core.stage("biased", "folded", "exp_done", "soft_done", "dt_done", "a_exp_done") as (
                block, biased, folded, exp_done, soft_done, dt_done, a_exp_done):
        @block.vector
        def _(dve):
            dve.tensor_tensor(dt[:], dt[:], spread(rows[:, 0:32], 1, tiles), ALU.add).then_inc(biased, 1)
            dve.wait_ge(biased, 1)
            dve.scalar_tensor_tensor(out=soft[:], in0=dt[:], scalar=-1.0, in1=dt[:], op0=ALU.mult, op1=ALU.min)\
               .then_inc(folded, 1)
            dve.wait_ge(soft_done, 1)
            dve.scalar_tensor_tensor(out=dt[:], in0=dt[:], scalar=0.0, in1=soft[:], op0=ALU.max, op1=ALU.add)\
               .then_inc(dt_done, 1)
            dve.wait_ge(dt_done, 1)
            dve.wait_ge(a_exp_done, 1)
            dve.scalar_tensor_tensor(out=a[:], in0=dt[:], scalar=-1.0, in1=spread(a_exp[:, :], 1, tiles),
                                     op0=ALU.mult, op1=ALU.mult)

        @block.scalar
        def _(act):
            act.activation(a_exp[:, :], rows[:, 32:64], ACT.Exp).then_inc(a_exp_done, 1)
            act.wait_ge(folded, 1)
            act.activation(soft[:], soft[:], ACT.Exp).then_inc(exp_done, 1)
            act.wait_ge(exp_done, 1)
            act.activation(soft[:], soft[:], ACT.Ln, bias=1.0).then_inc(soft_done, 1)


def ssd_chunk(core, d, token, tile, output, xbc, x_tok, b_tok, dt, a, state, y, buf):
    b_st, c_st, bt_st, a_st, xdt, xdtd, acum, left, decay, cb, diff, m_buf, ce_buf = buf
    banks = core.banks
    until, neg = (core.const("until"), core.const("neg_until")) if d == 0 else (core.const("since"), core.const("neg_since"))
    heads = slice(d * SSD_HEADS, (d + 1) * SSD_HEADS)
    here = bass.ds(token, CHUNK)
    quads = SSD_HEADS // 4
    names = ["b_staged", "a_staged", "x_scaled", "cols_done", "acum_done", "left_done", "decay_done", "x_decayed", "cb_done",
             "cb_taken", "acum_rows", "diff_done", "m_exp", "ce_exp", "m_done", "ce_done", "y_done", "y_added",
             "states_made", "state_faded"]
    with core.stage(*names) as (block, b_staged, a_staged, x_scaled, cols_done, acum_done, left_done, decay_done, x_decayed,
                                cb_done, cb_taken, acum_rows, diff_done, m_exp, ce_exp, m_done, ce_done, y_done, y_added,
                                states_made, state_faded):
        @block.gpsimd
        def _(pool):
            x3 = x_tok[:, bass.ds(tile, 1), :].rearrange("p a (h x) -> p (a h) x", x=SSD_P)
            dt_here = dt[:, bass.ds(tile, 1), heads].rearrange("p a h -> p (a h)")
            pool.tensor_tensor(xdt[:], x3, spread(dt_here, 2, SSD_P), ALU.mult).then_inc(x_scaled, 1)
            pool.wait_ge(x_scaled, 1)
            pool.wait_ge(decay_done, 1)
            pool.tensor_tensor(xdtd[:], xdt[:], spread(decay[:, 0:16], 2, SSD_P), ALU.mult).then_inc(x_decayed, 1)
            if output:
                for q in range(quads):
                    pool.wait_ge(ce_exp, q + 1)
                    if q == 0:
                        pool.wait_ge(b_staged, 3)
                    pool.tensor_tensor(ce_buf[:, q % 2], ce_buf[:, q % 2], spread(c_st[:, q // 2, :], 1, 4), ALU.mult)\
                        .then_inc(ce_done, 1)

        @block.tensor
        def _(pe):
            pe.wait_ge(a_staged, 1)
            pe.matmul(banks[0][:, 0:16], until, a_st[:, :], start=True, stop=True)
            pe.matmul(banks[0][:, 16:32], core.const("ones"), a_st[:, :], start=True, stop=True).then_inc(cols_done, 1)
            if output:
                pe.wait_ge(b_staged, 3)
                for g in range(SSD_G):
                    mm = pe.matmul(banks[1][:, g * P:(g + 1) * P], b_st[:, g, :], c_st[:, g, :], start=True, stop=True)
                mm.then_inc(cb_done, 1)

                def rows(q):
                    if q >= 2:
                        pe.wait_ge(diff_done, 4 * (q - 1))
                        pe.wait_ge(ce_exp, q - 1)
                    for n in range(4):
                        h = 4 * q + n
                        mm = pe.matmul(banks[2 + q % 2][:, n * P:(n + 1) * P], a_st[:, h:h + 1].broadcast_to([P, P]),
                                       until, start=True, stop=True)
                    mm.then_inc(acum_rows, 1)

                rows(0)
                rows(1)
                for q in range(quads):
                    if q == 0:
                        pe.wait_ge(x_scaled, 1)
                    pe.wait_ge(m_done, q + 1)
                    pe.wait_ge(ce_done, q + 1)
                    if q >= 2:
                        pe.wait_ge(y_added, q - 1)
                    for n in range(4):
                        h = 4 * q + n
                        out = banks[4 + q % 2][64 * (n % 2):64 * (n % 2) + 64, (n // 2) * P:(n // 2 + 1) * P]
                        pe.matmul(out, xdt[:, h, :], m_buf[:, q % 2, n, :], start=True, stop=False)
                        mm = pe.matmul(out, state[:, h, :], ce_buf[:, q % 2, n, :], start=False, stop=True)
                    mm.then_inc(y_done, 1)
                    if q + 2 < quads:
                        rows(q + 2)
            pe.wait_ge(x_decayed, 1)
            pe.wait_ge(b_staged, 3)
            for g in range(SSD_G):
                mm = pe.matmul(banks[6 + g][:, :], bt_st[:, g * P:(g + 1) * P],
                               xdtd[:, 8 * g:8 * g + 8, :].rearrange("p h x -> p (h x)"), start=True, stop=True)
            mm.then_inc(states_made, 1)

        @block.scalar
        def _(act):
            act.activation(b_st[:], xbc[:, B_T:B_T + 2, here], ACT.Identity).then_inc(b_staged, 1)
            act.activation(c_st[:], xbc[:, C_T:C_T + 2, here], ACT.Identity).then_inc(b_staged, 1)
            act.activation(bt_st[:].rearrange("p (a n) -> p a n", a=1), b_tok[:, bass.ds(tile, 1), :], ACT.Identity)\
               .then_inc(b_staged, 1)
            act.wait_ge(left_done, 1)
            act.activation(decay[:, :], left[:, :], ACT.Exp).then_inc(decay_done, 1)
            if output:
                for q in range(quads):
                    act.wait_ge(diff_done, 4 * (q + 1))
                    if q >= 2:
                        act.wait_ge(y_done, q - 1)
                    act.activation(m_buf[:, q % 2], diff[:, q % 2], ACT.Exp).then_inc(m_exp, 1)
                    act.activation(ce_buf[:, q % 2].rearrange("p n t -> p (n t)"), banks[2 + q % 2][:, :], ACT.Exp)\
                       .then_inc(ce_exp, 1)

        @block.vector
        def _(dve):
            dve.tensor_copy(a_st[:, :].unsqueeze(1), a[:, bass.ds(tile, 1), heads]).then_inc(a_staged, 1)
            dve.wait_ge(cols_done, 1)
            dve.tensor_copy(acum[:, :], banks[0][:, 0:16]).then_inc(acum_done, 1)
            dve.tensor_copy(left[:, 16:32], banks[0][:, 16:32]).then_inc(acum_done, 1)
            dve.wait_ge(acum_done, 2)
            dve.tensor_tensor(left[:, 0:16], left[:, 16:32], acum[:, :], ALU.subtract).then_inc(left_done, 1)
            if output:
                dve.wait_ge(cb_done, 1)
                dve.tensor_copy(cb[:].rearrange("p g t -> p (g t)"), banks[1][:, 0:2 * P]).then_inc(cb_taken, 1)

                def add_y(q):
                    dve.wait_ge(y_done, q + 1)
                    out = y[:, 2 * q:2 * q + 2, here]
                    dve.tensor_tensor(out, out, banks[4 + q % 2][:, 0:2 * P].rearrange("p (j t) -> p j t", j=2), ALU.add)\
                       .then_inc(y_added, 1)

                def differences(q):
                    dve.wait_ge(acum_rows, q + 1)
                    if q >= 2:
                        dve.wait_ge(m_exp, q - 1)
                    for n in range(4):
                        h = 4 * q + n
                        dve.scalar_tensor_tensor(out=diff[:, q % 2, n, :], in0=banks[2 + q % 2][:, n * P:(n + 1) * P],
                                                 scalar=acum[:, h:h + 1], in1=neg, op0=ALU.subtract, op1=ALU.add)\
                           .then_inc(diff_done, 1)

                differences(0)
                for q in range(quads):
                    if q + 1 < quads:
                        differences(q + 1)
                    dve.wait_ge(m_exp, q + 1)
                    if q == 0:
                        dve.wait_ge(cb_taken, 1)
                    dve.tensor_tensor(m_buf[:, q % 2], m_buf[:, q % 2], spread(cb[:, q // 2, :], 1, 4), ALU.mult)\
                       .then_inc(m_done, 1)
                    if q >= 1:
                        add_y(q - 1)
                add_y(quads - 1)
            dve.wait_ge(decay_done, 1)
            dve.wait_ge(states_made, 1)
            dve.tensor_tensor(state[:], state[:], spread(decay[:, 16:32], 2, SSD_P), ALU.mult).then_inc(state_faded, 1)
            dve.wait_ge(state_faded, 1)
            for g in range(SSD_G):
                dve.tensor_tensor(state[:, 8 * g:8 * g + 8, :].rearrange("p h x -> p (h x)"),
                                  state[:, 8 * g:8 * g + 8, :].rearrange("p h x -> p (h x)"), banks[6 + g][:, :], ALU.add)


def chunks_of(core, d, body):
    for first, count, output in ((SEQ // CHUNK, CTX // CHUNK, False), (0, SEQ // CHUNK, True)):
        with core.nc.Fori(0, count) as i:
            tile = i + first if d == 0 else i * -1 + (first + count - 1)
            body(tile * CHUNK, tile, output)


def ssd(core, w_in, h, y, rows):
    tiles = TOK // P
    with core.room(xbc=[P, XBC_T, TOK]) as (xbc,):
        ssd_inputs(core, w_in, h, xbc)
        with core.room(x_tok=[P, tiles, SSD_IN], b_tok=[P, tiles, SSD_G * SSD_N], dt=[P, tiles, 32], a=[P, tiles, 32],
                       state=[P, SSD_HEADS, SSD_P], b_st=[P, SSD_G, P], c_st=[P, SSD_G, P], bt_st=[P, SSD_G * P],
                       a_st=[P, 16], xdt=[P, SSD_HEADS, SSD_P], xdtd=[P, SSD_HEADS, SSD_P], acum=[P, 16], left=[P, 32],
                       decay=[P, 32], cb=[P, SSD_G, P], diff=[P, 2, 4, P], m_buf=[P, 2, 4, P], ce_buf=[P, 2, 4, P]) as (
                x_tok, b_tok, dt, a, state, *buf):
            ssd_tokens(core, xbc, x_tok, b_tok)
            gemm_tokens(core, "dt", w_in[:, MIX_AT["dt"]:MIX_AT["q"]], h, tiles, lambda t, s: dt[:, t, :], 32)
            step_sizes(core, dt, a, rows)
            with core.stage("skipped") as (block, skipped):
                @block.vector
                def _(dve):
                    for j in range(DT):
                        dve.tensor_scalar(y[:, j, :], xbc[:, j, 0:SEQ], rows[:, 64 + j:65 + j], None, ALU.mult)
            for d in range(2):
                with core.stage("cleared") as (block, cleared):
                    @block.vector
                    def _(dve):
                        dve.memset(state[:], 0.0)
                chunks_of(core, d, lambda token, tile, output: ssd_chunk(
                    core, d, token, tile, output, xbc, x_tok, b_tok, dt, a, state, y, buf))


def gla_chunk(core, d, token, tile, output, q, f, v, state, o, buf):
    key, acum, q_st, v_st, q_in, k_out, att, mix0, mix1, fade = buf
    t1, lf, kt = mix0, mix1, mix0
    mix = [mix0, mix1]
    banks = core.banks
    flat = lambda b: b[:].rearrange("p h t -> p (h t)")
    end = CHUNK - 1 if d == 0 else 0
    here = bass.ds(token, CHUNK)
    fh = f[:, :, here]
    names = ["folded", "exp_done", "ln_done", "lf_done", "key_arg", "key_done", "summed", "q_staged", "v_staged", "q_exp",
             "q_in_done", "left_done", "left_exp", "k_out_done", "fade_done"]
    with core.stage(*names) as (block, folded, exp_done, ln_done, lf_done, key_arg, key_done, summed, q_staged, v_staged,
                                q_exp, q_in_done, left_done, left_exp, k_out_done, fade_done):
        @block.vector
        def _(dve):
            dve.scalar_tensor_tensor(out=t1[:], in0=fh, scalar=-1.0, in1=fh, op0=ALU.mult, op1=ALU.min).then_inc(folded, 1)
            dve.wait_ge(ln_done, 1)
            dve.scalar_tensor_tensor(out=lf[:], in0=fh, scalar=0.0, in1=t1[:], op0=ALU.min, op1=ALU.subtract)\
               .then_inc(lf_done, 1)
            dve.wait_ge(lf_done, 1)
            dve.tensor_tensor(key[:], lf[:], fh, ALU.subtract).then_inc(key_arg, 1)
            step = 1 if d == 0 else -1
            for h in range(HG_HEADS):
                dve.tensor_tensor_scan(acum[:, h, ::step], core.const("ones"), lf[:, h, ::step], 0.0, ALU.mult, ALU.add)\
                   .then_inc(summed, 1)
            dve.wait_ge(summed, HG_HEADS)
            dve.tensor_tensor(k_out[:], spread(acum[:, :, end], 2, CHUNK), acum[:], ALU.subtract).then_inc(left_done, 1)
            dve.wait_ge(left_exp, 1)
            dve.wait_ge(key_done, 1)
            dve.tensor_tensor(k_out[:], k_out[:], key[:], ALU.mult).then_inc(k_out_done, 1)
            if output:
                dve.wait_ge(q_exp, 1)
                dve.wait_ge(q_staged, 1)
                dve.tensor_tensor(q_in[:], q_in[:], q_st[:], ALU.mult).then_inc(q_in_done, 1)

        @block.scalar
        def _(act):
            act.wait_ge(folded, 1)
            act.activation(t1[:], t1[:], ACT.Exp).then_inc(exp_done, 1)
            act.wait_ge(exp_done, 1)
            act.activation(t1[:], t1[:], ACT.Ln, bias=1.0).then_inc(ln_done, 1)
            act.wait_ge(key_arg, 1)
            act.activation(key[:], key[:], ACT.Exp).then_inc(key_done, 1)
            act.wait_ge(summed, HG_HEADS)
            act.activation(fade[:, :], acum[:, :, end], ACT.Exp).then_inc(fade_done, 1)
            act.wait_ge(left_done, 1)
            act.activation(k_out[:], k_out[:], ACT.Exp).then_inc(left_exp, 1)
            if output:
                act.activation(q_in[:], acum[:], ACT.Exp).then_inc(q_exp, 1)

        @block.gpsimd
        def _(pool):
            if output:
                pool.tensor_copy(q_st[:], q[:, :, here]).then_inc(q_staged, 1)
            pool.tensor_copy(flat(v_st).unsqueeze(1), v[:, bass.ds(tile, 1), :]).then_inc(v_staged, 1)

    def half(b, m, side):
        return flat(b).rearrange("p (b t) -> p b t", t=2 * m)[:, :, side * m:(side + 1) * m]

    if output:
        names = ["diff_done", "exp_done", "mixed", "products", "merged", "diagonal", "att_done", "o_done", "o_added"]
        with core.stage(*names) as (block, diff_done, exp_done, mixed, products, merged, diagonal, att_done, o_done, o_added):
            levels = list(enumerate(LEVELS))

            @block.gpsimd
            def _(pool):
                for n, m in levels:
                    if n >= 2:
                        pool.wait_ge(products, n - 1)
                    left, right = half(acum, m, 0), half(acum, m, 1)
                    middle = left[:, :, m - 1] if d == 0 else right[:, :, 0]
                    middle = spread(middle, 2, m)
                    a, b = (left, right) if d == 0 else (right, left)
                    out_a, out_b = half(mix[n % 2], m, d), half(mix[n % 2], m, 1 - d)
                    pool.tensor_tensor(out_a, middle, a, ALU.subtract).then_inc(diff_done, 1)
                    pool.tensor_tensor(out_b, b, middle, ALU.subtract).then_inc(diff_done, 1)

            @block.scalar
            def _(act):
                for n, m in levels:
                    act.wait_ge(diff_done, 2 * n + 2)
                    act.activation(mix[n % 2][:], mix[n % 2][:], ACT.Exp).then_inc(exp_done, 1)

            @block.tensor
            def _(pe):
                for h in range(HG_HEADS):
                    mm = pe.matmul(banks[4 + h // 4][:, (h % 4) * P:(h % 4 + 1) * P], key[:, h, :], q_st[:, h, :],
                                   start=True, stop=True)
                mm.then_inc(diagonal, 1)
                for n, m in levels:
                    pe.wait_ge(mixed, 2 * n + 2)
                    if n >= 2:
                        pe.wait_ge(merged, 2 * (n - 1))
                    for h in range(HG_HEADS):
                        mm = pe.matmul(banks[2 * (n % 2) + h // 4][:, (h % 4) * P:(h % 4 + 1) * P], mix[n % 2][:, h, :],
                                       mix[n % 2][:, h, :], start=True, stop=True)
                    mm.then_inc(products, 1)
                pe.wait_ge(merged, 2 * len(levels))
                for h in range(HG_HEADS):
                    out = banks[6 + h // 4][:, (h % 4) * P:(h % 4 + 1) * P]
                    pe.matmul(out, v_st[:, h, :], att[:, h, :], start=True, stop=False)
                    mm = pe.matmul(out, state[:, h, :], q_in[:, h, :], start=False, stop=True)
                mm.then_inc(o_done, 1)

            @block.vector
            def _(dve):
                def mix_level(n, m):
                    dve.wait_ge(exp_done, n + 1)
                    for side in range(2):
                        src = key if side == d else q_st
                        dve.tensor_tensor(half(mix[n % 2], m, side), half(mix[n % 2], m, side), half(src, m, side), ALU.mult)\
                           .then_inc(mixed, 1)

                mix_level(*levels[0])
                dve.wait_ge(diagonal, 1)
                for b in range(2):
                    four = slice(4 * b, 4 * b + 4)
                    dve.tensor_tensor(att[:, four, :], banks[4 + b][:, :].rearrange("p (h t) -> p h t", h=4),
                                      spread(core.const("ident"), 1, 4), ALU.mult).then_inc(att_done, 1)
                for n, m in levels:
                    if n + 1 < len(levels):
                        mix_level(*levels[n + 1])
                    side = "left_right" if d == 0 else "right_left"
                    mask = core.const(f"{side}_{m}").bitcast(U32)
                    dve.wait_ge(products, n + 1)
                    for b in range(2):
                        four = slice(4 * b, 4 * b + 4)
                        if n == 0:
                            dve.wait_ge(att_done, 2)
                        else:
                            dve.wait_ge(merged, 2 * n)
                        dve.copy_predicated(att[:, four, :], spread(mask, 1, 4),
                                            banks[2 * (n % 2) + b][:, :].rearrange("p (h t) -> p h t", h=4))\
                           .then_inc(merged, 1)
                dve.wait_ge(o_done, 1)
                for b in range(2):
                    out = o[:, 4 * b:4 * b + 4, here]
                    dve.tensor_tensor(out, out, banks[6 + b][:, :].rearrange("p (h t) -> p h t", h=4), ALU.add)\
                       .then_inc(o_added, 1)

    with core.stage("turned", "taken", "states_made", "faded") as (block, turned, taken, states_made, faded):
        @block.tensor
        def _(pe):
            for h in range(HG_HEADS):
                mm = pe.transpose(banks[h // 4][:, (h % 4) * P:(h % 4 + 1) * P], k_out[:, h, :], core.const("ident"))
                if h % 4 == 3:
                    mm.then_inc(turned, 1)
            for h in range(HG_HEADS):
                pe.wait_ge(taken, h // 4 + 1)
                mm = pe.matmul(banks[2 + h // 4][:, (h % 4) * P:(h % 4 + 1) * P], kt[:, h, :], v_st[:, h, :],
                               start=True, stop=True)
                if h % 4 == 3:
                    mm.then_inc(states_made, 1)

        @block.scalar
        def _(act):
            for b in range(2):
                act.wait_ge(turned, b + 1)
                act.activation(kt[:, 4 * b:4 * b + 4, :].rearrange("p h t -> p (h t)"), banks[b][:, :], ACT.Copy)\
                   .then_inc(taken, 1)

        @block.vector
        def _(dve):
            for h in range(HG_HEADS):
                dve.wait_ge(states_made, h // 4 + 1)
                dve.scalar_tensor_tensor(out=state[:, h, :], in0=state[:, h, :], scalar=fade[:, h:h + 1],
                                         in1=banks[2 + h // 4][:, (h % 4) * P:(h % 4 + 1) * P], op0=ALU.mult, op1=ALU.add)


def gla(core, w_in, h, o):
    tiles = TOK // P
    wide = [P, HG_HEADS, CHUNK]
    with core.room(v=[P, tiles, D], q=[P, HG_HEADS, SEQ]) as (v, q):
        gemm_tokens(core, "v", w_in[:, MIX_AT["v"]:MIX_AT["g"]], h, tiles,
                    lambda t, s: v[:, t, s * 256:(s + 1) * 256], 256)
        gemm(core, "q", w_in[:, MIX_AT["q"]:MIX_AT["f"]], h, [(0, SEQ)], lambda tile, n: q[:, bass.ds(tile, 1), :], DT, 4,
             func=ACT.Silu)
        with core.room(f=[P, HG_HEADS, TOK], hg_state=[P, HG_HEADS, P]) as (f, state):
            with core.stage("cleared") as (block, cleared):
                @block.gpsimd
                def _(pool):
                    pool.memset(o[:], 0.0).then_inc(cleared, 1)
            for d in range(2):
                at = MIX_AT["f"] + d * D
                gemm(core, f"f{d}", w_in[:, at:at + D], h, SPANS,
                     lambda tile, n: f[:, bass.ds(tile, 1), SPANS[n][0]:SPANS[n][0] + SPANS[n][1]], HG_HEADS, 4)
                with core.stage("cleared") as (block, cleared):
                    @block.vector
                    def _(dve):
                        dve.memset(state[:], 0.0)
                names = ["key", "acum", "q_st", "v_st", "q_in", "k_out", "att", "mix0", "mix1"]
                with core.room(**{f"{n}_{d}": wide for n in names}, **{f"fade_{d}": [P, HG_HEADS]}) as buf:
                    chunks_of(core, d, lambda token, tile, output: gla_chunk(
                        core, d, token, tile, output, q, f, v, state, o, buf))


def group_norm_gate(core, name, y, w_gate, x, groups, gain, gate_first):
    size = DT // groups
    width = size * P
    with core.room(**{f"{name}_gate": [P, DT, SEQ], f"{name}_sq": [P, DT, SEQ], f"{name}_rstd": [P, 2, SEQ]}) as (
            gate, sq, rstd):
        gemm(core, f"{name}_g", w_gate, x, [(0, SEQ)], lambda tile, n: gate[:, bass.ds(tile, 1), :], DT, 4, func=ACT.Silu)
        with core.stage("gated", "squared", "sq_summed", "var_done", "root_done", "inverse_done", "scaled") as (
                block, gated, squared, sq_summed, var_done, root_done, inverse_done, scaled):
            @block.vector
            def _(dve):
                if gate_first:
                    for k in range(DT):
                        dve.tensor_tensor(y[:, k, :], y[:, k, :], gate[:, k, :], ALU.mult).then_inc(gated, 1)
                for g in range(groups):
                    dve.wait_ge(sq_summed, g + 1)
                    if g >= 2:
                        dve.wait_ge(scaled, (g - 1) * size)
                    dve.tensor_scalar(rstd[:, g % 2, :], core.banks[g % 8][:, :], 1.0 / width, EPS, ALU.mult, ALU.add)\
                       .then_inc(var_done, 1)
                    dve.wait_ge(root_done, g + 1)
                    dve.reciprocal(rstd[:, g % 2, :], rstd[:, g % 2, :]).then_inc(inverse_done, 1)
                    dve.wait_ge(inverse_done, g + 1)
                    for k in range(g * size, (g + 1) * size):
                        dve.scalar_tensor_tensor(out=y[:, k, :], in0=y[:, k, :], scalar=gain(k), in1=rstd[:, g % 2, :],
                                                 op0=ALU.mult, op1=ALU.mult).then_inc(scaled, 1)
                if not gate_first:
                    for k in range(DT):
                        dve.wait_ge(scaled, k + 1)
                        dve.tensor_tensor(y[:, k, :], y[:, k, :], gate[:, k, :], ALU.mult).then_inc(gated, 1)

            @block.scalar
            def _(act):
                for k in range(DT):
                    if gate_first:
                        act.wait_ge(gated, k + 1)
                    act.activation(sq[:, k, :], y[:, k, :], ACT.Square).then_inc(squared, 1)
                for g in range(groups):
                    act.wait_ge(var_done, g + 1)
                    act.activation(rstd[:, g % 2, :], rstd[:, g % 2, :], ACT.Sqrt).then_inc(root_done, 1)

            @block.tensor
            def _(pe):
                for g in range(groups):
                    for k in range(g * size, (g + 1) * size):
                        pe.wait_ge(squared, k + 1)
                        mm = pe.matmul(core.banks[g % 8][:, :], core.const("ones"), sq[:, k, :], start=(k % size == 0),
                                       stop=(k % size == size - 1))
                    mm.then_inc(sq_summed, 1)


def even_mixer(core, w_in, w_out, h, y, rows):
    ssd(core, w_in, h, y, rows)
    with core.room(o_hg=[P, DT, SEQ]) as (o,):
        gla(core, w_in, h, o)
        group_norm_gate(core, "ssd", y, w_in[:, MIX_AT["z"]:MIX_AT["xbc"]], h, SSD_G,
                        lambda k: core.col("ssd_norm_w", k), True)
        group_norm_gate(core, "hg", o, w_in[:, MIX_AT["g"]:], h, HG_HEADS, lambda k: core.col("hg_norm_w", k), False)
        y_parts = [part[:, :, 0:SEQ] for part in h]
        with core.split_room(o_parts=[P, DT, SEQ]) as (o_parts,):
            split(core, [(y, y_parts), (o, o_parts)])
            gemm(core, "mix_out", w_out, y_parts, [(0, SEQ)], lambda tile, n: y[:, bass.ds(tile, 1), :], DT, 2, more=o_parts)

HEAD_SCALE = HD ** -0.5
PAIRS = NSA_H // 2
UNITS = 2 * TT
NC = SEQ // RW_C
RU = 2 * NC


def causal_attention(core, name, q, k, v, out, gates):
    banks = core.banks
    with core.room(**{f"{name}_q": [P, SEQ], f"{name}_k": [P, SEQ], f"{name}_v": [P, TT, 2 * HD], f"{name}_p": [P, 2, SEQ],
                      f"{name}_pt": [P, 2, SEQ], f"{name}_top": [P, UNITS], f"{name}_bias": [P, UNITS],
                      f"{name}_sum": [P, UNITS]}) as (q_st, k_st, v_st, prob, prob_t, top, bias, total), \
            core.nc.Fori(0, PAIRS) as j, \
            core.stage("staged", "scored", "masked", "top_done", "bias_done", "exp_done", "turned", "taken", "summed",
                       "guarded", "inverted", "weighed", "added") as (
                block, staged, scored, masked, top_done, bias_done, exp_done, turned, taken, summed, guarded, inverted,
                weighed, added):
        @block.gpsimd
        def _(pool):
            pool.tensor_copy(q_st[:, :].unsqueeze(1), q[:, bass.ds(j, 1), :]).then_inc(staged, 1)
            pool.tensor_copy(k_st[:, :].unsqueeze(1), k[:, bass.ds(j, 1), :]).then_inc(staged, 1)
            pool.tensor_copy(v_st[:], v[:, :, bass.ds(j * (2 * HD), 2 * HD)]).then_inc(staged, 1)

        @block.tensor
        def _(pe):
            def scores(u):
                e, t = u // TT, u % TT
                if u >= 2:
                    pe.wait_ge(exp_done, u - 1)
                pe.matmul(banks[u % 2][:, 0:(t + 1) * P], q_st[HD * e:HD * e + HD, t * P:(t + 1) * P],
                          k_st[HD * e:HD * e + HD, 0:(t + 1) * P], start=True, stop=True).then_inc(scored, 1)

            def turn(u):
                t = u % TT
                pe.wait_ge(exp_done, u + 1)
                if u >= 2:
                    pe.wait_ge(taken, u - 1)
                for n in range(t + 1):
                    mm = pe.transpose(banks[2 + u % 2][:, n * P:(n + 1) * P], prob[:, u % 2, n * P:(n + 1) * P],
                                      core.const("ident"))
                mm.then_inc(turned, 1)

            def values(u):
                e, t = u // TT, u % TT
                pe.wait_ge(taken, u + 1)
                if u >= 2:
                    pe.wait_ge(added, u - 1)
                for n in range(t + 1):
                    mm = pe.matmul(banks[4 + u % 2][:, 0:HD], prob_t[:, u % 2, n * P:(n + 1) * P],
                                   v_st[:, n, HD * e:HD * e + HD], start=(n == 0), stop=(n == t))
                mm.then_inc(summed, 1)

            pe.wait_ge(staged, 3)
            scores(0)
            scores(1)
            for u in range(UNITS):
                turn(u)
                if u + 2 < UNITS:
                    scores(u + 2)
                values(u)

        @block.scalar
        def _(act):
            for u in range(UNITS):
                n = (u % TT + 1) * P
                act.wait_ge(bias_done, u + 1)
                if u >= 2:
                    act.wait_ge(turned, u - 1)
                act.activation(prob[:, u % 2, 0:n], banks[u % 2][:, 0:n], ACT.Exp, bias=bias[:, u:u + 1],
                               scale=HEAD_SCALE, accum_out=total[:, u:u + 1]).then_inc(exp_done, 1)
                act.wait_ge(turned, u + 1)
                if u >= 2:
                    act.wait_ge(summed, u - 1)
                act.activation(prob_t[:, u % 2, 0:n], banks[2 + u % 2][:, 0:n], ACT.Copy).then_inc(taken, 1)

        @block.vector
        def _(dve):
            def finish(u):
                e, t = u // TT, u % TT
                dve.wait_ge(exp_done, u + 1)
                dve.tensor_scalar(total[:, u:u + 1], total[:, u:u + 1], 1e-30, None, ALU.max).then_inc(guarded, 1)
                dve.wait_ge(guarded, u + 1)
                dve.reciprocal(total[:, u:u + 1], total[:, u:u + 1]).then_inc(inverted, 1)
                dve.wait_ge(inverted, u + 1)
                dst = out[:, t, bass.ds(j * (2 * HD) + HD * e, HD)]
                if gates is None:
                    dve.wait_ge(summed, u + 1)
                    dve.tensor_scalar(dst, banks[4 + u % 2][:, 0:HD], total[:, u:u + 1], None, ALU.mult)\
                       .then_inc(added, 1)
                else:
                    dve.tensor_tensor(total[:, u:u + 1], total[:, u:u + 1], gates(j, e, t), ALU.mult).then_inc(weighed, 1)
                    dve.wait_ge(weighed, u + 1)
                    dve.wait_ge(summed, u + 1)
                    dve.scalar_tensor_tensor(out=dst, in0=banks[4 + u % 2][:, 0:HD], scalar=total[:, u:u + 1],
                                             in1=dst, op0=ALU.mult, op1=ALU.add).then_inc(added, 1)

            for u in range(UNITS):
                t = u % TT
                dve.wait_ge(scored, u + 1)
                last = banks[u % 2][:, t * P:(t + 1) * P]
                dve.tensor_tensor(last, last, core.const("neg_since"), ALU.add).then_inc(masked, 1)
                dve.wait_ge(masked, u + 1)
                dve.tensor_reduce(top[:, u:u + 1], banks[u % 2][:, 0:(t + 1) * P], AX_X, ALU.max).then_inc(top_done, 1)
                dve.wait_ge(top_done, u + 1)
                dve.tensor_scalar(bias[:, u:u + 1], top[:, u:u + 1], -HEAD_SCALE, None, ALU.mult).then_inc(bias_done, 1)
                if u >= 1:
                    finish(u - 1)
            finish(UNITS - 1)


def compress(core, n, kv, pos, w1, w2, k_out, v_out):
    half = SEQ // 2
    step = CMP_STRIDE // 2
    pairs = CMP_LEN // 2
    g_n = KV_H * N_CMP
    with core.room(**{f"cmp_even_odd{n}": [P, 2, half], f"cmp_pairs{n}": [P, KV_H, half],
                      f"cmp_x{n}": [P, pairs, KV_H, N_CMP], f"cmp_w1{n}": [P, pairs, CMP_HID], f"cmp_w2{n}": [P, 2, HD],
                      f"cmp_pos{n}": [P, pairs], f"cmp_hid{n}": [P, 2, g_n]}) as (
            even_odd, both, x, w1_sb, w2_sb, pos_sb, hid), \
            core.stage("w_in", "split", "moved", "placed", "hid_done", "active", "out_done", "out_taken", "cleared") as (
                block, w_in, split, moved, placed, hid_done, active, out_done, out_taken, cleared):
        @block.sync
        def _(sp):
            sp.dma_start(w1_sb[:], w1.rearrange("(k p) m -> p k m", p=P)).then_inc(w_in, 16)
            sp.dma_start(w2_sb[:], w2.rearrange("(k p) m -> p k m", p=P)).then_inc(w_in, 16)
            sp.dma_start(pos_sb[:], pos).then_inc(w_in, 16)
            sp.wait_ge(split, 1)
            for g in range(KV_H):
                for parity in range(2):
                    sp.dma_start(both[HD * parity:HD * parity + HD, g, :], even_odd[HD * g:HD * g + HD, parity, :])\
                      .then_inc(moved, 16)
            sp.wait_ge(moved, 64)

        @block.vector
        def _(dve):
            dve.tensor_copy(even_odd[:], kv.rearrange("p (t a) -> p a t", a=2)).then_inc(split, 1)
            if v_out is not None:
                dve.memset(v_out[:], 0.0).then_inc(cleared, 1)
            else:
                dve.memset(k_out[:], 0.0).then_inc(cleared, 1)
            dve.wait_ge(w_in, 48)
            dve.wait_ge(moved, 64)
            for g in range(KV_H):
                for a in range(pairs // step):
                    src = both[:, g, step * a:step * (a + N_CMP)].rearrange("p (i b) -> p i b", b=step)
                    dst = x[:, step * a:step * (a + 1), g, :].rearrange("p b i -> p i b")
                    dve.tensor_tensor(dst, src, spread(pos_sb[:, step * a:step * (a + 1)], 1, N_CMP), ALU.add)\
                       .then_inc(placed, 1)
            dve.wait_ge(out_done, 1)
            dve.wait_ge(cleared, 1)
            if v_out is not None:
                dve.tensor_copy(v_out[0:N_CMP, :], core.banks[2][0:N_CMP, 0:KV_H * HD]).then_inc(out_taken, 1)
            else:
                for j in range(PAIRS):
                    for e in range(2):
                        g = (2 * j + e) // (NSA_H // KV_H)
                        rows = slice(HD * e, HD * e + HD)
                        dve.tensor_copy(k_out[rows, j, 0:N_CMP], core.banks[2][rows, g * N_CMP:(g + 1) * N_CMP])\
                           .then_inc(out_taken, 1)

        @block.tensor
        def _(pe):
            pe.wait_ge(w_in, 48)
            pe.wait_ge(placed, 2 * KV_H)
            for m in range(2):
                for i in range(pairs):
                    mm = pe.matmul(core.banks[m][:, 0:g_n], w1_sb[:, i, m * P:(m + 1) * P],
                                   x[:, i, :, :].rearrange("p g i -> p (g i)"), start=(i == 0), stop=(i == pairs - 1))
                mm.then_inc(hid_done, 1)
            pe.wait_ge(active, 2)
            for e in range(2):
                for m in range(2):
                    if v_out is not None:
                        mm = pe.matmul(core.banks[2][0:N_CMP, HD * e:HD * e + HD], hid[:, m, N_CMP * e:N_CMP * (e + 1)],
                                       w2_sb[:, m, :], start=(m == 0), stop=(m == 1))
                    else:
                        mm = pe.matmul(core.banks[2][HD * e:HD * e + HD, 0:g_n], w2_sb[:, m, :], hid[:, m, :],
                                       start=(m == 0), stop=(m == 1))
            mm.then_inc(out_done, 1)

        @block.scalar
        def _(act):
            for m in range(2):
                act.wait_ge(hid_done, m + 1)
                act.activation(hid[:, m, :], core.banks[m][:, 0:g_n], ACT.Gelu_apprx_tanh).then_inc(active, 1)


def compressed_attention(core, q, k, v, out, gates):
    n_u = NSA_H * TT
    keys = N_CMP + 1
    banks = core.banks
    per_bank = 4
    with core.room(cs=[P, NSA_H, TT, keys], cs_top=[P, n_u], cs_sum=[P, n_u], cs_t=[keys, n_u, P]) as (cs, top, total, cs_t), \
            core.stage("scored", "masked", "top_done", "shifted", "exp_done", "kept", "total_done", "guarded", "inverted",
                       "weighed", "prob_done", "turned", "taken", "summed", "written") as (
                block, scored, masked, top_done, shifted, exp_done, kept, total_done, guarded, inverted, weighed,
                prob_done, turned, taken, summed, written):
        flat = cs[:].rearrange("p h t k -> p (h t) k")

        @block.tensor
        def _(pe):
            for h in range(NSA_H):
                rows = slice(HD * (h % 2), HD * (h % 2) + HD)
                for t in range(TT):
                    mm = pe.matmul(banks[h % 2][:, ((h // 2) * TT + t) * keys:((h // 2) * TT + t + 1) * keys],
                                   q[rows, h // 2, t * P:(t + 1) * P], k[rows, h // 2, :], start=True, stop=True)
                mm.then_inc(scored, 1)
            pe.wait_ge(prob_done, 1)
            for u in range(n_u):
                mm = pe.transpose(banks[2 + u // 4][0:keys, (u % 4) * P:(u % 4 + 1) * P], flat[:, u, :], core.const("ident"))
                if u % 4 == 3:
                    mm.then_inc(turned, 1)
            for u in range(n_u):
                g = (u // TT) // (NSA_H // KV_H)
                if u % 4 == 0:
                    pe.wait_ge(taken, u // 4 + 1)
                bank = banks[(0, 1, 2)[u // 8]]
                if u == 16:
                    pe.wait_ge(taken, 6)
                mm = pe.matmul(bank[:, (u % 8) * HD:(u % 8 + 1) * HD], cs_t[:, u, :], v[:, g * HD:(g + 1) * HD],
                               start=True, stop=True)
                if u % 8 == 7:
                    mm.then_inc(summed, 1)

        @block.vector
        def _(dve):
            mask = core.const("cmp_mask").rearrange("p (t k) -> p t k", t=TT)
            valid = core.const("cmp_valid").rearrange("p (t k) -> p t k", t=TT)
            dve.wait_ge(scored, NSA_H)
            for h in range(NSA_H):
                src = banks[h % 2][:, (h // 2) * P:(h // 2 + 1) * P].rearrange("p (t k) -> p t k", t=TT)
                dve.tensor_tensor(cs[:, h], src, mask, ALU.add).then_inc(masked, 1)
            dve.wait_ge(masked, NSA_H)
            dve.tensor_reduce(top[:, :], flat, AX_X, ALU.max).then_inc(top_done, 1)
            dve.wait_ge(top_done, 1)
            dve.tensor_tensor(flat, flat, spread(top[:, :], 2, keys), ALU.subtract).then_inc(shifted, 1)
            dve.wait_ge(exp_done, 1)
            for h in range(NSA_H):
                dve.tensor_tensor(cs[:, h], cs[:, h], valid, ALU.mult).then_inc(kept, 1)
            dve.wait_ge(kept, NSA_H)
            dve.tensor_reduce(total[:, :], flat, AX_X, ALU.add).then_inc(total_done, 1)
            dve.wait_ge(total_done, 1)
            dve.tensor_scalar(total[:, :], total[:, :], 1e-30, None, ALU.max).then_inc(guarded, 1)
            dve.wait_ge(guarded, 1)
            dve.reciprocal(total[:, :], total[:, :]).then_inc(inverted, 1)
            dve.wait_ge(inverted, 1)
            dve.tensor_tensor(total[:].rearrange("p (h t) -> p h t", t=TT), total[:].rearrange("p (h t) -> p h t", t=TT),
                              gates, ALU.mult).then_inc(weighed, 1)
            dve.wait_ge(weighed, 1)
            dve.tensor_tensor(flat, flat, spread(total[:, :], 2, keys), ALU.mult).then_inc(prob_done, 1)
            for n in range(3):
                dve.wait_ge(summed, n + 1)
                src = banks[n][:, :].rearrange("p (h t d) -> p t h d", h=2, t=TT)
                dst = out[:, :, 2 * n * HD:2 * (n + 1) * HD].rearrange("p t (h d) -> p t h d", h=2)
                dve.tensor_copy(dst, src).then_inc(written, 1)

        @block.scalar
        def _(act):
            act.wait_ge(shifted, 1)
            act.activation(cs[:], cs[:], ACT.Exp, scale=HEAD_SCALE).then_inc(exp_done, 1)
            for n in range(n_u // 4):
                act.wait_ge(turned, n + 1)
                act.activation(cs_t[:, 4 * n:4 * n + 4, :].rearrange("k u t -> k (u t)"), banks[2 + n][0:keys, :],
                               ACT.Copy).then_inc(taken, 1)


def head_norm(core, name, o, mix, first, gain):
    heads = o.shape[2] // HD
    n = TT * heads
    with core.room(**{f"{name}_sq": [P, TT, heads * HD], f"{name}_rs": [P, n]}) as (sq, rs), \
            core.stage("squared", "summed", "var_done", "root_done", "inverted", "scaled", "turned", "taken") as (
                block, squared, summed, var_done, root_done, inverted, scaled, turned, taken):
        @block.scalar
        def _(act):
            act.activation(sq[:], o[:], ACT.Square).then_inc(squared, 1)
            act.wait_ge(var_done, 1)
            act.activation(rs[:, :], rs[:, :], ACT.Sqrt).then_inc(root_done, 1)
            for j in range(heads // 2):
                act.wait_ge(turned, j + 1)
                act.activation(mix[:, first + j, :], core.banks[j][:, :], ACT.Identity, scale=gain(j)).then_inc(taken, 1)

        @block.vector
        def _(dve):
            dve.wait_ge(squared, 1)
            dve.tensor_reduce(rs[:, :], sq[:].rearrange("p t (h d) -> p (t h) d", d=HD), AX_X, ALU.add).then_inc(summed, 1)
            dve.wait_ge(summed, 1)
            dve.tensor_scalar(rs[:, :], rs[:, :], 1.0 / HD, NORM_EPS, ALU.mult, ALU.add).then_inc(var_done, 1)
            dve.wait_ge(root_done, 1)
            dve.reciprocal(rs[:, :], rs[:, :]).then_inc(inverted, 1)
            dve.wait_ge(inverted, 1)
            o3 = o[:].rearrange("p t (h d) -> p (t h) d", d=HD)
            dve.tensor_tensor(o3, o3, spread(rs[:, :], 2, HD), ALU.mult).then_inc(scaled, 1)

        @block.tensor
        def _(pe):
            pe.wait_ge(scaled, 1)
            for j in range(heads // 2):
                for t in range(TT):
                    mm = pe.transpose(core.banks[j][:, t * P:(t + 1) * P], o[:, t, j * P:(j + 1) * P], core.const("ident"))
                mm.then_inc(turned, 1)


def load(core, pairs):
    with core.stage("loaded") as (block, loaded):
        @block.sync
        def _(sp):
            for dst, src in pairs:
                sp.dma_start(dst, src).then_inc(loaded, 16)
            sp.wait_ge(loaded, 16 * len(pairs))


def key_pairs(k, out):
    top, low = slice(0, HD), slice(HD, P)
    return [(out[top, 0, :], k[top, :]), (out[low, 0, :], k[top, :]), (out[:, 1, :], k[:, :]),
            (out[top, 2, :], k[low, :]), (out[low, 2, :], k[low, :])]


def repeat_values(core, pairs):
    with core.stage("repeated") as (block, repeated):
        @block.vector
        def _(dve):
            for dst, src in pairs:
                for t in range(TT):
                    dve.tensor_copy(dst[:, t, :].rearrange("p (g r d) -> p g r d", g=KV_H, d=HD),
                                    spread(src[:, t, :].rearrange("p (g d) -> p g d", g=KV_H), 2, NSA_H // KV_H))\
                       .then_inc(repeated, 1)


def nsa(core, w, h, cmp, mix):
    with core.room(nsa_o=[P, TT, NSA_H * HD], nsa_q=[P, 6, SEQ], nsa_g=[P, TT, 146], nsa_kx=[P, PAIRS, SEQ],
                   nsa_vx=[P, TT, NSA_H * HD], kc=[P, PAIRS, N_CMP + 1], vc=[N_CMP + 1, KV_H * HD]) as (
            o, qk, vg, kx, vx, kc, vc):
        gemm(core, "nsa_qk", w[:, 0:768], h, [(0, SEQ)], lambda tile, n: qk[:, bass.ds(tile, 1), :], 6, 6)
        q = qk[:, 0:3, :]
        gemm_tokens(core, "nsa_vw", w[:, AT2["vw"]:AT2["rw"]], h, TT, lambda t, s: vg[:, t, :], 146)
        with core.stage("gated") as (block, gated):
            @block.scalar
            def _(act):
                act.activation(vg[:, :, 128:146], vg[:, :, 128:146], ACT.Sigmoid).then_inc(gated, 1)
        compress(core, 0, qk[:, 3, :], cmp["pos"][0], cmp["w1"][0, 0], cmp["w2"][0, 0], kc, None)
        compress(core, 1, qk[:, 4, :], cmp["pos"][1], cmp["w1"][0, 1], cmp["w2"][0, 1], None, vc)
        all_gates = vg[:, :, 128:146].rearrange("p t (h b) -> p h t b", b=3)
        compressed_attention(core, q, kc, vc, o, all_gates[:, :, :, 0])

        def gates(branch):
            return lambda j, e, t: vg[:, t, bass.ds(j * 6 + (128 + 3 * e + branch), 1)]

        load(core, key_pairs(qk[:, 5, :], kx))
        with core.room(vs=[P, TT, KV_H * HD]) as (vs,):
            gemm_tokens(core, "nsa_vs", w[:, AT2["vs"]:AT2["kw"]], h, TT, lambda t, s: vs[:, t, :], 128)
            repeat_values(core, [(vx, vs)])
        causal_attention(core, "slc", q, kx, vx, o, gates(1))
        gemm(core, "nsa_kw", w[:, AT2["kw"]:AT2["vw"]], h, [(0, SEQ)], lambda tile, n: qk[:, bass.ds(tile + 5, 1), :], 1, 1)
        load(core, key_pairs(qk[:, 5, :], kx))
        repeat_values(core, [(vx, vg[:, :, 0:128])])
        causal_attention(core, "win", q, kx, vx, o, gates(2))
        head_norm(core, "nsa", o, mix, 0, lambda j: core.col("nsa_gain", j))


def moba(core, w, h, mix):
    with core.room(moba_o=[P, TT, MOBA_H * HD], moba_qk=[P, 6, SEQ], moba_v=[P, TT, MOBA_H * HD]) as (o, qk, v):
        gemm(core, "moba_qk", w[:, AT2["mq"]:AT2["mv"]], h, [(0, SEQ)], lambda tile, n: qk[:, bass.ds(tile, 1), :], 6, 6)
        gemm_tokens(core, "moba_v", w[:, AT2["mv"]:], h, TT, lambda t, s: v[:, t, :], MOBA_H * HD)
        causal_attention(core, "moba_a", qk[:, 0:3, :], qk[:, 3:6, :], v, o, None)
        head_norm(core, "moba_n", o, mix, 5, lambda j: core.col("moba_gain", j))


def rwkv_inputs(core, w, h, lora, r, v, gate, bonus, a_in, b_out, k_out, r_in, fade):
    with core.room(rw_p=[P, 7, SEQ + 1], rw_m=[P, 7, SEQ], rw_log=[P, 2, SEQ], rw_cum=[P, 2, SEQ], rw_a=[P, 2, SEQ],
                   rw_kk=[P, 2, SEQ], rw_t=[P, 2, SEQ], rw_t2=[P, 2, SEQ], rw_reset=[P, 2 * SEQ], rw_lora=[P, 256]) as (
            p, m, log_w, cum, a, kk, t1, t2, reset, lora_sb):
        with core.stage("first", "ones_in", "lora_in") as (block, first, ones_in, lora_in):
            @block.sync
            def _(sp):
                sp.dma_start(lora_sb[:], lora).then_inc(lora_in, 16)
                sp.wait_ge(lora_in, 16)

            @block.vector
            def _(dve):
                dve.memset(p[:, :, 0:1], 0.0).then_inc(first, 1)
                dve.memset(reset[:, :], 1.0).then_inc(ones_in, 1)
                dve.wait_ge(ones_in, 1)
                dve.memset(reset[:, ::RW_C], 0.0)
        gemm(core, "rw", w[:, AT2["rw"]:AT2["mq"]], h, [(0, SEQ)], lambda tile, n: p[:, bass.ds(tile, 1), 1:SEQ + 1], 7, 7)
        k = m[:, 2:4, :]
        with core.stage("step", "mixed", "squashed", "low_rank", "w_done", "a_done", "g_done", "kk_raw", "kk_sq", "kk_sum",
                        "kk_root", "rkr", "rkr_sum", "cum_done", "cum_exp", "cum_neg_exp", "before_exp", "before") as (
                block, step, mixed, squashed, low_rank, w_done, a_done, g_done, kk_raw, kk_sq, kk_sum, kk_root, rkr,
                rkr_sum, cum_done, cum_exp, cum_neg_exp, before_exp, before):
            banks = core.banks

            @block.vector
            def _(dve):
                steps = 0
                for n in range(7):
                    dve.tensor_tensor(m[:, n, :], p[:, n, 0:SEQ], p[:, n, 1:SEQ + 1], ALU.subtract).then_inc(step, 1)
                for n in (6, 0, 1, 2, 3, 4, 5):
                    dve.wait_ge(step, 7)
                    dve.scalar_tensor_tensor(out=m[:, n, :], in0=m[:, n, :], scalar=core.col("rw_mu", n),
                                             in1=p[:, n, 1:SEQ + 1], op0=ALU.mult, op1=ALU.add).then_inc(mixed, 1)
                dve.wait_ge(mixed, 7)
                for j in range(2):
                    dve.tensor_scalar(kk[:, j, :], k[:, j, :], core.col("rw_k_k", j), None, ALU.mult).then_inc(kk_raw, 1)
                dve.wait_ge(w_done, 2)
                dve.tensor_scalar(log_w[:], log_w[:], -RW_DECAY, None, ALU.mult).then_inc(step, 1)
                dve.wait_ge(step, 8)
                dve.tensor_tensor_scan(cum[:].rearrange("p j t -> p (j t)"), reset[:, :],
                                       log_w[:].rearrange("p j t -> p (j t)"), 0.0, ALU.mult, ALU.add).then_inc(cum_done, 1)
                dve.wait_ge(cum_done, 1)
                dve.tensor_tensor(t1[:], cum[:], log_w[:], ALU.subtract).then_inc(before, 1)
                dve.wait_ge(a_done, 2)
                for j in range(2):
                    dve.tensor_scalar(t2[:, j, :], a[:, j, :], -1.0, core.col("rw_k_a", j), ALU.add, ALU.mult)\
                       .then_inc(step, 1)
                dve.wait_ge(step, 10)
                dve.wait_ge(kk_raw, 2)
                dve.scalar_tensor_tensor(out=k, in0=t2[:], scalar=1.0, in1=k, op0=ALU.add, op1=ALU.mult).then_inc(step, 1)
                dve.wait_ge(step, 11)
                for j in range(2):
                    dve.scalar_tensor_tensor(out=t2[:, j, :], in0=m[:, j, :], scalar=core.col("rw_r_k", j), in1=k[:, j, :],
                                             op0=ALU.mult, op1=ALU.mult).then_inc(rkr, 1)
                dve.tensor_copy(v[:], m[:, 4:6, :]).then_inc(step, 1)
                dve.wait_ge(rkr_sum, 1)
                dve.wait_ge(step, 12)
                for j in range(2):
                    dve.tensor_tensor(bonus[:, j, :], banks[6 + j][:, :], v[:, j, :], ALU.mult).then_inc(step, 1)
                dve.wait_ge(kk_root, 2)
                dve.tensor_scalar(t2[:], t2[:], 1e-12, None, ALU.max).then_inc(step, 1)
                dve.wait_ge(step, 15)
                dve.reciprocal(t2[:], t2[:]).then_inc(step, 1)
                dve.wait_ge(step, 16)
                dve.tensor_tensor(kk[:], kk[:], t2[:], ALU.mult).then_inc(step, 1)
                dve.wait_ge(step, 17)
                dve.wait_ge(before_exp, 1)
                dve.scalar_tensor_tensor(out=a_in[:], in0=kk[:], scalar=-1.0, in1=t1[:], op0=ALU.mult, op1=ALU.mult)\
                   .then_inc(step, 1)
                dve.tensor_tensor(a[:], a[:], kk[:], ALU.mult).then_inc(step, 1)
                dve.wait_ge(step, 19)
                dve.wait_ge(cum_neg_exp, 1)
                dve.tensor_tensor(b_out[:], a[:], log_w[:], ALU.mult).then_inc(step, 1)
                dve.tensor_tensor(k_out[:], k, log_w[:], ALU.mult).then_inc(step, 1)
                dve.wait_ge(cum_exp, 1)
                dve.tensor_tensor(r_in[:], m[:, 0:2, :], cum[:], ALU.mult).then_inc(step, 1)
                dve.tensor_copy(fade[:], cum[:, :, RW_C - 1::RW_C]).then_inc(step, 1)
                del steps

            @block.scalar
            def _(act):
                act.wait_ge(mixed, 1)
                act.activation(m[0:32, 6, :], m[0:32, 6, :], ACT.Tanh).then_inc(squashed, 1)
                act.activation(m[64:128, 6, :], m[64:128, 6, :], ACT.Sigmoid).then_inc(squashed, 1)
                for j in range(2):
                    act.wait_ge(low_rank, j + 1)
                    act.activation(log_w[:, j, :], banks[j][:, :], ACT.Sigmoid, bias=core.col("rw_w0", j)).then_inc(w_done, 1)
                    act.activation(a[:, j, :], banks[2 + j][:, :], ACT.Sigmoid, bias=core.col("rw_a0", j)).then_inc(a_done, 1)
                    act.activation(gate[:, j, :], banks[4 + j][:, :], ACT.Copy).then_inc(g_done, 1)
                act.wait_ge(kk_raw, 2)
                act.wait_ge(mixed, 7)
                act.activation(r[:], kk[:], ACT.Square).then_inc(kk_sq, 1)
                act.wait_ge(rkr_sum, 1)
                for j in range(2):
                    act.wait_ge(kk_sum, 1)
                    act.activation(t2[:, j, :], banks[j][:, :], ACT.Sqrt).then_inc(kk_root, 1)
                act.wait_ge(before, 1)
                act.activation(t1[:], t1[:], ACT.Exp).then_inc(before_exp, 1)
                act.activation(log_w[:], cum[:], ACT.Exp, scale=-1.0).then_inc(cum_neg_exp, 1)
                act.wait_ge(cum_neg_exp, 1)
                act.activation(cum[:], cum[:], ACT.Exp).then_inc(cum_exp, 1)

            @block.tensor
            def _(pe):
                pe.wait_ge(squashed, 2)
                for j in range(2):
                    cols = slice(j * P, (j + 1) * P)
                    pe.matmul(banks[j][:, :], lora_sb[0:32, cols], m[0:32, 6, :], start=True, stop=True)
                    pe.matmul(banks[2 + j][:, :], lora_sb[32:64, cols], m[32:64, 6, :], start=True, stop=True)
                    pe.matmul(banks[4 + j][:, :], lora_sb[64:128, cols], m[64:128, 6, :], start=True, stop=True)\
                      .then_inc(low_rank, 1)
                pe.wait_ge(rkr, 2)
                for j in range(2):
                    mm = pe.matmul(banks[6 + j][:, :], core.const("head_ones"), t2[:, j, :], start=True, stop=True)
                mm.then_inc(rkr_sum, 1)
                pe.wait_ge(kk_sq, 1)
                pe.wait_ge(w_done, 2)
                for j in range(2):
                    mm = pe.matmul(banks[j][:, :], core.const("head_ones"), r[:, j, :], start=True, stop=True)
                mm.then_inc(kk_sum, 1)


def unit(u):
    return slice(u * RW_C, (u + 1) * RW_C)


def each_head(pe, bank, lhs, rhs, start=True, stop=True):
    for e in range(2):
        rows = slice(HD * e, HD * e + HD)
        mm = pe.matmul(bank[rows], lhs(rows, e), rhs(rows, e), start=start, stop=stop)
    return mm


def rwkv_products(core, name, jobs):
    banks = core.banks
    with core.stage("made", "taken") as (block, made, taken):
        @block.tensor
        def _(pe):
            for n, (lhs, rhs, _, _) in enumerate(jobs):
                for j in range(2):
                    k = 2 * n + j
                    if k >= 8:
                        pe.wait_ge(taken, k - 7)
                    for c in range(NC):
                        tok = unit(c)
                        mm = each_head(pe, banks[k % 8][:, tok], lambda r, e: lhs[r, j, tok],
                                       lambda r, e: rhs[r, j, tok] if rhs is not None
                                       else core.const("ident")[r, HD * e:HD * e + HD])
                    mm.then_inc(made, 1)

        @block.vector
        def _(dve):
            for n, (_, _, mask, out) in enumerate(jobs):
                for j in range(2):
                    dve.wait_ge(made, 2 * n + j + 1)
                    dst = out[:, NC * j:NC * (j + 1), :]
                    src = banks[(2 * n + j) % 8][:, :].rearrange("p (c t) -> p c t", c=NC)
                    if mask is None:
                        dve.tensor_copy(dst, src).then_inc(taken, 1)
                    else:
                        dve.tensor_tensor(dst, src, spread(mask, 1, NC), ALU.mult).then_inc(taken, 1)


def rwkv_inverse(core, lab, lab_t, t_inv, tt_inv, level, y):
    banks = core.banks

    def level_mask(m, turned):
        pair = {1: (1, 0), 2: (1, 1), 4: (4, 0), 8: (4, 1), 16: (16, 0), 32: (16, 1)}[m]
        name = f"rw_level{'T' if turned else ''}_{pair[0]}_{2 * pair[0]}"
        return spread(core.const(name)[:, RW_C * pair[1]:RW_C * (pair[1] + 1)], 1, RU)

    with core.stage("masked", "t_done", "y_done", "y_taken", "z_done", "zt_done") as (
            block, masked, t_done, y_done, y_taken, z_done, zt_done):
        sizes = [2, 4, 8, 16, 32]

        @block.vector
        def _(dve):
            eye = spread(core.const("rw_eye")[:, 0:RW_C], 1, RU)
            dve.tensor_tensor(t_inv[:], lab[:], level_mask(1, False), ALU.mult).then_inc(masked, 1)
            dve.tensor_tensor(tt_inv[:], lab_t[:], level_mask(1, True), ALU.mult).then_inc(masked, 1)
            dve.wait_ge(masked, 2)
            dve.tensor_tensor(t_inv[:], t_inv[:], eye, ALU.add).then_inc(t_done, 1)
            dve.tensor_tensor(tt_inv[:], tt_inv[:], eye, ALU.add).then_inc(t_done, 1)
            for n, m in enumerate(sizes):
                if n:
                    dve.wait_ge(y_done, 2 * n)
                dve.tensor_tensor(level[:], lab_t[:], level_mask(m, True), ALU.mult).then_inc(masked, 1)
                for j in range(2):
                    units = slice(NC * j, NC * (j + 1))
                    dve.wait_ge(z_done, 2 * n + j + 1)
                    dve.wait_ge(t_done, 2 + 4 * n)
                    dve.tensor_tensor(t_inv[:, units, :], t_inv[:, units, :],
                                      banks[2 + j][:, :].rearrange("p (c t) -> p c t", c=NC), ALU.add).then_inc(t_done, 1)
                    dve.wait_ge(zt_done, 2 * n + 2)
                    dve.tensor_tensor(tt_inv[:, units, :], tt_inv[:, units, :],
                                      banks[4 + j][:, :].rearrange("p (c t) -> p c t", c=NC), ALU.add).then_inc(t_done, 1)

        @block.scalar
        def _(act):
            for n in range(len(sizes)):
                for j in range(2):
                    act.wait_ge(y_done, 2 * n + j + 1)
                    if n:
                        act.wait_ge(zt_done, 2 * n)
                    act.activation(y[:, NC * j:NC * (j + 1), :], banks[j][:, :].rearrange("p (c t) -> p c t", c=NC),
                                   ACT.Copy).then_inc(y_taken, 1)

        @block.tensor
        def _(pe):
            for n in range(len(sizes)):
                pe.wait_ge(masked, 3 + n)
                pe.wait_ge(t_done, 2 + 4 * n)
                for j in range(2):
                    for c in range(NC):
                        u = NC * j + c
                        mm = each_head(pe, banks[j][:, unit(c)], lambda r, e: level[r, u, :], lambda r, e: t_inv[r, u, :])
                    mm.then_inc(y_done, 1)
                for j in range(2):
                    pe.wait_ge(y_taken, 2 * n + j + 1)
                    for c in range(NC):
                        u = NC * j + c
                        mm = each_head(pe, banks[2 + j][:, unit(c)], lambda r, e: tt_inv[r, u, :], lambda r, e: y[r, u, :])
                    mm.then_inc(z_done, 1)
                    for c in range(NC):
                        u = NC * j + c
                        mm = each_head(pe, banks[4 + j][:, unit(c)], lambda r, e: y[r, u, :], lambda r, e: tt_inv[r, u, :])
                    mm.then_inc(zt_done, 1)


def rwkv_scan(core, a_in, r_in, lak_t, lrb_t, lrk_t, tt_inv, b_tok, k_tok, v_tok, fade, state, x, sa, o):
    banks = core.banks
    with core.stage("x_made", "x_taken", "sa_made", "sa_taken", "o_made", "o_taken", "s_made", "s_added", "s_faded",
                    "cleared") as (block, x_made, x_taken, sa_made, sa_taken, o_made, o_taken, s_made, s_added, s_faded,
                                   cleared):
        @block.tensor
        def _(pe):
            pe.wait_ge(cleared, 1)
            for c in range(NC):
                tok = unit(c)
                if c:
                    pe.wait_ge(s_faded, 2 * c)
                for j in range(2):
                    u = NC * j + c
                    each_head(pe, banks[0][:, unit(j)], lambda r, e: lak_t[r, u, :], lambda r, e: v_tok[r, u, :], stop=False)
                    mm = each_head(pe, banks[0][:, unit(j)], lambda r, e: a_in[r, j, tok], lambda r, e: state[r, j, :],
                                   start=False)
                mm.then_inc(x_made, 1)
                pe.wait_ge(x_taken, c + 1)
                for j in range(2):
                    u = NC * j + c
                    mm = each_head(pe, banks[1][:, unit(j)], lambda r, e: tt_inv[r, u, :], lambda r, e: x[r, j, :])
                mm.then_inc(sa_made, 1)
                pe.wait_ge(sa_taken, c + 1)
                if c:
                    pe.wait_ge(o_taken, c)
                for j in range(2):
                    u = NC * j + c
                    each_head(pe, banks[3][:, unit(j)], lambda r, e: b_tok[r, u, :], lambda r, e: sa[r, j, :], stop=False)
                    mm = each_head(pe, banks[3][:, unit(j)], lambda r, e: k_tok[r, u, :], lambda r, e: v_tok[r, u, :],
                                   start=False)
                mm.then_inc(s_made, 1)
                for j in range(2):
                    u = NC * j + c
                    each_head(pe, banks[2][:, unit(j)], lambda r, e: state[r, j, :], lambda r, e: r_in[r, j, tok], stop=False)
                    each_head(pe, banks[2][:, unit(j)], lambda r, e: sa[r, j, :], lambda r, e: lrb_t[r, u, :],
                              start=False, stop=False)
                    mm = each_head(pe, banks[2][:, unit(j)], lambda r, e: v_tok[r, u, :], lambda r, e: lrk_t[r, u, :],
                                   start=False)
                mm.then_inc(o_made, 1)

        @block.vector
        def _(dve):
            dve.memset(state[:], 0.0).then_inc(cleared, 1)
            for c in range(NC):
                dve.wait_ge(x_made, c + 1)
                dve.tensor_copy(x[:], banks[0][:, 0:P].rearrange("p (j t) -> p j t", j=2)).then_inc(x_taken, 1)
                dve.wait_ge(sa_made, c + 1)
                if c:
                    dve.wait_ge(o_made, c)
                dve.tensor_copy(sa[:], banks[1][:, 0:P].rearrange("p (j t) -> p j t", j=2)).then_inc(sa_taken, 1)
                dve.wait_ge(s_made, c + 1)
                dve.wait_ge(o_made, c + 1)
                dve.tensor_tensor(state[:], state[:], banks[3][:, 0:P].rearrange("p (j t) -> p j t", j=2), ALU.add)\
                   .then_inc(s_added, 1)
                dve.wait_ge(s_added, c + 1)
                for j in range(2):
                    dve.tensor_scalar(state[:, j, :], state[:, j, :], fade[:, j, c:c + 1], None, ALU.mult)\
                       .then_inc(s_faded, 1)

        @block.scalar
        def _(act):
            for c in range(NC):
                act.wait_ge(o_made, c + 1)
                act.activation(o[:, :, unit(c)], banks[2][:, 0:P].rearrange("p (j t) -> p j t", j=2), ACT.Copy)\
                   .then_inc(o_taken, 1)


def rwkv_output(core, o, bonus, gate, mix):
    banks = core.banks
    with core.room(rw_sq=[P, 2, SEQ], rw_rstd=[P, 2, SEQ]) as (sq, rstd), \
            core.stage("summed", "centered", "squared", "sq_summed", "var_done", "root_done", "inverted", "scaled",
                       "shifted", "bonused") as (block, summed, centered, squared, sq_summed, var_done, root_done,
                                                 inverted, scaled, shifted, bonused):
        @block.tensor
        def _(pe):
            for j in range(2):
                mm = pe.matmul(banks[j][:, :], core.const("head_ones"), o[:, j, :], start=True, stop=True)
            mm.then_inc(summed, 1)
            for j in range(2):
                pe.wait_ge(squared, j + 1)
                mm = pe.matmul(banks[2 + j][:, :], core.const("head_ones"), sq[:, j, :], start=True, stop=True)
                mm.then_inc(sq_summed, 1)

        @block.vector
        def _(dve):
            dve.wait_ge(summed, 1)
            for j in range(2):
                dve.scalar_tensor_tensor(out=o[:, j, :], in0=banks[j][:, :], scalar=-1.0 / HD, in1=o[:, j, :],
                                         op0=ALU.mult, op1=ALU.add).then_inc(centered, 1)
            for j in range(2):
                dve.wait_ge(sq_summed, j + 1)
                dve.tensor_scalar(rstd[:, j, :], banks[2 + j][:, :], 1.0 / HD, RW_LN_EPS, ALU.mult, ALU.add)\
                   .then_inc(var_done, 1)
            for j in range(2):
                dve.wait_ge(root_done, j + 1)
                dve.reciprocal(rstd[:, j, :], rstd[:, j, :]).then_inc(inverted, 1)
            for j in range(2):
                dve.wait_ge(inverted, j + 1)
                dve.scalar_tensor_tensor(out=o[:, j, :], in0=o[:, j, :], scalar=core.col("rw_lnx_w", j), in1=rstd[:, j, :],
                                         op0=ALU.mult, op1=ALU.mult).then_inc(scaled, 1)
            for j in range(2):
                dve.wait_ge(scaled, j + 1)
                dve.scalar_tensor_tensor(out=o[:, j, :], in0=o[:, j, :], scalar=core.col("rw_lnx_b", j), in1=bonus[:, j, :],
                                         op0=ALU.add, op1=ALU.add).then_inc(shifted, 1)
            for j in range(2):
                dve.wait_ge(shifted, j + 1)
                dve.tensor_tensor(mix[:, 3 + j, :], o[:, j, :], gate[:, j, :], ALU.mult).then_inc(bonused, 1)

        @block.scalar
        def _(act):
            for j in range(2):
                act.wait_ge(centered, j + 1)
                act.activation(sq[:, j, :], o[:, j, :], ACT.Square).then_inc(squared, 1)
            for j in range(2):
                act.wait_ge(var_done, j + 1)
                act.activation(rstd[:, j, :], rstd[:, j, :], ACT.Sqrt).then_inc(root_done, 1)


def rwkv(core, w, h, lora, mix):
    two, by_unit = [P, 2, SEQ], [P, RU, RW_C]
    with core.room(rw_v=two, rw_gate=two, rw_bonus=two, rw_a_in=two, rw_b_out=two, rw_k_out=two, rw_r_in=two, rw_o=two,
                   rw_fade=[P, 2, NC]) as (v, gate, bonus, a_in, b_out, k_out, r_in, o, fade):
        rwkv_inputs(core, w, h, lora, o, v, gate, bonus, a_in, b_out, k_out, r_in, fade)
        with core.room(lab=by_unit, lab_t=by_unit, lak_t=by_unit, lrb_t=by_unit, lrk_t=by_unit, b_tok=by_unit,
                       k_tok=by_unit, v_tok=by_unit, t_inv=by_unit, tt_inv=by_unit, level=by_unit, rw_y=by_unit,
                       rw_state=[P, 2, HD], rw_x=[P, 2, HD], rw_sa=[P, 2, HD]) as (
                lab, lab_t, lak_t, lrb_t, lrk_t, b_tok, k_tok, v_tok, t_inv, tt_inv, level, y, state, x, sa):
            before = core.const("rw_masks")[:, 0:RW_C]
            until = core.const("rw_masks")[:, RW_C:2 * RW_C]
            after = core.const("rw_eye")[:, RW_C:2 * RW_C]
            rwkv_products(core, "rw", [
                (b_out, a_in, before, lab_t), (a_in, b_out, after, lab), (k_out, a_in, before, lak_t),
                (b_out, r_in, until, lrb_t), (k_out, r_in, until, lrk_t),
                (b_out, None, None, b_tok), (k_out, None, None, k_tok), (v, None, None, v_tok)])
            rwkv_inverse(core, lab, lab_t, t_inv, tt_inv, level, y)
            rwkv_scan(core, a_in, r_in, lak_t, lrb_t, lrk_t, tt_inv, b_tok, k_tok, v_tok, fade, state, x, sa, o)
        rwkv_output(core, o, bonus, gate, mix)


def causal_tap(n):
    return lambda b: b[:, n:n + SEQ]


def second_block(core, x, w):
    with core.split_room(h2=[P, DT, SEQ]) as (h,), core.room(mix2=[P, DT, SEQ]) as (mix,):
        norm(core, "attn_norm", x, mix, lambda k: core.col("attn_norm", k), eps=NORM_EPS, center=False)
        split(core, [(mix, h)])
        with core.more_constants(ODD_CONST, w["const"]):
            nsa(core, w["w_in_2"], h, w["cmp"], mix)
            moba(core, w["w_in_2"], h, mix)
            rwkv(core, w["w_in_2"], h, w["lora"], mix)
        with core.room(y2=[P, DT, SEQ]) as (y,):
            split(core, [(mix, h)])
            gemm(core, "out2", w["w_out_2"], h, [(0, SEQ)], lambda tile, n: y[:, bass.ds(tile, 1), :], DT, 4)
            residual(core, x, y, None)

    def fill(parts):
        with core.room(normed=[P, DT, SEQ]) as (normed,):
            norm(core, "ffn_norm", x, normed, lambda k: core.col("ffn_norm", k), eps=NORM_EPS, center=False)
            split(core, [(normed, parts)])

    with glu_ffn(core, "ffn2", w["ffn_w_in_2"], D_FF, 0, w["ffn_w_out_2"], fill, lambda: core.room(y3=[P, DT, SEQ]),
                 SEQ + 2, lambda b: b[:, 2:SEQ + 2], [causal_tap(n) for n in range(3)],
                 lambda t, n: core.col("ffn2_conv_w", t, n), lambda t: core.col("ffn2_conv_b", t), ACT.Silu) as y:
        residual(core, x, y, None)
    norm(core, "final_norm", x, x, lambda k: core.col("final_norm", k), eps=NORM_EPS, center=False)


def condition(core, weights, cond, layer, mods):
    ring_n, width = 3, 512
    w = weights.rearrange("(k p) f -> p k f", p=P)
    slabs = weights.shape[1] // width
    steps = slabs // ring_n
    tiles = weights.shape[1] // P
    with core.room(ada_ring=[P, ring_n, DT, width], ada_rows=[2, slabs * width]) as (ring, rows), \
            core.stage("slab_in0", "slab_in1", "slab_in2", "slab_done", "banks_free", "slots_refilled", "turned", "biased") as (
                block, slab_in0, slab_in1, slab_in2, slab_done, banks_free, slots_refilled, turned, biased):
        slab_in = [slab_in0, slab_in1, slab_in2]

        @block.sync
        def _(sp):
            for u in range(ring_n):
                sp.dma_start(ring[:, u], w[:, :, u * width:(u + 1) * width]).then_inc(slab_in[u], 16)
            with sp.Fori(1, steps) as i:
                for u in range(ring_n):
                    feature = sp.snap((i * ring_n + u) * width)
                    sp.wait_ge(slab_done, (i - 1) * ring_n + u + 1)
                    sp.sem_inc(slots_refilled, 1)
                    sp.dma_start(ring[:, u], w[:, :, bass.ds(feature, width)]).then_inc(slab_in[u], 16)

        @block.tensor
        def _(pe):
            with pe.Fori(0, steps) as i:
                for u in range(ring_n):
                    pe.wait_ge(slab_in[u], (i + 1) * 16)
                    pe.wait_ge(banks_free, i * ring_n + u + 1)
                    for k in range(DT):
                        mm = pe.matmul(core.banks[u][0:2, :], cond[:, k, :], ring[:, u, k, :], start=(k == 0),
                                       stop=(k == DT - 1))
                    mm.then_inc(slab_done, 1)
            pe.wait_ge(banks_free, ring_n + slabs)
            for t in range(tiles):
                mm = pe.transpose(core.banks[4][:, 2 * t:2 * t + 2], rows[:, t * P:(t + 1) * P], core.const("ident")[0:2, 0:2])
            mm.then_inc(turned, 1)

        @block.scalar
        def _(act):
            act.sem_inc(banks_free, ring_n)
            with act.Fori(0, steps) as i:
                for u in range(ring_n):
                    act.wait_ge(slab_done, i * ring_n + u + 1)
                    act.activation(rows[:, bass.ds((i * ring_n + u) * width, width)], core.banks[u][0:2, :], ACT.Copy)\
                       .then_inc(banks_free, 1)

        @block.vector
        def _(dve):
            at = COL_AT[f"ada_b{layer}"]
            dve.wait_ge(turned, 1)
            dve.tensor_tensor(mods[:], core.banks[4][:, 0:2 * tiles].rearrange("p (t w) -> p t w", w=2),
                              spread(core.cols_sb[:, at:at + tiles], 2, 2), ALU.add).then_inc(biased, 1)


def conditioning(core, ada_w, mods):
    with core.room(cond=[P, DT, 2]) as (cond,):
        with core.stage("cond_done") as (block, cond_done):
            @block.scalar
            def _(act):
                at = COL_AT["c"]
                act.activation(cond[:].rearrange("p k w -> p (k w)"), core.cols_sb[:, at:at + 2 * DT], ACT.Silu)\
                   .then_inc(cond_done, 1)
        for layer in range(DEPTH):
            condition(core, ada_w[layer], cond, layer, mods[layer])
    with core.stage("raised") as (block, raised):
        @block.vector
        def _(dve):
            for layer in range(DEPTH):
                for part in (1, 4):
                    scale = mods[layer][:, part * DT:(part + 1) * DT, :]
                    dve.tensor_scalar(scale, scale, 1.0, None, ALU.add).then_inc(raised, 1)


def model(nc, x, ctx, const, cols, rows, lora, pos, ada_w, mix_w_in, mix_w_out, conf_w1, conf_w2, ffn_w_up, ffn_w_down,
          w_in_2, cmp_w1, cmp_w2, w_out_2, ffn_w_in_2, ffn_w_out_2, out):
    features = lambda a: a.rearrange("(k p) t -> p k t", p=P)
    with ExitStack() as stack:
        core = Core(nc, stack)
        mods = [stack.enter_context(nc.sbuf_tensor(f"mods{layer}", [P, 6 * DT, 2], F32)) for layer in range(DEPTH)]
        load(core, [(core.const_sb[:], const[:, 0:ALWAYS, :]), (core.cols_sb[:], cols)])
        conditioning(core, ada_w, mods)

        def mod(layer, part, who=0):
            return lambda k: mods[layer][:, part * DT + k, who:who + 1]

        def finish_half(name, layer, n, x_sb, y_sb):
            residual(core, x_sb, y_sb, mod(layer, 3 * n + 2))
            norm(core, name, x_sb, x_sb, lambda k: core.col("post_ln_g", k, 2 * layer + n),
                 lambda k: core.col("post_ln_b", k, 2 * layer + n))

        def ffn(layer, x_sb):
            def fill(parts):
                with core.room(modulated=[P, DT, SEQ]) as (modulated,):
                    modulate(core, x_sb, mod(layer, 3), mod(layer, 4), modulated)
                    split(core, [(modulated, parts)])

            with glu_ffn(core, f"ffn{layer}", ffn_w_up[layer], D_FF, 0, ffn_w_down[layer], fill,
                         lambda: core.room(ffn_y=[P, DT, SEQ]), GRID_PAD, grid_window(1, 1), GRID_TAPS,
                         lambda t, n: core.col(f"ffn_conv_w{layer}", t, n), lambda t: core.col("ffn_conv_b", t, layer),
                         ACT.Gelu) as y:
                finish_half(f"ln_ffn{layer}", layer, 1, x_sb, y)

        with core.room(x_sb=[P, DT, SEQ]) as (x_sb,):
            with core.split_room(h0=[P, DT, TOK]) as (h,), core.room(rows_sb=[P, 72]) as (rows_sb,):
                with core.room(tokens=[P, DT, TOK]) as (tokens,):
                    lat, both = slice(0, SEQ), slice(SEQ, TOK)
                    load(core, [(tokens[:, :, lat], features(x)), (tokens[:, :, both], features(ctx)), (rows_sb[:], rows)])
                    split(core, [(tokens[:, :, part], [side[:, :, part] for side in h]) for part in (lat, both)],
                          [(mod(0, 0), mod(0, 1)), (mod(0, 0, 1), mod(0, 1, 1))])
                with core.more_constants(MIXER_CONST, const):
                    even_mixer(core, mix_w_in[0], mix_w_out[0], h, x_sb, rows_sb)
            with core.room(x_again=[P, DT, SEQ]) as (x_again,):
                load(core, [(x_again[:], features(x))])
                with core.stage("scaled", "added") as (block, scaled, added):
                    @block.scalar
                    def _(act):
                        for k in range(DT):
                            act.activation(x_again[:, k, :], x_again[:, k, :], ACT.Identity, scale=ALPHA)\
                               .then_inc(scaled, 1)

                    @block.vector
                    def _(dve):
                        for k in range(DT):
                            dve.wait_ge(scaled, k + 1)
                            dve.scalar_tensor_tensor(out=x_sb[:, k, :], in0=x_sb[:, k, :], scalar=mod(0, 2)(k),
                                                     in1=x_again[:, k, :], op0=ALU.mult, op1=ALU.add).then_inc(added, 1)
            norm(core, "ln_mix0", x_sb, x_sb, lambda k: core.col("post_ln_g", k), lambda k: core.col("post_ln_b", k))
            ffn(0, x_sb)
            with core.split_room(h1=[P, DT, SEQ]) as (h,), core.room(y1=[P, DT, SEQ]) as (y,):
                modulate(core, x_sb, mod(1, 0), mod(1, 1), y)
                split(core, [(y, h)])
                conformer(core, conf_w1[0], conf_w2[0], h, y)
                finish_half("ln_mix1", 1, 0, x_sb, y)
            ffn(1, x_sb)
            second_block(core, x_sb, {"const": const, "w_in_2": w_in_2[0], "cmp": {"pos": pos, "w1": cmp_w1, "w2": cmp_w2}, "lora": lora,
                                      "w_out_2": w_out_2[0], "ffn_w_in_2": ffn_w_in_2[0], "ffn_w_out_2": ffn_w_out_2[0]})
            with core.stage("stored") as (block, stored):
                @block.sync
                def _(sp):
                    sp.dma_start(features(out), x_sb[:]).then_inc(stored, 16)
                    sp.wait_ge(stored, 16)


WEIGHTS = {
    "ada_w": "ada_w", "mix_w_in": "mix_w_in", "mix_w_out": "mix_w_out", "conf_w1": "conf_w1", "conf_w2": "conf_w2",
    "ffn_w_up": "ffn_w_up", "ffn_w_down": "ffn_w_down", "w_in_2": "w_in_2", "cmp_w1": "nsa_cmp_w1_2",
    "cmp_w2": "nsa_cmp_w2_2", "w_out_2": "w_out_2", "ffn_w_in_2": "ffn_w_in_2", "ffn_w_out_2": "ffn_w_out_2",
}


def laid_out(inputs):
    vectors = {name: inputs[name] for name in COLS if name in inputs}
    vectors["c"] = np.concatenate([inputs["c"], inputs["c_ctx"][None]])
    for layer in range(DEPTH):
        vectors[f"ada_b{layer}"] = inputs["ada_b"][layer]
        vectors[f"ffn_conv_w{layer}"] = inputs["ffn_conv_w"][layer]
    for name, source in (("attn_norm", "attn_norm_2"), ("ffn_norm", "ffn_norm_2"), ("final_norm", "final_norm_2"),
                         ("ffn2_conv_w", "ffn_conv_w_2"), ("ffn2_conv_b", "ffn_conv_b_2"), ("nsa_gain", "nsa_out_gain_2"),
                         ("moba_gain", "moba_out_gain_2")):
        vectors[name] = inputs[source]
    for name in ("mu", "w0", "a0", "k_k", "k_a", "r_k", "lnx_w", "lnx_b"):
        vectors[f"rw_{name}"] = inputs[f"rw_{name}_2"]
    arrays = {
        "x": np.ascontiguousarray(np.transpose(inputs["x"][0])),
        "ctx": np.ascontiguousarray(np.transpose(inputs["ctx"][0])),
        "const": constants(),
        "cols": columns(vectors),
        "rows": np.ascontiguousarray(np.concatenate([
            np.broadcast_to(np.reshape(inputs["ssd_dt_bias"], (1, 32)), (P, 32)),
            np.broadcast_to(np.reshape(inputs["ssd_a_log"], (1, 32)), (P, 32)),
            np.transpose(np.repeat(np.reshape(inputs["ssd_d"], (DT, 2)), SSD_P, axis=1))], axis=1)),
        "lora": np.ascontiguousarray(np.concatenate([inputs["rw_w2_2"][0], inputs["rw_a2_2"][0], inputs["rw_g2_2"][0]])),
        "pos": np.ascontiguousarray(np.transpose(np.reshape(inputs["nsa_cmp_pos_2"], (2, CMP_LEN // 2, P)), (0, 2, 1))),
    }
    for name, source in WEIGHTS.items():
        arrays[name] = np.ascontiguousarray(inputs[source])
    return arrays


def kernel(**inputs):
    import concourse.bacc as bacc
    from concourse.bass_utils import run_bass_kernel_spmd

    nc = bacc.Bacc("TRN2", target_bir_lowering=False, num_devices=1)
    arrays = {f"in_{name}": a for name, a in laid_out({k: np.asarray(v) for k, v in inputs.items()}).items()}
    args = [nc.dram_tensor(name, a.shape, mybir.dt.from_np(a.dtype), kind="ExternalInput").ap()
            for name, a in arrays.items()]
    out = nc.dram_tensor("out", (D, SEQ), F32, kind="ExternalOutput").ap()
    model(nc, *args, out)
    result = run_bass_kernel_spmd(nc, [arrays], core_ids=[0])
    return np.ascontiguousarray(np.transpose(result.results[0]["out"]))[None]
```

```python
from contextlib import ExitStack, contextmanager


import numpy as np

import concourse.bass as bass
from concourse import mybir

F32 = mybir.dt.float32
F32R = mybir.dt.float32r
U32 = mybir.dt.uint32
ALU = mybir.AluOpType
ACT = mybir.ActivationFunctionType
AX_X = mybir.AxisListType.X

P = 128
D = 1024
DT = D // P
SEQ = 512
CTX = 256
TOK = SEQ + CTX
DEPTH = 2
ALPHA = (2 * DEPTH) ** 0.25
EPS = 1e-5
D_FF = 2816
FT = D_FF // P
GRID_W = 64
ROWS = SEQ // GRID_W

SSD_HEADS = 16
SSD_P = 64
SSD_IN = SSD_HEADS * SSD_P
SSD_G = 2
SSD_N = 128
SSD_XBC = SSD_IN + 2 * SSD_G * SSD_N
SSD_K = 5
HG_HEADS = 8
MIX_AT = {}
at = 0
for part, size in (("z", SSD_IN), ("xbc", SSD_XBC), ("dt", 2 * SSD_HEADS), ("q", D), ("f", 2 * D), ("v", D), ("g", D)):
    MIX_AT[part] = at
    at += size
CONF_K = 31
CHUNK = 128
NEG = -1e30

HD = 64
NSA_H, KV_H, RW_H, MOBA_H = 6, 2, 4, 6
NORM_EPS = 1e-6
RW_C = 64
RW_DECAY = 0.606531
RW_LN_EPS = 64e-5
CMP_LEN, CMP_STRIDE, CMP_HID = 32, 16, 256
N_CMP = (SEQ - CMP_LEN) // CMP_STRIDE + 1
TT = SEQ // P
AT2 = {}
at = 0
for part, size in (("q", 384), ("kc", 128), ("vc", 128), ("ks", 128), ("vs", 128), ("kw", 128), ("vw", 128), ("gt", 18),
                   ("rw", 896), ("mq", 384), ("mk", 384), ("mv", 384)):
    AT2[part] = at
    at += size

LEVELS = [CHUNK >> (n + 1) for n in range(7)]
CONST = ["ident", "ones", "head_ones", "neg_since"]
ALWAYS = len(CONST)
SSD_CONST = ["until", "since", "neg_until"]
LEVEL_CONST = [[f"left_right_{m}" for m in LEVELS], [f"right_left_{m}" for m in LEVELS]]
ODD_CONST = ["rw_masks", "rw_level_1_2", "rw_level_4_8", "rw_level_16_32", "rw_levelT_1_2", "rw_levelT_4_8",
          "rw_levelT_16_32", "cmp_mask", "cmp_valid", "rw_eye"]
CONST += SSD_CONST + LEVEL_CONST[0] + LEVEL_CONST[1] + ODD_CONST
CONST_AT = {name: n for n, name in enumerate(CONST)}

COLS = {
    "ada_b0": (1, 6 * D), "ada_b1": (1, 6 * D), "post_ln_g": (4, D), "post_ln_b": (4, D), "ssd_conv_w": (SSD_K, SSD_XBC), "ssd_conv_b": (1, SSD_XBC),
    "ssd_norm_w": (1, D), "hg_norm_w": (1, D), "conf_b1": (2, D), "conf_dw_w": (CONF_K, D), "conf_dw_b": (1, D),
    "conf_ln_g": (1, D), "conf_ln_b": (1, D), "conf_b2": (1, D), "ffn_conv_w0": (9, D_FF), "ffn_conv_w1": (9, D_FF),
    "ffn_conv_b": (2, D_FF), "attn_norm": (1, D), "ffn_norm": (1, D), "final_norm": (1, D), "ffn2_conv_w": (3, D_FF),
    "ffn2_conv_b": (1, D_FF), "rw_mu": (1, 896), "rw_w0": (1, 256), "rw_a0": (1, 256), "rw_k_k": (1, 256),
    "rw_k_a": (1, 256), "rw_r_k": (1, 256), "rw_lnx_w": (1, 256), "rw_lnx_b": (1, 256), "nsa_gain": (1, 384),
    "moba_gain": (1, 384), "c": (2, D),
}
COL_AT = {}
at = 0
for name, (rows, length) in COLS.items():
    COL_AT[name] = at
    at += rows * length // P
N_COLS = at


def constants():
    s, t = np.meshgrid(np.arange(P), np.arange(P), indexing="ij")
    out = {
        "ident": s == t, "ones": s >= 0, "head_ones": s // HD == t // HD, "until": s <= t, "since": s >= t,
        "neg_until": np.where(s <= t, 0, NEG), "neg_since": np.where(s >= t, 0, NEG),
    }
    for m in LEVELS:
        lr = (s // (2 * m) == t // (2 * m)) & (s % (2 * m) < m) & (t % (2 * m) >= m)
        out[f"left_right_{m}"], out[f"right_left_{m}"] = lr, lr.T
    s, t = np.meshgrid(np.arange(P) % RW_C, np.arange(RW_C), indexing="ij")
    out["rw_masks"] = np.concatenate([s < t, s <= t], axis=1)

    def below(m, a, b):
        return (a // (2 * m) == b // (2 * m)) & (a % (2 * m) >= m) & (b % (2 * m) < m)

    for m in (1, 4, 16):
        out[f"rw_level_{m}_{2 * m}"] = np.concatenate([below(m, s, t), below(2 * m, s, t)], axis=1)
        out[f"rw_levelT_{m}_{2 * m}"] = np.concatenate([below(m, t, s), below(2 * m, t, s)], axis=1)
    out["rw_eye"] = np.concatenate([s == t, s > t], axis=1)
    tok = np.arange(P)[:, None, None] + P * np.arange(TT)[None, :, None]
    seen = CMP_STRIDE * np.arange(N_CMP + 1)[None, None, :] + CMP_LEN - 1 <= tok
    seen[:, :, N_CMP:] = False
    out["cmp_mask"] = np.where(seen, 0, NEG).reshape(P, P)
    out["cmp_valid"] = np.broadcast_to(seen.any(axis=2, keepdims=True), seen.shape).reshape(P, P)
    return np.stack([out[n].astype(np.float32) for n in CONST], axis=1)


def columns(arrays):
    out = []
    for name, (rows, length) in COLS.items():
        a = np.reshape(arrays[name], (rows, length // P, P))
        out.append(np.transpose(a, (2, 1, 0)).reshape(P, -1))
    return np.ascontiguousarray(np.concatenate(out, axis=1))


class Core:

    def __init__(self, nc, ctx):
        self.nc = nc
        self.stages = self.rooms = 0
        self.banks = [ctx.enter_context(nc.psum_tensor(f"bank{i}", [P, SEQ], F32)) for i in range(8)]
        self.const_sb = ctx.enter_context(nc.sbuf_tensor("const_sb", [P, ALWAYS, P], F32))
        self.some = {}
        self.cols_sb = ctx.enter_context(nc.sbuf_tensor("cols_sb", [P, N_COLS], F32))

    def const(self, name):
        return self.const_sb[:, CONST_AT[name], :] if CONST_AT[name] < ALWAYS else self.some[name]

    @contextmanager
    def more_constants(self, names, source):
        first = CONST_AT[names[0]]
        with self.room(**{f"const_{names[0]}": [P, len(names), P]}) as (buf,):
            load(self, [(buf[:], source[:, first:first + len(names), :])])
            self.some = {name: buf[:, n, :] for n, name in enumerate(names)}
            yield

    def col(self, name, tile, row=0):
        start = COL_AT[name] + tile * COLS[name][0] + row
        return self.cols_sb[:, bass.ds(start, 1)]

    @contextmanager
    def room(self, **shapes):
        self.rooms += 1
        n = self.rooms
        with ExitStack() as ctx:
            yield [ctx.enter_context(self.nc.sbuf_tensor(f"{name}_{n}", shape, F32)) for name, shape in shapes.items()]

    @contextmanager
    def split_room(self, **shapes):
        self.rooms += 1
        n = self.rooms
        with ExitStack() as ctx:
            yield [tuple(ctx.enter_context(self.nc.sbuf_tensor(f"{name}_{part}_{n}", shape, F32R))
                         for part in ("high", "low")) for name, shape in shapes.items()]

    @contextmanager
    def stage(self, *names):
        self.stages += 1
        with self.nc.cleanup_on_exit():
            sems = [self.nc.alloc_semaphore(f"{n}_{self.stages}") for n in names]
            with self.nc.Block() as block:
                yield [block, *sems]


def three_passes(pe, bank, weights, acts, start, stop):
    pe.matmul(bank, weights[0], acts[0], start=start, stop=False)
    pe.matmul(bank, weights[0], acts[1], start=False, stop=False)
    return pe.matmul(bank, weights[1], acts[0], start=False, stop=stop)


def split_half(dve, slab, high, low, half, count, high_done, low_done):
    kt = slab.shape[1]
    some = slice(0, kt // 2) if half == 0 else slice(kt // 2, kt)
    dve.tensor_copy(high[:, some], slab[:, some]).then_inc(high_done, 1)
    dve.wait_ge(high_done, count + 1)
    dve.tensor_tensor(low[:, some], slab[:, some], high[:, some].bitcast(F32), ALU.subtract).then_inc(low_done, 1)


def gemm(core, name, weights, acts, spans, out, tiles, unroll, bias=None, func=ACT.Identity, more=None,
         at=None, extra=(), dve_behind=None, act_behind=None):
    kt = weights.shape[0] // P
    w = weights.rearrange("(k p) f -> p k f", p=P)
    steps = tiles // unroll
    slots = 2 if unroll % 2 == 0 or steps == 1 else unroll
    rings = min(unroll, 4) if steps == 1 else unroll
    assert steps * unroll == tiles and unroll * len(spans) <= 8
    names = [f"slab_in{u}" for u in range(rings)] + ["high_done", "low_done", "tile_done", "banks_free", "slots_refilled"]
    at = at or (lambda tile: tile * P)
    with core.room(**{f"{name}_ring": [P, rings, kt, P]}) as (ring,), \
            core.split_room(**{f"{name}_w": [P, slots, kt, P]}) as ((high, low),), core.stage(*names, *extra) as (block, *sems):
        slab_in, (high_done, low_done, tile_done, banks_free, slots_refilled, *extra) = sems[:rings], sems[rings:]

        def bank(u, n):
            return core.banks[u * len(spans) + n][:, 0:spans[n][1]]

        def taken(k, start, size):
            source, at = (more, k - DT) if more and k >= DT else (acts, k)
            return [part[:, at, start:start + size] for part in source]

        @block.sync
        def _(sp):
            for u in range(unroll):
                if u >= rings:
                    sp.wait_ge(low_done, 2 * (u - rings + 1))
                sp.dma_start(ring[:, u % rings], w[:, :, at(u):at(u) + P]).then_inc(slab_in[u % rings], 16)
            if steps > 1:
                with sp.Fori(1, steps) as i:
                    for u in range(unroll):
                        feature = sp.snap(at(i * unroll + u))
                        sp.wait_ge(low_done, 2 * ((i - 1) * unroll + u + 1))
                        sp.sem_inc(slots_refilled, 1)
                        sp.dma_start(ring[:, u], w[:, :, bass.ds(feature, P)]).then_inc(slab_in[u], 16)

        @block.vector
        def _(dve):
            def step(i, behind):
                for u in range(unroll):
                    dve.wait_ge(slab_in[u % rings], (i + 1 + u // rings) * 16)
                    dve.wait_ge(tile_done, i * unroll + u + 1)
                    for half in range(2):
                        split_half(dve, ring[:, u % rings], high[:, u % slots], low[:, u % slots], half,
                                   2 * (i * unroll + u) + half, high_done, low_done)
                    if behind:
                        dve_behind(dve, (i - 1) * unroll + u, banks_free, *extra)

            if dve_behind is None:
                with dve.Fori(0, steps) as i:
                    step(i, False)
            else:
                step(0, False)
                with dve.Fori(1, steps) as i:
                    step(i, True)
                for u in range(unroll):
                    dve_behind(dve, (steps - 1) * unroll + u, banks_free, *extra)

        @block.tensor
        def _(pe):
            pe.sem_inc(tile_done, slots)
            with pe.Fori(0, steps) as i:
                for u in range(unroll):
                    pe.wait_ge(banks_free, i * unroll + u + 1)
                    for n, (start, size) in enumerate(spans):
                        for k in range(kt):
                            if n == 0 and k in (0, kt // 2):
                                pe.wait_ge(low_done, 2 * (i * unroll + u) + (k > 0) + 1)
                            mm = three_passes(pe, bank(u, n), [part[:, u % slots, k, :] for part in (high, low)],
                                              taken(k, start, size), k == 0, k == kt - 1)
                    mm.then_inc(tile_done, 1)

        @block.scalar
        def _(act):
            act.sem_inc(banks_free, unroll)

            def step(i, behind):
                for u in range(unroll):
                    if behind:
                        act_behind(act, (i - 1) * unroll + u, *extra)
                    act.wait_ge(tile_done, i * unroll + u + 1 + slots)
                    tile = i * unroll + u
                    for n in range(len(spans)):
                        b = bias(tile) if bias else 0.0
                        done = act.activation(out(tile, n), bank(u, n), func, bias=b)
                    done.then_inc(banks_free, 1)

            if act_behind is None:
                with act.Fori(0, steps) as i:
                    step(i, False)
            else:
                step(0, False)
                with act.Fori(1, steps) as i:
                    step(i, True)
                for u in range(unroll):
                    act_behind(act, (steps - 1) * unroll + u, *extra)


def gemm_tokens(core, name, weights, acts, tiles, out, slabs):
    w = weights if len(weights.shape) == 3 else weights.rearrange("(k p) f -> p k f", p=P)
    kt = w.shape[1]
    slots = min(len(slabs), 2)
    most = max(width for _, width in slabs)
    with core.room(**{f"{name}_ring": [P, slots, kt, most]}) as (ring,), \
            core.split_room(**{f"{name}_w": [P, slots, kt, most]}) as ((high, low),), \
            core.stage("slab_in0", "slab_in1", "high_done", "low_done", "tile_done", "banks_free") as (
                block, slab_in0, slab_in1, high_done, low_done, tile_done, banks_free):
        slab_in = [slab_in0, slab_in1]

        @block.sync
        def _(sp):
            for s, (start, width) in enumerate(slabs):
                if s >= 2:
                    sp.wait_ge(low_done, 2 * (s - 1))
                sp.dma_start(ring[:, s % 2, :, 0:width], w[:, :, start:start + width]).then_inc(slab_in[s % 2], 16)

        @block.vector
        def _(dve):
            for s, (start, width) in enumerate(slabs):
                dve.wait_ge(slab_in[s % 2], 16 * (s // 2 + 1))
                if s >= 2:
                    dve.wait_ge(tile_done, (s - 1) * tiles)
                for half in range(2):
                    split_half(dve, *(b[:, s % 2, :, 0:width] for b in (ring, high, low)), half, 2 * s + half, high_done, low_done)

        @block.tensor
        def _(pe):
            for s, (start, width) in enumerate(slabs):
                for t in range(tiles):
                    n = s * tiles + t
                    if n >= 8:
                        pe.wait_ge(banks_free, n - 7)
                    for k in range(kt):
                        if t == 0 and k in (0, kt // 2):
                            pe.wait_ge(low_done, 2 * s + (k > 0) + 1)
                        bank = core.banks[n % 8][:, 0:width]
                        pe.matmul(bank, acts[0][:, k, t * P:(t + 1) * P], high[:, s % 2, k, 0:width], start=(k == 0), stop=False)
                        pe.matmul(bank, acts[0][:, k, t * P:(t + 1) * P], low[:, s % 2, k, 0:width], start=False, stop=False)
                        mm = pe.matmul(bank, acts[1][:, k, t * P:(t + 1) * P], high[:, s % 2, k, 0:width], start=False,
                                       stop=(k == kt - 1))
                    mm.then_inc(tile_done, 1)

        @block.scalar
        def _(act):
            for n in range(len(slabs) * tiles):
                width = slabs[n // tiles][1]
                act.wait_ge(tile_done, n + 1)
                act.activation(out(n % tiles, n // tiles), core.banks[n % 8][:, 0:width], ACT.Identity)\
                   .then_inc(banks_free, 1)


def split(core, parts, modulation=None):
    with core.stage("modulated", "high_done", "low_done") as (block, modulated, high_done, low_done):
        tiles = [(src[:, k, :], high[:, k, :], low[:, k, :], k, shift_scale)
                 for (src, (high, low)), shift_scale in zip(parts, modulation or [None] * len(parts))
                 for k in range(src.shape[1])]

        @block.vector
        def _(dve):
            def take_low(n):
                src, high, low, _, _ = tiles[n]
                dve.wait_ge(high_done, n + 1)
                dve.tensor_tensor(low, src, high.bitcast(F32), ALU.subtract).then_inc(low_done, 1)

            for n, (src, _, _, k, shift_scale) in enumerate(tiles):
                if shift_scale:
                    shift, scale = shift_scale
                    dve.tensor_scalar(src, src, scale(k), shift(k), ALU.mult, ALU.add).then_inc(modulated, 1)
                if n >= 2 and n % 2 == 0:
                    take_low(n - 2)
            take_low(len(tiles) - 2)

        @block.scalar
        def _(act):
            for n, (src, high, _, _, shift_scale) in enumerate(tiles):
                if shift_scale:
                    act.wait_ge(modulated, n + 1)
                act.activation(high, src, ACT.Copy).then_inc(high_done, 1)

        @block.gpsimd
        def _(pool):
            for n, (src, high, low, _, _) in enumerate(tiles):
                if n % 2 == 1:
                    pool.wait_ge(high_done, n + 1)
                    pool.tensor_tensor(low, src, high.bitcast(F32), ALU.subtract).then_inc(low_done, 1)


def modulate(core, x, shift, scale1, out):
    with core.stage("modulated") as (block, modulated):
        @block.vector
        def _(dve):
            for k in range(DT):
                dve.tensor_scalar(out[:, k, :], x[:, k, :], scale1(k), shift(k), ALU.mult, ALU.add).then_inc(modulated, 1)


def residual(core, x, y, gate):
    with core.stage("scaled") as (block, scaled):
        if gate is None:
            @block.vector
            def _(dve):
                for k in range(DT):
                    dve.tensor_tensor(x[:, k, :], x[:, k, :], y[:, k, :], ALU.add)
            return

        @block.scalar
        def _(act):
            for k in range(DT):
                act.activation(x[:, k, :], x[:, k, :], ACT.Identity, scale=ALPHA).then_inc(scaled, 1)

        @block.vector
        def _(dve):
            for k in range(DT):
                dve.wait_ge(scaled, k + 1)
                dve.scalar_tensor_tensor(out=x[:, k, :], in0=y[:, k, :], scalar=gate(k), in1=x[:, k, :],
                                         op0=ALU.mult, op1=ALU.add)


def norm(core, name, src, out, gain, bias=None, eps=EPS, center=True, func=ACT.Identity):
    total, squares = core.banks[0], core.banks[1]
    ones = core.const("ones")
    with core.room(**{f"{name}_sq": [P, DT, SEQ], f"{name}_mean": [P, SEQ], f"{name}_rstd": [P, SEQ]}) as (sq, mean, rstd), \
            core.stage("summed", "mean_done", "centered", "squared", "sq_summed", "var_done", "root_done", "inverse_done",
                       "scaled") as (block, summed, mean_done, centered, squared, sq_summed, var_done, root_done,
                                     inverse_done, scaled):
        @block.tensor
        def _(pe):
            if center:
                for k in range(DT):
                    mm = pe.matmul(total[:, :], ones, src[:, k, :], start=(k == 0), stop=(k == DT - 1))
                mm.then_inc(summed, 1)
            for k in range(DT):
                pe.wait_ge(squared, k + 1)
                mm = pe.matmul(squares[:, :], ones, sq[:, k, :], start=(k == 0), stop=(k == DT - 1))
            mm.then_inc(sq_summed, 1)

        @block.vector
        def _(dve):
            if center:
                dve.wait_ge(summed, 1)
                dve.tensor_scalar(mean[:, :], total[:, :], 1.0 / D, None, ALU.mult).then_inc(mean_done, 1)
                dve.wait_ge(mean_done, 1)
                for k in range(DT):
                    dve.tensor_tensor(out[:, k, :], src[:, k, :], mean[:, :], ALU.subtract).then_inc(centered, 1)
            dve.wait_ge(sq_summed, 1)
            dve.tensor_scalar(rstd[:, :], squares[:, :], 1.0 / D, eps, ALU.mult, ALU.add).then_inc(var_done, 1)
            dve.wait_ge(root_done, 1)
            dve.reciprocal(rstd[:, :], rstd[:, :]).then_inc(inverse_done, 1)
            dve.wait_ge(inverse_done, 1)
            for k in range(DT):
                dve.scalar_tensor_tensor(out=out[:, k, :], in0=(out if center else src)[:, k, :], scalar=gain(k),
                                         in1=rstd[:, :], op0=ALU.mult, op1=ALU.mult).then_inc(scaled, 1)

        @block.scalar
        def _(act):
            for k in range(DT):
                if center:
                    act.wait_ge(centered, k + 1)
                act.activation(sq[:, k, :], (out if center else src)[:, k, :], ACT.Square).then_inc(squared, 1)
            act.wait_ge(var_done, 1)
            act.activation(rstd[:, :], rstd[:, :], ACT.Sqrt).then_inc(root_done, 1)
            if bias is not None:
                for k in range(DT):
                    act.wait_ge(scaled, k + 1)
                    act.activation(out[:, k, :], out[:, k, :], func, bias=bias(k))


@contextmanager
def glu_ffn(core, name, w_up, gate_at, value_at, w_down, fill_x, y_of, width, interior, taps, conv_w, conv_b, func):
    slots = 4
    with core.split_room(**{f"{name}_h": [P, FT, SEQ]}) as (h,):
        w = w_up.rearrange("(k p) f -> p k f", p=P)
        with core.split_room(**{f"{name}_x": [P, DT, SEQ]}) as (x,):
            fill_x(x)
            with core.room(**{f"{name}_ring": [P, 2, DT, P], f"{name}_pad": [P, 2, width], f"{name}_acc": [P, 2, SEQ],
                              f"{name}_val": [P, 2, SEQ]}) as (ring, pad, acc, val), \
                    core.split_room(**{f"{name}_w": [P, slots, DT, P]}) as ((high, low),), \
                    core.stage("slab_in0", "slab_in1", "high_done", "low_done", "tile_done", "banks_free", "tapped0",
                               "tapped1", "active", "products", "h_high", "h_low", "slots_refilled") as (
                        block, slab_in0, slab_in1, high_done, low_done, tile_done, banks_free, tapped0, tapped1, active,
                        products, h_high, h_low, slots_refilled):
                slab_in = [slab_in0, slab_in1]
                tapped = [tapped0, tapped1]
                steps = FT // 2

                def slab_at(i, u):
                    return (2 * i + u % 2) * P + (gate_at, value_at)[u // 2]

                @block.sync
                def _(sp):
                    for u in range(2):
                        sp.dma_start(ring[:, u], w[:, :, bass.ds(slab_at(0, u), P)]).then_inc(slab_in[u], 16)
                    for u in range(2, 4):
                        sp.wait_ge(low_done, u - 1)
                        sp.dma_start(ring[:, u % 2], w[:, :, bass.ds(slab_at(0, u), P)]).then_inc(slab_in[u % 2], 16)
                    with sp.Fori(1, steps) as i:
                        for u in range(4):
                            feature = sp.snap(slab_at(i, u))
                            sp.wait_ge(low_done, 4 * i + u - 1)
                            sp.sem_inc(slots_refilled, 1)
                            sp.dma_start(ring[:, u % 2], w[:, :, bass.ds(feature, P)]).then_inc(slab_in[u % 2], 16)

                @block.gpsimd
                def _(pool):
                    with pool.Fori(0, steps) as i:
                        for u in range(4):
                            pool.wait_ge(high_done, 4 * i + u + 1)
                            pool.tensor_tensor(low[:, u], ring[:, u % 2], high[:, u].bitcast(F32), ALU.subtract)\
                                .then_inc(low_done, 1)

                @block.tensor
                def _(pe):
                    with pe.Fori(0, steps) as i:
                        for u in range(4):
                            pe.wait_ge(low_done, 4 * i + u + 1)
                            pe.wait_ge(banks_free, 4 * i + u + 1)
                            for k in range(DT):
                                mm = three_passes(pe, core.banks[u][:, :], (high[:, u, k, :], low[:, u, k, :]),
                                                  (x[0][:, k, :], x[1][:, k, :]), k == 0, k == DT - 1)
                            mm.then_inc(tile_done, 1)

                @block.scalar
                def _(act):
                    def take_high(i, u):
                        act.wait_ge(slab_in[u % 2], 16 * (2 * i + u // 2 + 1))
                        act.activation(high[:, u], ring[:, u % 2], ACT.Copy).then_inc(high_done, 1)

                    def step(i, more):
                        for u in range(4):
                            act.wait_ge(tile_done, 4 * i + u + 1)
                            j = u % 2
                            if u < 2:
                                act.wait_ge(tapped[j], len(taps) * i + 1)
                                src, dst = core.banks[u][:, :], interior(pad[:, j, :])
                                if len(dst.shape) == 3:
                                    src = src.rearrange("p (a b) -> p a b", b=dst.shape[2])
                            else:
                                act.wait_ge(products, 2 * i + j + 1)
                                src, dst = core.banks[u][:, :], val[:, j, :]
                            act.activation(dst, src, ACT.Identity).then_inc(banks_free, 1)
                            if more:
                                take_high(i + 1, u)
                        for j in range(2):
                            act.wait_ge(tapped[j], len(taps) * (i + 1) + 1)
                            act.activation(acc[:, j, :], acc[:, j, :], func, bias=conv_b(2 * i + j)).then_inc(active, 1)
                        for j in range(2):
                            act.wait_ge(products, 2 + 2 * i + j + 1)
                            act.activation(h[0][:, bass.ds(2 * i + j, 1), :], acc[:, j:j + 1, :], ACT.Copy)\
                               .then_inc(h_high, 1)

                    act.sem_inc(banks_free, 4)
                    for u in range(4):
                        take_high(0, u)
                    with act.Fori(0, steps - 1) as i:
                        step(i, True)
                    step(steps - 1, False)

                @block.vector
                def _(dve):
                    for j in range(2):
                        dve.memset(pad[:, j, :], 0.0).then_inc(tapped[j], 1)
                    dve.sem_inc(products, 2)
                    dve.sem_inc(h_low, 2)
                    with dve.Fori(0, steps) as i:
                        for n, tap in enumerate(taps):
                            for j in range(2):
                                if n == 0:
                                    dve.wait_ge(banks_free, 4 + 4 * i + j + 1)
                                    dve.wait_ge(h_low, 2 * i + j + 1)
                                src = tap(pad[:, j, :])
                                dst = acc[:, j, :]
                                if len(src.shape) == 3:
                                    dst = dst.rearrange("p (a b) -> p a b", b=src.shape[2])
                                dve.wait_ge(tapped[j], len(taps) * i + n + 1)
                                if n == 0:
                                    dve.tensor_scalar(dst, src, conv_w(2 * i + j, n), None, ALU.mult)\
                                       .then_inc(tapped[j], 1)
                                else:
                                    dve.scalar_tensor_tensor(out=dst, in0=src, scalar=conv_w(2 * i + j, n), in1=dst,
                                                             op0=ALU.mult, op1=ALU.add).then_inc(tapped[j], 1)
                        for j in range(2):
                            dve.wait_ge(active, 2 * i + j + 1)
                            dve.wait_ge(banks_free, 4 + 4 * i + j + 3)
                            dve.tensor_tensor(acc[:, j, :], acc[:, j, :], val[:, j, :], ALU.mult).then_inc(products, 1)
                        for j in range(2):
                            dve.wait_ge(h_high, 2 * i + j + 1)
                            tile = bass.ds(2 * i + j, 1)
                            dve.tensor_tensor(h[1][:, tile, :], acc[:, j:j + 1, :], h[0][:, tile, :].bitcast(F32),
                                              ALU.subtract).then_inc(h_low, 1)

        with y_of() as (y,):
            gemm(core, f"{name}_down", w_down, h, [(0, SEQ)], lambda tile, n: y[:, bass.ds(tile, 1), :], DT, 2)
            yield y


GRID_PAD = (ROWS + 2) * (GRID_W + 2)


def grid_window(r, c):
    return lambda b: b.rearrange("p (a b) -> p a b", b=GRID_W + 2)[:, r:r + ROWS, c:c + GRID_W]


GRID_TAPS = [grid_window(r, c) for r in range(3) for c in range(3)]


def conformer(core, w1, w2, x, y):
    half = CONF_K // 2
    pe_taps = 11
    early_taps = 5
    dve_taps = CONF_K - pe_taps

    def tap(dve, tile, n, tapped, before):
        here = bass.ds(tile, 1)
        src, dst = pad[:, here, n:n + SEQ], conv[:, here, :]
        weight = core.col("conf_dw_w", tile, n)
        if n == 0:
            dve.tensor_scalar(dst, src, weight, core.col("conf_dw_b", tile), ALU.mult, ALU.add).then_inc(tapped, 1)
        else:
            if before is not None:
                dve.wait_ge(tapped, before)
            dve.scalar_tensor_tensor(out=dst, in0=src, scalar=weight, in1=dst, op0=ALU.mult, op1=ALU.add)\
               .then_inc(tapped, 1)

    with core.room(conf_pad=[P, DT, SEQ + 2 * half], conf_u=[P, DT, SEQ]) as (pad, conv):
        with core.stage("border") as (block, border):
            @block.gpsimd
            def _(pool):
                for at in (0, half + SEQ):
                    pool.memset(pad[:, :, at:at + half], 0.0).then_inc(border, 1)
        with core.room(conf_gate=[P, DT, SEQ]) as (gate,):
            gemm(core, "conf_gate", w1[:, D:], x, [(0, SEQ)], lambda tile, n: gate[:, bass.ds(tile, 1), :], DT, 4,
                 bias=lambda tile: core.col("conf_b1", tile, 1), func=ACT.Sigmoid)

            def gate_and_tap(dve, tile, out_done, gated, tapped):
                here = bass.ds(tile, 1)
                dve.wait_ge(out_done, tile + 1 + 4)
                inner = pad[:, here, half:half + SEQ]
                dve.tensor_tensor(inner, inner, gate[:, here, :], ALU.mult).then_inc(gated, 1)
                dve.wait_ge(gated, tile + 1)
                for n in range(early_taps):
                    tap(dve, tile, n, tapped, tile * early_taps + n)

            gemm(core, "conf_val", w1[:, 0:D], x, [(0, SEQ)], lambda tile, n: pad[:, bass.ds(tile, 1), half:half + SEQ],
                 DT, 4, bias=lambda tile: core.col("conf_b1", tile), extra=("gated", "tapped"), dve_behind=gate_and_tap)
        with core.room(conf_diag=[P, 2, pe_taps, P]) as (diag,), \
                core.stage("tapped0", "tapped1", "diag_done", "pe_tapped", "tile_added") as (
                    block, tapped0, tapped1, diag_done, pe_tapped, tile_added):
            tapped = [tapped0, tapped1]
            late_taps = dve_taps - early_taps

            @block.vector
            def _(dve):
                dve.sem_inc(tile_added, 2)
                with dve.Fori(0, DT // 2) as i:
                    for n in range(late_taps):
                        for j in range(2):
                            tap(dve, 2 * i + j, early_taps + n, tapped[j], late_taps * i + n if n else None)
                    for j in range(2):
                        tile = bass.ds(2 * i + j, 1)
                        dve.wait_ge(tapped[j], late_taps * (i + 1))
                        dve.wait_ge(pe_tapped, 2 * i + j + 1)
                        dve.tensor_tensor(conv[:, tile, :], conv[:, tile, :], core.banks[j][:, :].unsqueeze(1), ALU.add)\
                           .then_inc(tile_added, 1)

            @block.scalar
            def _(act):
                with act.Fori(0, DT // 2) as i:
                    for j in range(2):
                        act.wait_ge(tile_added, 2 * i + j + 1)
                        for n in range(pe_taps):
                            done = act.activation(diag[:, j, n, :], core.const("ident"), ACT.Copy,
                                                  scale=core.col("conf_dw_w", 2 * i + j, dve_taps + n))
                        done.then_inc(diag_done, 1)

            @block.tensor
            def _(pe):
                with pe.Fori(0, DT // 2) as i:
                    for j in range(2):
                        pe.wait_ge(diag_done, 2 * i + j + 1)
                        for n in range(pe_taps):
                            at = dve_taps + n
                            mm = pe.matmul(core.banks[j][:, :], diag[:, j, n, :],
                                           pad[:, bass.ds(2 * i + j, 1), at:at + SEQ].rearrange("p a t -> p (a t)"),
                                           start=(n == 0), stop=(n == pe_taps - 1))
                        mm.then_inc(pe_tapped, 1)
        norm(core, "conf_ln", conv, conv, lambda k: core.col("conf_ln_g", k), lambda k: core.col("conf_ln_b", k),
             func=ACT.Silu)
        with core.split_room(conf_in=[P, DT, SEQ]) as (parts,):
            split(core, [(conv, parts)])
            gemm(core, "conf_out", w2, parts, [(0, SEQ)], lambda tile, n: y[:, bass.ds(tile, 1), :], DT, 4,
                 bias=lambda tile: core.col("conf_b2", tile))


def spread(ap, axis, count):
    ap = ap.unsqueeze(axis)
    shape = list(ap.shape)
    shape[axis] = count
    return ap.broadcast_to(shape)


LAT_PAD = SEQ + SSD_K - 1
CTX_PAD = CTX + SSD_K - 1
SPANS = [(0, SEQ), (SEQ, CTX)]
XS_T, B_T, C_T = 0, SSD_IN // P, SSD_IN // P + SSD_G
XBC_T = SSD_XBC // P


def ssd_inputs(core, w_in, h, xbc):
    half = SSD_K // 2
    with core.room(xbc_pad=[P, XBC_T, LAT_PAD + CTX_PAD]) as (pad,):
        def inner(tile, n):
            at, size = ((half, SEQ), (LAT_PAD + half, CTX))[n]
            return pad[:, bass.ds(tile, 1), at:at + size]

        with core.stage("border") as (block, border):
            @block.gpsimd
            def _(pool):
                for at, size in ((0, half), (LAT_PAD - half, 2 * half), (LAT_PAD + CTX_PAD - half, half)):
                    pool.memset(pad[:, :, at:at + size], 0.0).then_inc(border, 1)

        def convolve(dve, tile, out_done, lat_tapped, ctx_tapped):
            dve.wait_ge(out_done, tile + 1 + 4)
            for n in range(SSD_K):
                for tapped, at, start, size in ((lat_tapped, 0, 0, SEQ), (ctx_tapped, LAT_PAD, SEQ, CTX)):
                    src = pad[:, bass.ds(tile, 1), at + n:at + n + size]
                    dst = xbc[:, bass.ds(tile, 1), start:start + size]
                    tap = core.col("ssd_conv_w", tile, n)
                    if n == 0:
                        dve.tensor_scalar(dst, src, tap, None, ALU.mult).then_inc(tapped, 1)
                    else:
                        dve.wait_ge(tapped, tile * SSD_K + n)
                        dve.scalar_tensor_tensor(out=dst, in0=src, scalar=tap, in1=dst, op0=ALU.mult, op1=ALU.add)\
                           .then_inc(tapped, 1)

        def activate(act, tile, lat_tapped, ctx_tapped):
            act.wait_ge(lat_tapped, (tile + 1) * SSD_K)
            act.wait_ge(ctx_tapped, (tile + 1) * SSD_K)
            act.activation(xbc[:, bass.ds(tile, 1), :], xbc[:, bass.ds(tile, 1), :], ACT.Silu,
                           bias=core.col("ssd_conv_b", tile))

        gemm(core, "xbc", w_in[:, MIX_AT["xbc"]:MIX_AT["dt"]], h, SPANS, inner, XBC_T, 4,
             extra=("lat_tapped", "ctx_tapped"), dve_behind=convolve, act_behind=activate)


def ssd_tokens(core, xbc, x_tok, b_tok):
    with core.stage("turned", "taken") as (block, turned, taken):
        jobs = [(t, j, x_tok[:, t, j * P:(j + 4) * P], range(j, j + 4)) for t in range(TOK // P) for j in (0, 4)]
        jobs += [(t, B_T, b_tok[:, t, :], range(B_T, B_T + 2)) for t in range(TOK // P)]

        @block.tensor
        def _(pe):
            for n, (t, _, _, tiles) in enumerate(jobs):
                if n >= 8:
                    pe.wait_ge(taken, n - 7)
                for m, j in enumerate(tiles):
                    mm = pe.transpose(core.banks[n % 8][:, m * P:(m + 1) * P], xbc[:, j, t * P:(t + 1) * P],
                                      core.const("ident"))
                mm.then_inc(turned, 1)

        @block.scalar
        def _(act):
            for n, (_, _, out, tiles) in enumerate(jobs):
                act.wait_ge(turned, n + 1)
                act.activation(out, core.banks[n % 8][:, 0:len(tiles) * P], ACT.Copy).then_inc(taken, 1)


def raw_steps(core, weights, h, dt):
    heads = 2 * SSD_HEADS
    tiles = TOK // P
    with core.room(dt_in=[P, DT, heads], dt_rows=[heads, TOK]) as (w, by_head), \
            core.split_room(dt_w=[P, DT, heads]) as ((high, low),), \
            core.stage("w_in", "high_done", "low_done", "made", "taken", "turned", "stored") as (
                block, w_in, high_done, low_done, made, taken, turned, stored):
        @block.sync
        def _(sp):
            sp.dma_start(w[:], weights).then_inc(w_in, 16)

        @block.vector
        def _(dve):
            dve.wait_ge(w_in, 16)
            for half in range(2):
                split_half(dve, w, high, low, half, half, high_done, low_done)
            dve.wait_ge(turned, 1)
            dve.tensor_copy(dt[:].rearrange("p t h -> p (t h)"), core.banks[2][:, 0:tiles * heads]).then_inc(stored, 1)

        @block.tensor
        def _(pe):
            pe.wait_ge(low_done, 2)
            for n, (start, size) in enumerate(SPANS):
                for k in range(DT):
                    mm = three_passes(pe, core.banks[n][0:heads, 0:size], (high[:, k, :], low[:, k, :]),
                                      [part[:, k, start:start + size] for part in h], k == 0, k == DT - 1)
                mm.then_inc(made, 1)
            pe.wait_ge(taken, len(SPANS))
            for t in range(tiles):
                mm = pe.transpose(core.banks[2][:, t * heads:(t + 1) * heads], by_head[:, t * P:(t + 1) * P],
                                  core.const("ident")[0:heads, 0:heads])
            mm.then_inc(turned, 1)

        @block.scalar
        def _(act):
            for n, (start, size) in enumerate(SPANS):
                act.wait_ge(made, n + 1)
                act.activation(by_head[:, start:start + size], core.banks[n][0:heads, 0:size], ACT.Copy).then_inc(taken, 1)


def step_sizes(core, dt, a, rows):
    tiles = TOK // P
    with core.room(dt_soft=[P, tiles, 32], a_exp=[P, 32]) as (soft, a_exp), \
            core.stage("biased", "folded", "exp_done", "soft_done", "dt_done", "a_exp_done") as (
                block, biased, folded, exp_done, soft_done, dt_done, a_exp_done):
        @block.vector
        def _(dve):
            dve.tensor_tensor(dt[:], dt[:], spread(rows[:, 0:32], 1, tiles), ALU.add).then_inc(biased, 1)
            dve.wait_ge(biased, 1)
            dve.scalar_tensor_tensor(out=soft[:], in0=dt[:], scalar=-1.0, in1=dt[:], op0=ALU.mult, op1=ALU.min)\
               .then_inc(folded, 1)
            dve.wait_ge(soft_done, 1)
            dve.scalar_tensor_tensor(out=dt[:], in0=dt[:], scalar=0.0, in1=soft[:], op0=ALU.max, op1=ALU.add)\
               .then_inc(dt_done, 1)
            dve.wait_ge(dt_done, 1)
            dve.wait_ge(a_exp_done, 1)
            dve.scalar_tensor_tensor(out=a[:], in0=dt[:], scalar=-1.0, in1=spread(a_exp[:, :], 1, tiles),
                                     op0=ALU.mult, op1=ALU.mult)

        @block.scalar
        def _(act):
            act.activation(a_exp[:, :], rows[:, 32:64], ACT.Exp).then_inc(a_exp_done, 1)
            act.wait_ge(folded, 1)
            act.activation(soft[:], soft[:], ACT.Exp).then_inc(exp_done, 1)
            act.wait_ge(exp_done, 1)
            act.activation(soft[:], soft[:], ACT.Ln, bias=1.0).then_inc(soft_done, 1)


def ssd_chunk(core, d, token, tile, output, xbc, x_tok, b_tok, dt, a, state, y, buf):
    b_st, c_st, bt_st, a_st, xdt, xdtd, acum, left, decay, cb, diff, m_buf, ce_buf = buf
    banks = core.banks
    until, neg = (core.const("until"), core.const("neg_until")) if d == 0 else (core.const("since"), core.const("neg_since"))
    heads = slice(d * SSD_HEADS, (d + 1) * SSD_HEADS)
    here = bass.ds(token, CHUNK)
    quads = SSD_HEADS // 4
    row_banks = (2, 3, 6, 7)
    names = ["b_staged", "a_staged", "x_scaled", "cols_done", "acum_done", "left_done", "decay_done", "x_decayed", "cb_done",
             "cb_taken", "acum_rows", "diff_done", "m_exp", "ce_exp", "m_done", "ce_done", "y_done", "y_added",
             "states_made", "state_faded"]
    with core.stage(*names) as (block, b_staged, a_staged, x_scaled, cols_done, acum_done, left_done, decay_done, x_decayed,
                                cb_done, cb_taken, acum_rows, diff_done, m_exp, ce_exp, m_done, ce_done, y_done, y_added,
                                states_made, state_faded):
        def make_states(pe):
            pe.wait_ge(x_decayed, 1)
            for g in range(SSD_G):
                mm = pe.matmul(banks[6 + g][:, :], bt_st[:, g * P:(g + 1) * P],
                               xdtd[:, 8 * g:8 * g + 8, :].rearrange("p h x -> p (h x)"), start=True, stop=True)
            mm.then_inc(states_made, 1)

        @block.gpsimd
        def _(pool):
            pool.wait_ge(x_scaled, 1)
            pool.wait_ge(decay_done, 1)
            pool.tensor_tensor(xdtd[:], xdt[:], spread(decay[:, 0:16], 2, SSD_P), ALU.mult).then_inc(x_decayed, 1)
            if output:
                for q in range(quads):
                    pool.wait_ge(ce_exp, q + 1)
                    if q == 0:
                        pool.wait_ge(b_staged, 3)
                    pool.tensor_tensor(ce_buf[:, q % 2], ce_buf[:, q % 2], spread(c_st[:, q // 2, :], 1, 4), ALU.mult)\
                        .then_inc(ce_done, 1)

        @block.tensor
        def _(pe):
            pe.wait_ge(a_staged, 1)
            pe.matmul(banks[0][:, 0:16], until, a_st[:, :], start=True, stop=True)
            pe.matmul(banks[0][:, 16:32], core.const("ones"), a_st[:, :], start=True, stop=True).then_inc(cols_done, 1)
            if output:
                pe.wait_ge(b_staged, 3)
                for g in range(SSD_G):
                    mm = pe.matmul(banks[1][:, g * P:(g + 1) * P], b_st[:, g, :], c_st[:, g, :], start=True, stop=True)
                mm.then_inc(cb_done, 1)

                for q in range(quads):
                    for n in range(4):
                        h = 4 * q + n
                        mm = pe.matmul(banks[row_banks[q]][:, n * P:(n + 1) * P], a_st[:, h:h + 1].broadcast_to([P, P]),
                                       until, start=True, stop=True)
                    mm.then_inc(acum_rows, 1)
                for q in range(quads):
                    if q == 0:
                        pe.wait_ge(x_scaled, 1)
                    if q == quads - 1:
                        pe.wait_ge(diff_done, 4 * quads)
                        pe.wait_ge(ce_exp, quads)
                        make_states(pe)
                    pe.wait_ge(m_done, q + 1)
                    pe.wait_ge(ce_done, q + 1)
                    if q >= 2:
                        pe.wait_ge(y_added, q - 1)
                    for n in range(4):
                        h = 4 * q + n
                        out = banks[4 + q % 2][64 * (n % 2):64 * (n % 2) + 64, (n // 2) * P:(n // 2 + 1) * P]
                        pe.matmul(out, xdt[:, h, :], m_buf[:, q % 2, n, :], start=True, stop=False)
                        mm = pe.matmul(out, state[:, h, :], ce_buf[:, q % 2, n, :], start=False, stop=True)
                    mm.then_inc(y_done, 1)
            else:
                pe.wait_ge(b_staged, 3)
                make_states(pe)

        @block.scalar
        def _(act):
            act.activation(b_st[:], xbc[:, B_T:B_T + 2, here], ACT.Identity).then_inc(b_staged, 1)
            act.activation(c_st[:], xbc[:, C_T:C_T + 2, here], ACT.Identity).then_inc(b_staged, 1)
            act.activation(bt_st[:].rearrange("p (a n) -> p a n", a=1), b_tok[:, bass.ds(tile, 1), :], ACT.Identity)\
               .then_inc(b_staged, 1)
            act.wait_ge(left_done, 1)
            act.activation(decay[:, :], left[:, :], ACT.Exp).then_inc(decay_done, 1)
            if output:
                for q in range(quads):
                    act.wait_ge(diff_done, 4 * (q + 1))
                    if q >= 2:
                        act.wait_ge(y_done, q - 1)
                    act.activation(m_buf[:, q % 2], diff[:, q % 2], ACT.Exp).then_inc(m_exp, 1)
                    act.activation(ce_buf[:, q % 2].rearrange("p n t -> p (n t)"), banks[row_banks[q]][:, :], ACT.Exp)\
                       .then_inc(ce_exp, 1)

        @block.vector
        def _(dve):
            dve.tensor_copy(a_st[:, :].unsqueeze(1), a[:, bass.ds(tile, 1), heads]).then_inc(a_staged, 1)
            x3 = x_tok[:, bass.ds(tile, 1), :].rearrange("p a (h x) -> p (a h) x", x=SSD_P)
            dt_here = dt[:, bass.ds(tile, 1), heads].rearrange("p a h -> p (a h)")
            dve.tensor_tensor(xdt[:], x3, spread(dt_here, 2, SSD_P), ALU.mult).then_inc(x_scaled, 1)
            dve.wait_ge(cols_done, 1)
            dve.tensor_copy(acum[:, :], banks[0][:, 0:16]).then_inc(acum_done, 1)
            dve.tensor_copy(left[:, 16:32], banks[0][:, 16:32]).then_inc(acum_done, 1)
            dve.wait_ge(acum_done, 2)
            dve.tensor_tensor(left[:, 0:16], left[:, 16:32], acum[:, :], ALU.subtract).then_inc(left_done, 1)
            if output:
                dve.wait_ge(cb_done, 1)
                dve.tensor_copy(cb[:].rearrange("p g t -> p (g t)"), banks[1][:, 0:2 * P]).then_inc(cb_taken, 1)

                def add_y(q):
                    dve.wait_ge(y_done, q + 1)
                    out = y[:, 2 * q:2 * q + 2, here]
                    dve.tensor_tensor(out, out, banks[4 + q % 2][:, 0:2 * P].rearrange("p (j t) -> p j t", j=2), ALU.add)\
                       .then_inc(y_added, 1)

                def differences(q):
                    dve.wait_ge(acum_rows, q + 1)
                    if q >= 2:
                        dve.wait_ge(m_exp, q - 1)
                    for n in range(4):
                        h = 4 * q + n
                        dve.scalar_tensor_tensor(out=diff[:, q % 2, n, :], in0=banks[row_banks[q]][:, n * P:(n + 1) * P],
                                                 scalar=acum[:, h:h + 1], in1=neg, op0=ALU.subtract, op1=ALU.add)\
                           .then_inc(diff_done, 1)

                differences(0)
                for q in range(quads):
                    if q + 1 < quads:
                        differences(q + 1)
                    dve.wait_ge(m_exp, q + 1)
                    if q == 0:
                        dve.wait_ge(cb_taken, 1)
                    dve.tensor_tensor(m_buf[:, q % 2], m_buf[:, q % 2], spread(cb[:, q // 2, :], 1, 4), ALU.mult)\
                       .then_inc(m_done, 1)
                    if q >= 2:
                        add_y(q - 2)
                add_y(quads - 2)
                add_y(quads - 1)
            dve.wait_ge(decay_done, 1)
            dve.wait_ge(states_made, 1)
            dve.tensor_tensor(state[:], state[:], spread(decay[:, 16:32], 2, SSD_P), ALU.mult).then_inc(state_faded, 1)
            dve.wait_ge(state_faded, 1)
            for g in range(SSD_G):
                dve.tensor_tensor(state[:, 8 * g:8 * g + 8, :].rearrange("p h x -> p (h x)"),
                                  state[:, 8 * g:8 * g + 8, :].rearrange("p h x -> p (h x)"), banks[6 + g][:, :], ALU.add)


def chunks_of(core, d, body):
    for first, count, output in ((SEQ // CHUNK, CTX // CHUNK, False), (0, SEQ // CHUNK, True)):
        with core.nc.Fori(0, count) as i:
            tile = i + first if d == 0 else i * -1 + (first + count - 1)
            body(tile * CHUNK, tile, output)


def ssd(core, w_in, w_dt, h, y, rows):
    tiles = TOK // P
    with core.room(xbc=[P, XBC_T, TOK]) as (xbc,):
        ssd_inputs(core, w_in, h, xbc)
        with core.room(x_tok=[P, tiles, SSD_IN], b_tok=[P, tiles, SSD_G * SSD_N], dt=[P, tiles, 32], a=[P, tiles, 32],
                       state=[P, SSD_HEADS, SSD_P], b_st=[P, SSD_G, P], c_st=[P, SSD_G, P], bt_st=[P, SSD_G * P],
                       a_st=[P, 16], xdt=[P, SSD_HEADS, SSD_P], xdtd=[P, SSD_HEADS, SSD_P], acum=[P, 16], left=[P, 32],
                       decay=[P, 32], cb=[P, SSD_G, P], diff=[P, 2, 4, P], m_buf=[P, 2, 4, P], ce_buf=[P, 2, 4, P]) as (
                x_tok, b_tok, dt, a, state, *buf):
            ssd_tokens(core, xbc, x_tok, b_tok)
            raw_steps(core, w_dt, h, dt)
            step_sizes(core, dt, a, rows)
            with core.stage("skipped") as (block, skipped):
                @block.vector
                def _(dve):
                    for j in range(DT):
                        dve.tensor_scalar(y[:, j, :], xbc[:, j, 0:SEQ], rows[:, 64 + j:65 + j], None, ALU.mult)
            for d in range(2):
                with core.stage("cleared") as (block, cleared):
                    @block.vector
                    def _(dve):
                        dve.memset(state[:], 0.0)
                chunks_of(core, d, lambda token, tile, output: ssd_chunk(
                    core, d, token, tile, output, xbc, x_tok, b_tok, dt, a, state, y, buf))


def gla_chunk(core, d, token, tile, output, q, f, v, state, o, buf):
    key, acum, q_st, v_st, q_in, k_out, att, *mix, fade = buf
    kt = k_out
    t1, lf = mix[0:2]
    ring = len(mix)
    banks = core.banks
    flat = lambda b: b[:].rearrange("p h t -> p (h t)")
    end = CHUNK - 1 if d == 0 else 0
    here = bass.ds(token, CHUNK)
    fh = f[:, :, here]
    levels = list(enumerate(LEVELS))
    names = ["folded", "exp_done", "ln_done", "lf_done", "key_arg", "key_done", "summed", "q_staged", "v_staged", "q_exp",
             "q_in_done", "left_done", "left_exp", "k_out_done", "fade_done", "diff_done", "level_exp", "mixed", "products",
             "merged", "diagonal", "att_done", "o_done", "o_added", "turned", "taken", "states_made"]

    def half(b, m, side):
        return flat(b).rearrange("p (b t) -> p b t", t=2 * m)[:, :, side * m:(side + 1) * m]

    with core.stage(*names) as (block, folded, exp_done, ln_done, lf_done, key_arg, key_done, summed, q_staged, v_staged,
                                q_exp, q_in_done, left_done, left_exp, k_out_done, fade_done, diff_done, level_exp, mixed,
                                products, merged, diagonal, att_done, o_done, o_added, turned, taken, states_made):
        @block.gpsimd
        def _(pool):
            if output:
                pool.tensor_copy(q_st[:], q[:, :, here]).then_inc(q_staged, 1)
            pool.tensor_copy(flat(v_st).unsqueeze(1), v[:, bass.ds(tile, 1), :]).then_inc(v_staged, 1)
            if output:
                pool.wait_ge(summed, HG_HEADS)
                for n, m in levels:
                    if n >= ring:
                        pool.wait_ge(products, 2 * (n - ring + 1))
                    left, right = half(acum, m, 0), half(acum, m, 1)
                    middle = left[:, :, m - 1] if d == 0 else right[:, :, 0]
                    middle = spread(middle, 2, m)
                    a, b = (left, right) if d == 0 else (right, left)
                    out_a, out_b = half(mix[n % ring], m, d), half(mix[n % ring], m, 1 - d)
                    pool.tensor_tensor(out_a, middle, a, ALU.subtract).then_inc(diff_done, 1)
                    pool.tensor_tensor(out_b, b, middle, ALU.subtract).then_inc(diff_done, 1)

        @block.scalar
        def _(act):
            act.wait_ge(folded, 1)
            act.activation(t1[:], t1[:], ACT.Exp).then_inc(exp_done, 1)
            act.wait_ge(exp_done, 1)
            act.activation(t1[:], t1[:], ACT.Ln, bias=1.0).then_inc(ln_done, 1)
            act.wait_ge(key_arg, 1)
            act.activation(key[:], key[:], ACT.Exp).then_inc(key_done, 1)
            act.wait_ge(summed, HG_HEADS)
            act.activation(fade[:, :], acum[:, :, end], ACT.Exp).then_inc(fade_done, 1)
            act.wait_ge(left_done, 1)
            act.activation(k_out[:], k_out[:], ACT.Exp).then_inc(left_exp, 1)

            def take_keys():
                for b in range(2):
                    act.wait_ge(turned, b + 1)
                    act.activation(kt[:, 4 * b:4 * b + 4, :].rearrange("p h t -> p (h t)"), banks[4 + b][:, :], ACT.Copy)\
                       .then_inc(taken, 1)

            if output:
                for n, m in levels:
                    act.wait_ge(diff_done, 2 * n + 2)
                    act.activation(mix[n % ring][:], mix[n % ring][:], ACT.Exp).then_inc(level_exp, 1)
                    if n == 1:
                        act.activation(q_in[:], acum[:], ACT.Exp).then_inc(q_exp, 1)
                    if n == 4:
                        take_keys()
            else:
                take_keys()

        @block.tensor
        def _(pe):
            def head_bank(first, h):
                return banks[first + h // 4][:, (h % 4) * P:(h % 4 + 1) * P]

            def turn_keys():
                pe.wait_ge(k_out_done, 1)
                for h in range(HG_HEADS):
                    mm = pe.transpose(head_bank(4, h), k_out[:, h, :], core.const("ident"))
                    if h % 4 == 3:
                        mm.then_inc(turned, 1)

            def make_states():
                pe.wait_ge(v_staged, 1)
                for h in range(HG_HEADS):
                    pe.wait_ge(taken, h // 4 + 1)
                    mm = pe.matmul(head_bank(4, h), kt[:, h, :], v_st[:, h, :], start=True, stop=True)
                    if h % 4 == 3:
                        mm.then_inc(states_made, 1)

            if output:
                pe.wait_ge(q_staged, 1)
                pe.wait_ge(key_done, 1)
                for h in range(HG_HEADS):
                    mm = pe.matmul(head_bank(4, h), key[:, h, :], q_st[:, h, :], start=True, stop=True)
                mm.then_inc(diagonal, 1)
                for n, m in levels:
                    if n == 2:
                        pe.wait_ge(att_done, 2)
                        turn_keys()
                    if n == 5:
                        pe.wait_ge(q_in_done, 1)
                        for h in range(HG_HEADS):
                            pe.matmul(head_bank(6, h), state[:, h, :], q_in[:, h, :], start=(h % 4 == 0), stop=False)
                    if n == 6:
                        make_states()
                    pe.wait_ge(mixed, 2 * n + 2)
                    if n >= 2:
                        pe.wait_ge(merged, 2 * (n - 1))
                    for h in range(HG_HEADS):
                        mm = pe.matmul(head_bank(2 * (n % 2), h), mix[n % ring][:, h, :], mix[n % ring][:, h, :],
                                       start=True, stop=True)
                        if h % 4 == 3:
                            mm.then_inc(products, 1)
                for h in range(HG_HEADS):
                    pe.wait_ge(merged, 2 * len(levels) - 1 + h // 4)
                    mm = pe.matmul(head_bank(6, h), v_st[:, h, :], att[:, h, :], start=False, stop=(h % 4 == 3))
                    if h % 4 == 3:
                        mm.then_inc(o_done, 1)
            else:
                turn_keys()
                make_states()

        @block.vector
        def _(dve):
            dve.scalar_tensor_tensor(out=t1[:], in0=fh, scalar=-1.0, in1=fh, op0=ALU.mult, op1=ALU.min).then_inc(folded, 1)
            dve.wait_ge(ln_done, 1)
            dve.scalar_tensor_tensor(out=lf[:], in0=fh, scalar=0.0, in1=t1[:], op0=ALU.min, op1=ALU.subtract)\
               .then_inc(lf_done, 1)
            dve.wait_ge(lf_done, 1)
            dve.tensor_tensor(key[:], lf[:], fh, ALU.subtract).then_inc(key_arg, 1)
            step = 1 if d == 0 else -1
            for h in range(HG_HEADS):
                dve.tensor_tensor_scan(acum[:, h, ::step], core.const("ones"), lf[:, h, ::step], 0.0, ALU.mult, ALU.add)\
                   .then_inc(summed, 1)
            dve.wait_ge(summed, HG_HEADS)
            dve.tensor_tensor(k_out[:], spread(acum[:, :, end], 2, CHUNK), acum[:], ALU.subtract).then_inc(left_done, 1)
            dve.wait_ge(left_exp, 1)
            dve.wait_ge(key_done, 1)
            dve.tensor_tensor(k_out[:], k_out[:], key[:], ALU.mult).then_inc(k_out_done, 1)

            def mix_level(n, m):
                dve.wait_ge(level_exp, n + 1)
                for side in range(2):
                    src = key if side == d else q_st
                    dve.tensor_tensor(half(mix[n % ring], m, side), half(mix[n % ring], m, side), half(src, m, side),
                                      ALU.mult).then_inc(mixed, 1)

            if output:
                dve.wait_ge(q_staged, 1)
                mix_level(*levels[0])
                dve.wait_ge(diagonal, 1)
                for b in range(2):
                    four = slice(4 * b, 4 * b + 4)
                    dve.tensor_tensor(att[:, four, :], banks[4 + b][:, :].rearrange("p (h t) -> p h t", h=4),
                                      spread(core.const("ident"), 1, 4), ALU.mult).then_inc(att_done, 1)
                mix_level(*levels[1])
                for n, m in levels:
                    if n + 2 < len(levels):
                        mix_level(*levels[n + 2])
                    side = "left_right" if d == 0 else "right_left"
                    mask = core.const(f"{side}_{m}").bitcast(U32)
                    for b in range(2):
                        dve.wait_ge(products, 2 * n + b + 1)
                        four = slice(4 * b, 4 * b + 4)
                        if n == 0:
                            dve.wait_ge(att_done, 2)
                        else:
                            dve.wait_ge(merged, 2 * n)
                        dve.copy_predicated(att[:, four, :], spread(mask, 1, 4),
                                            banks[2 * (n % 2) + b][:, :].rearrange("p (h t) -> p h t", h=4))\
                           .then_inc(merged, 1)
                    if n == 1:
                        dve.wait_ge(q_exp, 1)
                        dve.tensor_tensor(q_in[:], q_in[:], q_st[:], ALU.mult).then_inc(q_in_done, 1)
                for b in range(2):
                    dve.wait_ge(o_done, b + 1)
                    out = o[:, 4 * b:4 * b + 4, here]
                    dve.tensor_tensor(out, out, banks[6 + b][:, :].rearrange("p (h t) -> p h t", h=4), ALU.add)\
                       .then_inc(o_added, 1)
            dve.wait_ge(fade_done, 1)
            for h in range(HG_HEADS):
                dve.wait_ge(states_made, h // 4 + 1)
                dve.scalar_tensor_tensor(out=state[:, h, :], in0=state[:, h, :], scalar=fade[:, h:h + 1],
                                         in1=banks[4 + h // 4][:, (h % 4) * P:(h % 4 + 1) * P], op0=ALU.mult, op1=ALU.add)


def gla(core, w_in, h, o, const):
    tiles = TOK // P
    wide = [P, HG_HEADS, CHUNK]
    with core.room(v=[P, tiles, D], q=[P, HG_HEADS, SEQ]) as (v, q):
        gemm_tokens(core, "v", w_in[:, MIX_AT["v"]:MIX_AT["g"]], h, tiles,
                    lambda t, s: v[:, t, s * 256:(s + 1) * 256], [(at, 256) for at in range(0, D, 256)])
        gemm(core, "q", w_in[:, MIX_AT["q"]:MIX_AT["f"]], h, [(0, SEQ)], lambda tile, n: q[:, bass.ds(tile, 1), :], DT, 4,
             func=ACT.Silu)
        with core.room(f=[P, HG_HEADS, TOK], hg_state=[P, HG_HEADS, P]) as (f, state):
            with core.stage("cleared") as (block, cleared):
                @block.gpsimd
                def _(pool):
                    pool.memset(o[:], 0.0).then_inc(cleared, 1)
            for d in range(2):
                at = MIX_AT["f"] + d * D
                gemm(core, f"f{d}", w_in[:, at:at + D], h, SPANS,
                     lambda tile, n: f[:, bass.ds(tile, 1), SPANS[n][0]:SPANS[n][0] + SPANS[n][1]], HG_HEADS, 4)
                with core.stage("cleared") as (block, cleared):
                    @block.vector
                    def _(dve):
                        dve.memset(state[:], 0.0)
                names = ["key", "acum", "q_st", "v_st", "q_in", "k_out", "att", "mix0", "mix1", "mix2", "mix3"]
                with core.more_constants(LEVEL_CONST[d], const), core.room(**{f"{n}_{d}": wide for n in names}, **{f"fade_{d}": [P, HG_HEADS]}) as buf:
                    chunks_of(core, d, lambda token, tile, output: gla_chunk(
                        core, d, token, tile, output, q, f, v, state, o, buf))


def gate_by(core, name, y, w_gate, x, sq=None):
    with core.room(**{f"{name}_gate": [P, DT, SEQ]}) as (gate,):
        def apply(dve, tile, out_done, gated):
            dve.wait_ge(out_done, tile + 1 + 4)
            here = bass.ds(tile, 1)
            dve.tensor_tensor(y[:, here, :], y[:, here, :], gate[:, here, :], ALU.mult).then_inc(gated, 1)

        def square(act, tile, gated):
            act.wait_ge(gated, tile + 1)
            here = bass.ds(tile, 1)
            act.activation(sq[:, here, :], y[:, here, :], ACT.Square)

        gemm(core, f"{name}_g", w_gate, x, [(0, SEQ)], lambda tile, n: gate[:, bass.ds(tile, 1), :], DT, 4, func=ACT.Silu,
             extra=("gated",), dve_behind=apply, act_behind=square if sq is not None else None)


def group_norm(core, y, sq, groups, gain, square):
    size = DT // groups
    width = size * P
    with core.stage("squared", "sq_summed", "var_done", "root_done", "inverse_done", "scaled") as (
            block, squared, sq_summed, var_done, root_done, inverse_done, scaled):
        @block.vector
        def _(dve):
            for g in range(groups):
                dve.wait_ge(sq_summed, g + 1)
                dve.tensor_scalar(sq[:, g * size, :], core.banks[g][:, :], 1.0 / width, EPS, ALU.mult, ALU.add)\
                    .then_inc(var_done, 1)
            for g in range(groups):
                rstd = sq[:, g * size, :]
                dve.wait_ge(root_done, g + 1)
                dve.reciprocal(rstd, rstd).then_inc(inverse_done, 1)
                dve.wait_ge(inverse_done, g + 1)
                for k in range(g * size, (g + 1) * size):
                    dve.scalar_tensor_tensor(out=y[:, k, :], in0=y[:, k, :], scalar=gain(k), in1=rstd, op0=ALU.mult,
                                             op1=ALU.mult).then_inc(scaled, 1)

        @block.scalar
        def _(act):
            if square:
                for k in range(DT):
                    act.activation(sq[:, k, :], y[:, k, :], ACT.Square).then_inc(squared, 1)
            for g in range(groups):
                act.wait_ge(var_done, g + 1)
                act.activation(sq[:, g * size, :], sq[:, g * size, :], ACT.Sqrt).then_inc(root_done, 1)

        @block.tensor
        def _(pe):
            for g in range(groups):
                for k in range(g * size, (g + 1) * size):
                    if square:
                        pe.wait_ge(squared, k + 1)
                    mm = pe.matmul(core.banks[g][:, :], core.const("ones"), sq[:, k, :], start=(k % size == 0),
                                   stop=(k % size == size - 1))
                mm.then_inc(sq_summed, 1)


def even_mixer(core, w_in, w_dt, w_out, h, y, rows, const):
    with core.more_constants(SSD_CONST, const):
        ssd(core, w_in, w_dt, h, y, rows)
    with core.room(o_hg=[P, DT, SEQ]) as (o,):
        gla(core, w_in, h, o, const)
        with core.room(branch_sq=[P, DT, SEQ]) as (sq,):
            gate_by(core, "ssd", y, w_in[:, MIX_AT["z"]:MIX_AT["xbc"]], h, sq)
            group_norm(core, y, sq, SSD_G, lambda k: core.col("ssd_norm_w", k), False)
            group_norm(core, o, sq, HG_HEADS, lambda k: core.col("hg_norm_w", k), True)
        gate_by(core, "hg", o, w_in[:, MIX_AT["g"]:], h)
        y_parts = [part[:, :, 0:SEQ] for part in h]
        with core.split_room(o_parts=[P, DT, SEQ]) as (o_parts,):
            split(core, [(y, y_parts), (o, o_parts)])
            gemm(core, "mix_out", w_out, y_parts, [(0, SEQ)], lambda tile, n: y[:, bass.ds(tile, 1), :], DT, 2, more=o_parts)

HEAD_SCALE = HD ** -0.5
PAIRS = NSA_H // 2
UNITS = 2 * TT
NC = SEQ // RW_C
RU = 2 * NC


def causal_attention(core, name, q, k, v, out, gates):
    banks = core.banks
    with core.room(**{f"{name}_q": [P, SEQ], f"{name}_k": [P, SEQ], f"{name}_p": [P, 2, SEQ],
                      f"{name}_pt": [P, 2, SEQ], f"{name}_top": [P, UNITS], f"{name}_bias": [P, UNITS],
                      f"{name}_sum": [P, UNITS]}) as (q_st, k_st, prob, prob_t, top, bias, total), \
            core.nc.Fori(0, PAIRS) as j, \
            core.stage("staged", "scored", "masked", "top_done", "bias_done", "exp_done", "turned", "taken", "summed",
                       "guarded", "inverted", "weighed", "added") as (
                block, staged, scored, masked, top_done, bias_done, exp_done, turned, taken, summed, guarded, inverted,
                weighed, added):
        @block.tensor
        def _(pe):
            def scores(u):
                e, t = u // TT, u % TT
                if u >= 2:
                    pe.wait_ge(exp_done, u - 1)
                pe.matmul(banks[u % 2][:, 0:(t + 1) * P], q_st[HD * e:HD * e + HD, t * P:(t + 1) * P],
                          k_st[HD * e:HD * e + HD, 0:(t + 1) * P], start=True, stop=True).then_inc(scored, 1)

            def turn(u):
                t = u % TT
                pe.wait_ge(exp_done, u + 1)
                if u >= 2:
                    pe.wait_ge(taken, u - 1)
                for n in range(t + 1):
                    mm = pe.transpose(banks[2 + u % 2][:, n * P:(n + 1) * P], prob[:, u % 2, n * P:(n + 1) * P],
                                      core.const("ident"))
                mm.then_inc(turned, 1)

            def values(u):
                e, t = u // TT, u % TT
                pe.wait_ge(taken, u + 1)
                if u >= 2:
                    pe.wait_ge(added, u - 1)
                for n in range(t + 1):
                    mm = pe.matmul(banks[4 + u % 2][:, 0:HD], prob_t[:, u % 2, n * P:(n + 1) * P],
                                   v[:, n, bass.ds(j * (2 * HD) + HD * e, HD)], start=(n == 0), stop=(n == t))
                mm.then_inc(summed, 1)

            pe.wait_ge(staged, 2)
            scores(0)
            scores(1)
            for u in range(UNITS):
                turn(u)
                if u + 2 < UNITS:
                    scores(u + 2)
                if u >= 1:
                    values(u - 1)
            values(UNITS - 1)

        @block.scalar
        def _(act):
            act.activation(k_st[:, :].unsqueeze(1), k[:, bass.ds(j, 1), :], ACT.Copy).then_inc(staged, 1)

            def take(u):
                n = (u % TT + 1) * P
                act.wait_ge(turned, u + 1)
                if u >= 2:
                    act.wait_ge(summed, u - 1)
                act.activation(prob_t[:, u % 2, 0:n], banks[2 + u % 2][:, 0:n], ACT.Copy).then_inc(taken, 1)

            for u in range(UNITS):
                n = (u % TT + 1) * P
                act.wait_ge(bias_done, u + 1)
                if u >= 2:
                    act.wait_ge(turned, u - 1)
                act.activation(prob[:, u % 2, 0:n], banks[u % 2][:, 0:n], ACT.Exp, bias=bias[:, u:u + 1],
                               scale=HEAD_SCALE, accum_out=total[:, u:u + 1]).then_inc(exp_done, 1)
                if u >= 1:
                    take(u - 1)
            take(UNITS - 1)

        @block.vector
        def _(dve):
            def finish(u):
                e, t = u // TT, u % TT
                dve.wait_ge(exp_done, u + 1)
                dve.tensor_scalar(total[:, u:u + 1], total[:, u:u + 1], 1e-30, None, ALU.max).then_inc(guarded, 1)
                dve.wait_ge(guarded, u + 1)
                dve.reciprocal(total[:, u:u + 1], total[:, u:u + 1]).then_inc(inverted, 1)
                dve.wait_ge(inverted, u + 1)
                dst = out[:, t, bass.ds(j * (2 * HD) + HD * e, HD)]
                if gates is None:
                    dve.wait_ge(summed, u + 1)
                    dve.tensor_scalar(dst, banks[4 + u % 2][:, 0:HD], total[:, u:u + 1], None, ALU.mult)\
                       .then_inc(added, 1)
                else:
                    dve.tensor_tensor(total[:, u:u + 1], total[:, u:u + 1], gates(j, e, t), ALU.mult).then_inc(weighed, 1)
                    dve.wait_ge(weighed, u + 1)
                    dve.wait_ge(summed, u + 1)
                    dve.scalar_tensor_tensor(out=dst, in0=banks[4 + u % 2][:, 0:HD], scalar=total[:, u:u + 1],
                                             in1=dst, op0=ALU.mult, op1=ALU.add).then_inc(added, 1)

            dve.tensor_copy(q_st[:, :].unsqueeze(1), q[:, bass.ds(j, 1), :]).then_inc(staged, 1)
            for u in range(UNITS):
                t = u % TT
                dve.wait_ge(scored, u + 1)
                last = banks[u % 2][:, t * P:(t + 1) * P]
                dve.tensor_tensor(last, last, core.const("neg_since"), ALU.add).then_inc(masked, 1)
                dve.wait_ge(masked, u + 1)
                dve.tensor_reduce(top[:, u:u + 1], banks[u % 2][:, 0:(t + 1) * P], AX_X, ALU.max).then_inc(top_done, 1)
                dve.wait_ge(top_done, u + 1)
                dve.tensor_scalar(bias[:, u:u + 1], top[:, u:u + 1], -HEAD_SCALE, None, ALU.mult).then_inc(bias_done, 1)
                if u >= 2:
                    finish(u - 2)
            finish(UNITS - 2)
            finish(UNITS - 1)


def compress(core, n, kv, pos, w1, w2, k_out, v_out):
    half = SEQ // 2
    step = CMP_STRIDE // 2
    pairs = CMP_LEN // 2
    g_n = KV_H * N_CMP
    with core.room(**{f"cmp_even_odd{n}": [P, 2, half], f"cmp_pairs{n}": [P, KV_H, half],
                      f"cmp_x{n}": [P, pairs, KV_H, N_CMP], f"cmp_w1{n}": [P, pairs, CMP_HID], f"cmp_w2{n}": [P, 2, HD],
                      f"cmp_pos{n}": [P, pairs], f"cmp_hid{n}": [P, 2, g_n]}) as (
            even_odd, both, x, w1_sb, w2_sb, pos_sb, hid), \
            core.stage("w_in", "split", "moved", "placed", "hid_done", "active", "out_done", "out_taken", "cleared") as (
                block, w_in, split, moved, placed, hid_done, active, out_done, out_taken, cleared):
        @block.sync
        def _(sp):
            sp.dma_start(w1_sb[:], w1.rearrange("(k p) m -> p k m", p=P)).then_inc(w_in, 16)
            sp.dma_start(w2_sb[:], w2.rearrange("(k p) m -> p k m", p=P)).then_inc(w_in, 16)
            sp.dma_start(pos_sb[:], pos).then_inc(w_in, 16)
            sp.wait_ge(split, 1)
            for g in range(KV_H):
                for parity in range(2):
                    sp.dma_start(both[HD * parity:HD * parity + HD, g, :], even_odd[HD * g:HD * g + HD, parity, :])\
                      .then_inc(moved, 16)
            sp.wait_ge(moved, 64)

        @block.vector
        def _(dve):
            dve.tensor_copy(even_odd[:], kv.rearrange("p (t a) -> p a t", a=2)).then_inc(split, 1)
            if v_out is not None:
                dve.memset(v_out[:], 0.0).then_inc(cleared, 1)
            else:
                dve.memset(k_out[:], 0.0).then_inc(cleared, 1)
            dve.wait_ge(w_in, 48)
            dve.wait_ge(moved, 64)
            for g in range(KV_H):
                for a in range(pairs // step):
                    src = both[:, g, step * a:step * (a + N_CMP)].rearrange("p (i b) -> p i b", b=step)
                    dst = x[:, step * a:step * (a + 1), g, :].rearrange("p b i -> p i b")
                    dve.tensor_tensor(dst, src, spread(pos_sb[:, step * a:step * (a + 1)], 1, N_CMP), ALU.add)\
                       .then_inc(placed, 1)
            dve.wait_ge(out_done, 1)
            dve.wait_ge(cleared, 1)
            if v_out is not None:
                dve.tensor_copy(v_out[0:N_CMP, :], core.banks[2][0:N_CMP, 0:KV_H * HD]).then_inc(out_taken, 1)
            else:
                for j in range(PAIRS):
                    for e in range(2):
                        g = (2 * j + e) // (NSA_H // KV_H)
                        rows = slice(HD * e, HD * e + HD)
                        dve.tensor_copy(k_out[rows, j, 0:N_CMP], core.banks[2][rows, g * N_CMP:(g + 1) * N_CMP])\
                           .then_inc(out_taken, 1)

        @block.tensor
        def _(pe):
            pe.wait_ge(w_in, 48)
            pe.wait_ge(placed, 2 * KV_H)
            for m in range(2):
                for i in range(pairs):
                    mm = pe.matmul(core.banks[m][:, 0:g_n], w1_sb[:, i, m * P:(m + 1) * P],
                                   x[:, i, :, :].rearrange("p g i -> p (g i)"), start=(i == 0), stop=(i == pairs - 1))
                mm.then_inc(hid_done, 1)
            pe.wait_ge(active, 2)
            for e in range(2):
                for m in range(2):
                    if v_out is not None:
                        mm = pe.matmul(core.banks[2][0:N_CMP, HD * e:HD * e + HD], hid[:, m, N_CMP * e:N_CMP * (e + 1)],
                                       w2_sb[:, m, :], start=(m == 0), stop=(m == 1))
                    else:
                        mm = pe.matmul(core.banks[2][HD * e:HD * e + HD, 0:g_n], w2_sb[:, m, :], hid[:, m, :],
                                       start=(m == 0), stop=(m == 1))
            mm.then_inc(out_done, 1)

        @block.scalar
        def _(act):
            for m in range(2):
                act.wait_ge(hid_done, m + 1)
                act.activation(hid[:, m, :], core.banks[m][:, 0:g_n], ACT.Gelu_apprx_tanh).then_inc(active, 1)


def compressed_attention(core, q, k, v, out, gates):
    n_u = NSA_H * TT
    keys = N_CMP + 1
    banks = core.banks
    per_bank = 4
    with core.room(cs=[P, NSA_H, TT, keys], cs_top=[P, n_u], cs_sum=[P, n_u], cs_t=[keys, n_u, P]) as (cs, top, total, cs_t), \
            core.stage("scored", "masked", "top_done", "shifted", "exp_done", "kept", "total_done", "guarded", "inverted",
                       "weighed", "prob_done", "turned", "taken", "summed", "written") as (
                block, scored, masked, top_done, shifted, exp_done, kept, total_done, guarded, inverted, weighed,
                prob_done, turned, taken, summed, written):
        flat = cs[:].rearrange("p h t k -> p (h t) k")

        @block.tensor
        def _(pe):
            for h in range(NSA_H):
                rows = slice(HD * (h % 2), HD * (h % 2) + HD)
                for t in range(TT):
                    mm = pe.matmul(banks[h % 2][:, ((h // 2) * TT + t) * keys:((h // 2) * TT + t + 1) * keys],
                                   q[rows, h // 2, t * P:(t + 1) * P], k[rows, h // 2, :], start=True, stop=True)
                mm.then_inc(scored, 1)
            pe.wait_ge(prob_done, 1)
            for u in range(n_u):
                mm = pe.transpose(banks[2 + u // 4][0:keys, (u % 4) * P:(u % 4 + 1) * P], flat[:, u, :], core.const("ident"))
                if u % 4 == 3:
                    mm.then_inc(turned, 1)
            for u in range(n_u):
                g = (u // TT) // (NSA_H // KV_H)
                if u % 4 == 0:
                    pe.wait_ge(taken, u // 4 + 1)
                bank = banks[(0, 1, 2)[u // 8]]
                if u == 16:
                    pe.wait_ge(taken, 6)
                mm = pe.matmul(bank[:, (u % 8) * HD:(u % 8 + 1) * HD], cs_t[:, u, :], v[:, g * HD:(g + 1) * HD],
                               start=True, stop=True)
                if u % 8 == 7:
                    mm.then_inc(summed, 1)

        @block.vector
        def _(dve):
            mask = core.const("cmp_mask").rearrange("p (t k) -> p t k", t=TT)
            valid = core.const("cmp_valid").rearrange("p (t k) -> p t k", t=TT)
            dve.wait_ge(scored, NSA_H)
            for h in range(NSA_H):
                src = banks[h % 2][:, (h // 2) * P:(h // 2 + 1) * P].rearrange("p (t k) -> p t k", t=TT)
                dve.tensor_tensor(cs[:, h], src, mask, ALU.add).then_inc(masked, 1)
            dve.wait_ge(masked, NSA_H)
            dve.tensor_reduce(top[:, :], flat, AX_X, ALU.max).then_inc(top_done, 1)
            dve.wait_ge(top_done, 1)
            dve.tensor_tensor(flat, flat, spread(top[:, :], 2, keys), ALU.subtract).then_inc(shifted, 1)
            dve.wait_ge(exp_done, 1)
            for h in range(NSA_H):
                dve.tensor_tensor(cs[:, h], cs[:, h], valid, ALU.mult).then_inc(kept, 1)
            dve.wait_ge(kept, NSA_H)
            dve.tensor_reduce(total[:, :], flat, AX_X, ALU.add).then_inc(total_done, 1)
            dve.wait_ge(total_done, 1)
            dve.tensor_scalar(total[:, :], total[:, :], 1e-30, None, ALU.max).then_inc(guarded, 1)
            dve.wait_ge(guarded, 1)
            dve.reciprocal(total[:, :], total[:, :]).then_inc(inverted, 1)
            dve.wait_ge(inverted, 1)
            dve.tensor_tensor(total[:].rearrange("p (h t) -> p h t", t=TT), total[:].rearrange("p (h t) -> p h t", t=TT),
                              gates, ALU.mult).then_inc(weighed, 1)
            dve.wait_ge(weighed, 1)
            dve.tensor_tensor(flat, flat, spread(total[:, :], 2, keys), ALU.mult).then_inc(prob_done, 1)
            for n in range(3):
                dve.wait_ge(summed, n + 1)
                src = banks[n][:, :].rearrange("p (h t d) -> p t h d", h=2, t=TT)
                dst = out[:, :, 2 * n * HD:2 * (n + 1) * HD].rearrange("p t (h d) -> p t h d", h=2)
                dve.tensor_copy(dst, src).then_inc(written, 1)

        @block.scalar
        def _(act):
            act.wait_ge(shifted, 1)
            act.activation(cs[:], cs[:], ACT.Exp, scale=HEAD_SCALE).then_inc(exp_done, 1)
            for n in range(n_u // 4):
                act.wait_ge(turned, n + 1)
                act.activation(cs_t[:, 4 * n:4 * n + 4, :].rearrange("k u t -> k (u t)"), banks[2 + n][0:keys, :],
                               ACT.Copy).then_inc(taken, 1)


def head_norm(core, name, o, mix, first, gain):
    heads = o.shape[2] // HD
    n = TT * heads
    with core.room(**{f"{name}_sq": [P, TT, heads * HD], f"{name}_rs": [P, n]}) as (sq, rs), \
            core.stage("squared", "summed", "var_done", "root_done", "inverted", "scaled", "turned", "taken") as (
                block, squared, summed, var_done, root_done, inverted, scaled, turned, taken):
        @block.scalar
        def _(act):
            act.activation(sq[:], o[:], ACT.Square).then_inc(squared, 1)
            act.wait_ge(var_done, 1)
            act.activation(rs[:, :], rs[:, :], ACT.Sqrt).then_inc(root_done, 1)
            for j in range(heads // 2):
                act.wait_ge(turned, j + 1)
                act.activation(mix[:, first + j, :], core.banks[j][:, :], ACT.Identity, scale=gain(j)).then_inc(taken, 1)

        @block.vector
        def _(dve):
            dve.wait_ge(squared, 1)
            dve.tensor_reduce(rs[:, :], sq[:].rearrange("p t (h d) -> p (t h) d", d=HD), AX_X, ALU.add).then_inc(summed, 1)
            dve.wait_ge(summed, 1)
            dve.tensor_scalar(rs[:, :], rs[:, :], 1.0 / HD, NORM_EPS, ALU.mult, ALU.add).then_inc(var_done, 1)
            dve.wait_ge(root_done, 1)
            dve.reciprocal(rs[:, :], rs[:, :]).then_inc(inverted, 1)
            dve.wait_ge(inverted, 1)
            o3 = o[:].rearrange("p t (h d) -> p (t h) d", d=HD)
            dve.tensor_tensor(o3, o3, spread(rs[:, :], 2, HD), ALU.mult).then_inc(scaled, 1)

        @block.tensor
        def _(pe):
            pe.wait_ge(scaled, 1)
            for j in range(heads // 2):
                for t in range(TT):
                    mm = pe.transpose(core.banks[j][:, t * P:(t + 1) * P], o[:, t, j * P:(j + 1) * P], core.const("ident"))
                mm.then_inc(turned, 1)


def load(core, pairs):
    with core.stage("loaded") as (block, loaded):
        @block.sync
        def _(sp):
            for dst, src in pairs:
                sp.dma_start(dst, src).then_inc(loaded, 16)
            sp.wait_ge(loaded, 16 * len(pairs))


def key_pairs(k, out):
    top, low = slice(0, HD), slice(HD, P)
    return [(out[top, 0, :], k[top, :]), (out[low, 0, :], k[top, :]), (out[:, 1, :], k[:, :]),
            (out[top, 2, :], k[low, :]), (out[low, 2, :], k[low, :])]


def repeat_values(core, pairs):
    with core.stage("repeated") as (block, repeated):
        @block.vector
        def _(dve):
            for dst, src in pairs:
                for t in range(TT):
                    dve.tensor_copy(dst[:, t, :].rearrange("p (g r d) -> p g r d", g=KV_H, d=HD),
                                    spread(src[:, t, :].rearrange("p (g d) -> p g d", g=KV_H), 2, NSA_H // KV_H))\
                       .then_inc(repeated, 1)


def nsa(core, w, h, cmp, mix):
    with core.room(nsa_o=[P, TT, NSA_H * HD], nsa_q=[P, 7, SEQ], nsa_g=[P, TT, AT2["rw"] - AT2["vs"]], nsa_kx=[P, PAIRS, SEQ],
                   nsa_vx=[P, TT, NSA_H * HD], kc=[P, PAIRS, N_CMP + 1], vc=[N_CMP + 1, KV_H * HD]) as (
            o, qk, vg, kx, vx, kc, vc):
        gemm(core, "nsa_qk", w, h, [(0, SEQ)], lambda tile, n: qk[:, bass.ds(tile, 1), :], 7, 7,
             at=lambda tile: tile * P if tile < 6 else AT2["kw"])
        q = qk[:, 0:3, :]
        gemm_tokens(core, "nsa_v", w, h, TT, lambda t, s: vg[:, t, :], [(AT2["vs"], AT2["rw"] - AT2["vs"])])
        vs, vw, vgt = (vg[:, :, AT2[part] - AT2["vs"]:AT2[after] - AT2["vs"]]
                       for part, after in (("vs", "kw"), ("vw", "gt"), ("gt", "rw")))
        with core.stage("gated") as (block, gated):
            @block.scalar
            def _(act):
                act.activation(vgt, vgt, ACT.Sigmoid).then_inc(gated, 1)
        compress(core, 0, qk[:, 3, :], cmp["pos"][0], cmp["w1"][0, 0], cmp["w2"][0, 0], kc, None)
        compress(core, 1, qk[:, 4, :], cmp["pos"][1], cmp["w1"][0, 1], cmp["w2"][0, 1], None, vc)
        all_gates = vgt.rearrange("p t (h b) -> p h t b", b=3)
        compressed_attention(core, q, kc, vc, o, all_gates[:, :, :, 0])

        def gates(branch):
            return lambda j, e, t: vg[:, t, bass.ds(j * 6 + (AT2["gt"] - AT2["vs"] + 3 * e + branch), 1)]

        load(core, key_pairs(qk[:, 5, :], kx))
        repeat_values(core, [(vx, vs)])
        causal_attention(core, "slc", q, kx, vx, o, gates(1))
        load(core, key_pairs(qk[:, 6, :], kx))
        repeat_values(core, [(vx, vw)])
        causal_attention(core, "win", q, kx, vx, o, gates(2))
        head_norm(core, "nsa", o, mix, 0, lambda j: core.col("nsa_gain", j))


def moba(core, w, h, mix):
    with core.room(moba_o=[P, TT, MOBA_H * HD], moba_qk=[P, 6, SEQ], moba_v=[P, TT, MOBA_H * HD]) as (o, qk, v):
        gemm(core, "moba_qk", w[:, AT2["mq"]:AT2["mv"]], h, [(0, SEQ)], lambda tile, n: qk[:, bass.ds(tile, 1), :], 6, 6)
        gemm_tokens(core, "moba_v", w[:, AT2["mv"]:], h, TT, lambda t, s: v[:, t, :], [(0, MOBA_H * HD)])
        causal_attention(core, "moba_a", qk[:, 0:3, :], qk[:, 3:6, :], v, o, None)
        head_norm(core, "moba_n", o, mix, 5, lambda j: core.col("moba_gain", j))


def rwkv_inputs(core, w, h, lora, r, v, gate, bonus, a_in, b_out, k_out, r_in, fade):
    with core.room(rw_p=[P, 7, SEQ + 1], rw_m=[P, 7, SEQ], rw_log=[P, 2, SEQ], rw_cum=[P, 2, SEQ], rw_a=[P, 2, SEQ],
                   rw_kk=[P, 2, SEQ], rw_t=[P, 2, SEQ], rw_t2=[P, 2, SEQ], rw_reset=[P, 2 * SEQ], rw_lora=[P, 256]) as (
            p, m, log_w, cum, a, kk, t1, t2, reset, lora_sb):
        with core.stage("first", "ones_in", "lora_in") as (block, first, ones_in, lora_in):
            @block.sync
            def _(sp):
                sp.dma_start(lora_sb[:], lora).then_inc(lora_in, 16)
                sp.wait_ge(lora_in, 16)

            @block.vector
            def _(dve):
                dve.memset(p[:, :, 0:1], 0.0).then_inc(first, 1)
                dve.memset(reset[:, :], 1.0).then_inc(ones_in, 1)
                dve.wait_ge(ones_in, 1)
                dve.memset(reset[:, ::RW_C], 0.0)
        gemm(core, "rw", w[:, AT2["rw"]:AT2["mq"]], h, [(0, SEQ)], lambda tile, n: p[:, bass.ds(tile, 1), 1:SEQ + 1], 7, 7)
        k = m[:, 2:4, :]
        with core.stage("step", "mixed", "squashed", "low_rank", "w_done", "a_done", "g_done", "kk_raw", "kk_sq", "kk_sum",
                        "kk_root", "rkr", "rkr_sum", "cum_done", "cum_exp", "cum_neg_exp", "before_exp", "before") as (
                block, step, mixed, squashed, low_rank, w_done, a_done, g_done, kk_raw, kk_sq, kk_sum, kk_root, rkr,
                rkr_sum, cum_done, cum_exp, cum_neg_exp, before_exp, before):
            banks = core.banks

            @block.vector
            def _(dve):
                steps = 0
                for n in range(7):
                    dve.tensor_tensor(m[:, n, :], p[:, n, 0:SEQ], p[:, n, 1:SEQ + 1], ALU.subtract).then_inc(step, 1)
                for n in (6, 0, 1, 2, 3, 4, 5):
                    dve.wait_ge(step, 7)
                    dve.scalar_tensor_tensor(out=m[:, n, :], in0=m[:, n, :], scalar=core.col("rw_mu", n),
                                             in1=p[:, n, 1:SEQ + 1], op0=ALU.mult, op1=ALU.add).then_inc(mixed, 1)
                dve.wait_ge(mixed, 7)
                for j in range(2):
                    dve.tensor_scalar(kk[:, j, :], k[:, j, :], core.col("rw_k_k", j), None, ALU.mult).then_inc(kk_raw, 1)
                dve.wait_ge(w_done, 2)
                dve.tensor_scalar(log_w[:], log_w[:], -RW_DECAY, None, ALU.mult).then_inc(step, 1)
                dve.wait_ge(step, 8)
                dve.tensor_tensor_scan(cum[:].rearrange("p j t -> p (j t)"), reset[:, :],
                                       log_w[:].rearrange("p j t -> p (j t)"), 0.0, ALU.mult, ALU.add).then_inc(cum_done, 1)
                dve.wait_ge(cum_done, 1)
                dve.tensor_tensor(t1[:], cum[:], log_w[:], ALU.subtract).then_inc(before, 1)
                dve.wait_ge(a_done, 2)
                for j in range(2):
                    dve.tensor_scalar(t2[:, j, :], a[:, j, :], -1.0, core.col("rw_k_a", j), ALU.add, ALU.mult)\
                       .then_inc(step, 1)
                dve.wait_ge(step, 10)
                dve.wait_ge(kk_raw, 2)
                dve.scalar_tensor_tensor(out=k, in0=t2[:], scalar=1.0, in1=k, op0=ALU.add, op1=ALU.mult).then_inc(step, 1)
                dve.wait_ge(step, 11)
                for j in range(2):
                    dve.scalar_tensor_tensor(out=t2[:, j, :], in0=m[:, j, :], scalar=core.col("rw_r_k", j), in1=k[:, j, :],
                                             op0=ALU.mult, op1=ALU.mult).then_inc(rkr, 1)
                dve.tensor_copy(v[:], m[:, 4:6, :]).then_inc(step, 1)
                dve.wait_ge(rkr_sum, 1)
                dve.wait_ge(step, 12)
                for j in range(2):
                    dve.tensor_tensor(bonus[:, j, :], banks[6 + j][:, :], v[:, j, :], ALU.mult).then_inc(step, 1)
                dve.wait_ge(kk_root, 2)
                dve.tensor_scalar(t2[:], t2[:], 1e-12, None, ALU.max).then_inc(step, 1)
                dve.wait_ge(step, 15)
                dve.reciprocal(t2[:], t2[:]).then_inc(step, 1)
                dve.wait_ge(step, 16)
                dve.tensor_tensor(kk[:], kk[:], t2[:], ALU.mult).then_inc(step, 1)
                dve.wait_ge(step, 17)
                dve.wait_ge(before_exp, 1)
                dve.scalar_tensor_tensor(out=a_in[:], in0=kk[:], scalar=-1.0, in1=t1[:], op0=ALU.mult, op1=ALU.mult)\
                   .then_inc(step, 1)
                dve.tensor_tensor(a[:], a[:], kk[:], ALU.mult).then_inc(step, 1)
                dve.wait_ge(step, 19)
                dve.wait_ge(cum_neg_exp, 1)
                dve.tensor_tensor(b_out[:], a[:], log_w[:], ALU.mult).then_inc(step, 1)
                dve.tensor_tensor(k_out[:], k, log_w[:], ALU.mult).then_inc(step, 1)
                dve.wait_ge(cum_exp, 1)
                dve.tensor_tensor(r_in[:], m[:, 0:2, :], cum[:], ALU.mult).then_inc(step, 1)
                dve.tensor_copy(fade[:], cum[:, :, RW_C - 1::RW_C]).then_inc(step, 1)
                del steps

            @block.scalar
            def _(act):
                act.wait_ge(mixed, 1)
                act.activation(m[0:32, 6, :], m[0:32, 6, :], ACT.Tanh).then_inc(squashed, 1)
                act.activation(m[64:128, 6, :], m[64:128, 6, :], ACT.Sigmoid).then_inc(squashed, 1)
                for j in range(2):
                    act.wait_ge(low_rank, j + 1)
                    act.activation(log_w[:, j, :], banks[j][:, :], ACT.Sigmoid, bias=core.col("rw_w0", j)).then_inc(w_done, 1)
                    act.activation(a[:, j, :], banks[2 + j][:, :], ACT.Sigmoid, bias=core.col("rw_a0", j)).then_inc(a_done, 1)
                    act.activation(gate[:, j, :], banks[4 + j][:, :], ACT.Copy).then_inc(g_done, 1)
                act.wait_ge(kk_raw, 2)
                act.wait_ge(mixed, 7)
                act.activation(r[:], kk[:], ACT.Square).then_inc(kk_sq, 1)
                act.wait_ge(rkr_sum, 1)
                for j in range(2):
                    act.wait_ge(kk_sum, 1)
                    act.activation(t2[:, j, :], banks[j][:, :], ACT.Sqrt).then_inc(kk_root, 1)
                act.wait_ge(before, 1)
                act.activation(t1[:], t1[:], ACT.Exp).then_inc(before_exp, 1)
                act.activation(log_w[:], cum[:], ACT.Exp, scale=-1.0).then_inc(cum_neg_exp, 1)
                act.wait_ge(cum_neg_exp, 1)
                act.activation(cum[:], cum[:], ACT.Exp).then_inc(cum_exp, 1)

            @block.tensor
            def _(pe):
                pe.wait_ge(squashed, 2)
                for j in range(2):
                    cols = slice(j * P, (j + 1) * P)
                    pe.matmul(banks[j][:, :], lora_sb[0:32, cols], m[0:32, 6, :], start=True, stop=True)
                    pe.matmul(banks[2 + j][:, :], lora_sb[32:64, cols], m[32:64, 6, :], start=True, stop=True)
                    pe.matmul(banks[4 + j][:, :], lora_sb[64:128, cols], m[64:128, 6, :], start=True, stop=True)\
                      .then_inc(low_rank, 1)
                pe.wait_ge(rkr, 2)
                for j in range(2):
                    mm = pe.matmul(banks[6 + j][:, :], core.const("head_ones"), t2[:, j, :], start=True, stop=True)
                mm.then_inc(rkr_sum, 1)
                pe.wait_ge(kk_sq, 1)
                pe.wait_ge(w_done, 2)
                for j in range(2):
                    mm = pe.matmul(banks[j][:, :], core.const("head_ones"), r[:, j, :], start=True, stop=True)
                mm.then_inc(kk_sum, 1)


def unit(u):
    return slice(u * RW_C, (u + 1) * RW_C)


def each_head(pe, bank, lhs, rhs, start=True, stop=True):
    for e in range(2):
        rows = slice(HD * e, HD * e + HD)
        mm = pe.matmul(bank[rows], lhs(rows, e), rhs(rows, e), start=start, stop=stop)
    return mm


def rwkv_products(core, name, jobs):
    banks = core.banks
    with core.stage("made", "taken") as (block, made, taken):
        @block.tensor
        def _(pe):
            for n, (lhs, rhs, _, _) in enumerate(jobs):
                for j in range(2):
                    k = 2 * n + j
                    if k >= 8:
                        pe.wait_ge(taken, k - 7)
                    for c in range(NC):
                        tok = unit(c)
                        mm = each_head(pe, banks[k % 8][:, tok], lambda r, e: lhs[r, j, tok],
                                       lambda r, e: rhs[r, j, tok] if rhs is not None
                                       else core.const("ident")[r, HD * e:HD * e + HD])
                    mm.then_inc(made, 1)

        @block.vector
        def _(dve):
            for n, (_, _, mask, out) in enumerate(jobs):
                for j in range(2):
                    dve.wait_ge(made, 2 * n + j + 1)
                    dst = out[:, NC * j:NC * (j + 1), :]
                    src = banks[(2 * n + j) % 8][:, :].rearrange("p (c t) -> p c t", c=NC)
                    if mask is None:
                        dve.tensor_copy(dst, src).then_inc(taken, 1)
                    else:
                        dve.tensor_tensor(dst, src, spread(mask, 1, NC), ALU.mult).then_inc(taken, 1)


def rwkv_inverse(core, lab, lab_t, t_inv, tt_inv, level, y):
    banks = core.banks

    def level_mask(m, turned):
        pair = {1: (1, 0), 2: (1, 1), 4: (4, 0), 8: (4, 1), 16: (16, 0), 32: (16, 1)}[m]
        name = f"rw_level{'T' if turned else ''}_{pair[0]}_{2 * pair[0]}"
        return spread(core.const(name)[:, RW_C * pair[1]:RW_C * (pair[1] + 1)], 1, RU)

    with core.stage("masked", "t_done", "y_done", "y_taken", "z_done", "zt_done") as (
            block, masked, t_done, y_done, y_taken, z_done, zt_done):
        sizes = [2, 4, 8, 16, 32]

        @block.vector
        def _(dve):
            eye = spread(core.const("rw_eye")[:, 0:RW_C], 1, RU)
            dve.tensor_tensor(t_inv[:], lab[:], level_mask(1, False), ALU.mult).then_inc(masked, 1)
            dve.tensor_tensor(tt_inv[:], lab_t[:], level_mask(1, True), ALU.mult).then_inc(masked, 1)
            dve.wait_ge(masked, 2)
            dve.tensor_tensor(t_inv[:], t_inv[:], eye, ALU.add).then_inc(t_done, 1)
            dve.tensor_tensor(tt_inv[:], tt_inv[:], eye, ALU.add).then_inc(t_done, 1)
            for n, m in enumerate(sizes):
                if n:
                    dve.wait_ge(y_done, 2 * n)
                dve.tensor_tensor(level[:], lab_t[:], level_mask(m, True), ALU.mult).then_inc(masked, 1)
                for j in range(2):
                    units = slice(NC * j, NC * (j + 1))
                    dve.wait_ge(z_done, 2 * n + j + 1)
                    dve.wait_ge(t_done, 2 + 4 * n)
                    dve.tensor_tensor(t_inv[:, units, :], t_inv[:, units, :],
                                      banks[2 + j][:, :].rearrange("p (c t) -> p c t", c=NC), ALU.add).then_inc(t_done, 1)
                    dve.wait_ge(zt_done, 2 * n + 2)
                    dve.tensor_tensor(tt_inv[:, units, :], tt_inv[:, units, :],
                                      banks[4 + j][:, :].rearrange("p (c t) -> p c t", c=NC), ALU.add).then_inc(t_done, 1)

        @block.scalar
        def _(act):
            for n in range(len(sizes)):
                for j in range(2):
                    act.wait_ge(y_done, 2 * n + j + 1)
                    if n:
                        act.wait_ge(zt_done, 2 * n)
                    act.activation(y[:, NC * j:NC * (j + 1), :], banks[j][:, :].rearrange("p (c t) -> p c t", c=NC),
                                   ACT.Copy).then_inc(y_taken, 1)

        @block.tensor
        def _(pe):
            for n in range(len(sizes)):
                pe.wait_ge(masked, 3 + n)
                pe.wait_ge(t_done, 2 + 4 * n)
                for j in range(2):
                    for c in range(NC):
                        u = NC * j + c
                        mm = each_head(pe, banks[j][:, unit(c)], lambda r, e: level[r, u, :], lambda r, e: t_inv[r, u, :])
                    mm.then_inc(y_done, 1)
                for j in range(2):
                    pe.wait_ge(y_taken, 2 * n + j + 1)
                    for c in range(NC):
                        u = NC * j + c
                        mm = each_head(pe, banks[2 + j][:, unit(c)], lambda r, e: tt_inv[r, u, :], lambda r, e: y[r, u, :])
                    mm.then_inc(z_done, 1)
                    for c in range(NC):
                        u = NC * j + c
                        mm = each_head(pe, banks[4 + j][:, unit(c)], lambda r, e: y[r, u, :], lambda r, e: tt_inv[r, u, :])
                    mm.then_inc(zt_done, 1)


def rwkv_scan(core, a_in, r_in, lak_t, lrb_t, lrk_t, tt_inv, b_tok, k_tok, v_tok, fade, state, x, sa, o):
    banks = core.banks
    with core.stage("x_made", "x_taken", "sa_made", "sa_taken", "o_made", "o_taken", "s_made", "s_added", "s_faded",
                    "cleared") as (block, x_made, x_taken, sa_made, sa_taken, o_made, o_taken, s_made, s_added, s_faded,
                                   cleared):
        @block.tensor
        def _(pe):
            pe.wait_ge(cleared, 1)
            for c in range(NC):
                tok = unit(c)
                if c:
                    pe.wait_ge(s_faded, 2 * c)
                for j in range(2):
                    u = NC * j + c
                    each_head(pe, banks[0][:, unit(j)], lambda r, e: lak_t[r, u, :], lambda r, e: v_tok[r, u, :], stop=False)
                    mm = each_head(pe, banks[0][:, unit(j)], lambda r, e: a_in[r, j, tok], lambda r, e: state[r, j, :],
                                   start=False)
                mm.then_inc(x_made, 1)
                pe.wait_ge(x_taken, c + 1)
                for j in range(2):
                    u = NC * j + c
                    mm = each_head(pe, banks[1][:, unit(j)], lambda r, e: tt_inv[r, u, :], lambda r, e: x[r, j, :])
                mm.then_inc(sa_made, 1)
                pe.wait_ge(sa_taken, c + 1)
                if c:
                    pe.wait_ge(o_taken, c)
                for j in range(2):
                    u = NC * j + c
                    each_head(pe, banks[3][:, unit(j)], lambda r, e: b_tok[r, u, :], lambda r, e: sa[r, j, :], stop=False)
                    mm = each_head(pe, banks[3][:, unit(j)], lambda r, e: k_tok[r, u, :], lambda r, e: v_tok[r, u, :],
                                   start=False)
                mm.then_inc(s_made, 1)
                for j in range(2):
                    u = NC * j + c
                    each_head(pe, banks[2][:, unit(j)], lambda r, e: state[r, j, :], lambda r, e: r_in[r, j, tok], stop=False)
                    each_head(pe, banks[2][:, unit(j)], lambda r, e: sa[r, j, :], lambda r, e: lrb_t[r, u, :],
                              start=False, stop=False)
                    mm = each_head(pe, banks[2][:, unit(j)], lambda r, e: v_tok[r, u, :], lambda r, e: lrk_t[r, u, :],
                                   start=False)
                mm.then_inc(o_made, 1)

        @block.vector
        def _(dve):
            dve.memset(state[:], 0.0).then_inc(cleared, 1)
            for c in range(NC):
                dve.wait_ge(x_made, c + 1)
                dve.tensor_copy(x[:], banks[0][:, 0:P].rearrange("p (j t) -> p j t", j=2)).then_inc(x_taken, 1)
                dve.wait_ge(sa_made, c + 1)
                if c:
                    dve.wait_ge(o_made, c)
                dve.tensor_copy(sa[:], banks[1][:, 0:P].rearrange("p (j t) -> p j t", j=2)).then_inc(sa_taken, 1)
                dve.wait_ge(s_made, c + 1)
                dve.wait_ge(o_made, c + 1)
                dve.tensor_tensor(state[:], state[:], banks[3][:, 0:P].rearrange("p (j t) -> p j t", j=2), ALU.add)\
                   .then_inc(s_added, 1)
                dve.wait_ge(s_added, c + 1)
                for j in range(2):
                    dve.tensor_scalar(state[:, j, :], state[:, j, :], fade[:, j, c:c + 1], None, ALU.mult)\
                       .then_inc(s_faded, 1)

        @block.scalar
        def _(act):
            for c in range(NC):
                act.wait_ge(o_made, c + 1)
                act.activation(o[:, :, unit(c)], banks[2][:, 0:P].rearrange("p (j t) -> p j t", j=2), ACT.Copy)\
                   .then_inc(o_taken, 1)


def rwkv_output(core, o, bonus, gate, mix):
    banks = core.banks
    with core.room(rw_sq=[P, 2, SEQ], rw_rstd=[P, 2, SEQ]) as (sq, rstd), \
            core.stage("summed", "centered", "squared", "sq_summed", "var_done", "root_done", "inverted", "scaled",
                       "shifted", "bonused") as (block, summed, centered, squared, sq_summed, var_done, root_done,
                                                 inverted, scaled, shifted, bonused):
        @block.tensor
        def _(pe):
            for j in range(2):
                mm = pe.matmul(banks[j][:, :], core.const("head_ones"), o[:, j, :], start=True, stop=True)
            mm.then_inc(summed, 1)
            for j in range(2):
                pe.wait_ge(squared, j + 1)
                mm = pe.matmul(banks[2 + j][:, :], core.const("head_ones"), sq[:, j, :], start=True, stop=True)
                mm.then_inc(sq_summed, 1)

        @block.vector
        def _(dve):
            dve.wait_ge(summed, 1)
            for j in range(2):
                dve.scalar_tensor_tensor(out=o[:, j, :], in0=banks[j][:, :], scalar=-1.0 / HD, in1=o[:, j, :],
                                         op0=ALU.mult, op1=ALU.add).then_inc(centered, 1)
            for j in range(2):
                dve.wait_ge(sq_summed, j + 1)
                dve.tensor_scalar(rstd[:, j, :], banks[2 + j][:, :], 1.0 / HD, RW_LN_EPS, ALU.mult, ALU.add)\
                   .then_inc(var_done, 1)
            for j in range(2):
                dve.wait_ge(root_done, j + 1)
                dve.reciprocal(rstd[:, j, :], rstd[:, j, :]).then_inc(inverted, 1)
            for j in range(2):
                dve.wait_ge(inverted, j + 1)
                dve.scalar_tensor_tensor(out=o[:, j, :], in0=o[:, j, :], scalar=core.col("rw_lnx_w", j), in1=rstd[:, j, :],
                                         op0=ALU.mult, op1=ALU.mult).then_inc(scaled, 1)
            for j in range(2):
                dve.wait_ge(scaled, j + 1)
                dve.scalar_tensor_tensor(out=o[:, j, :], in0=o[:, j, :], scalar=core.col("rw_lnx_b", j), in1=bonus[:, j, :],
                                         op0=ALU.add, op1=ALU.add).then_inc(shifted, 1)
            for j in range(2):
                dve.wait_ge(shifted, j + 1)
                dve.tensor_tensor(mix[:, 3 + j, :], o[:, j, :], gate[:, j, :], ALU.mult).then_inc(bonused, 1)

        @block.scalar
        def _(act):
            for j in range(2):
                act.wait_ge(centered, j + 1)
                act.activation(sq[:, j, :], o[:, j, :], ACT.Square).then_inc(squared, 1)
            for j in range(2):
                act.wait_ge(var_done, j + 1)
                act.activation(rstd[:, j, :], rstd[:, j, :], ACT.Sqrt).then_inc(root_done, 1)


def rwkv(core, w, h, lora, mix):
    two, by_unit = [P, 2, SEQ], [P, RU, RW_C]
    with core.room(rw_v=two, rw_gate=two, rw_bonus=two, rw_a_in=two, rw_b_out=two, rw_k_out=two, rw_r_in=two, rw_o=two,
                   rw_fade=[P, 2, NC]) as (v, gate, bonus, a_in, b_out, k_out, r_in, o, fade):
        rwkv_inputs(core, w, h, lora, o, v, gate, bonus, a_in, b_out, k_out, r_in, fade)
        with core.room(lab=by_unit, lab_t=by_unit, lak_t=by_unit, lrb_t=by_unit, lrk_t=by_unit, b_tok=by_unit,
                       k_tok=by_unit, v_tok=by_unit, t_inv=by_unit, tt_inv=by_unit, level=by_unit, rw_y=by_unit,
                       rw_state=[P, 2, HD], rw_x=[P, 2, HD], rw_sa=[P, 2, HD]) as (
                lab, lab_t, lak_t, lrb_t, lrk_t, b_tok, k_tok, v_tok, t_inv, tt_inv, level, y, state, x, sa):
            before = core.const("rw_masks")[:, 0:RW_C]
            until = core.const("rw_masks")[:, RW_C:2 * RW_C]
            after = core.const("rw_eye")[:, RW_C:2 * RW_C]
            rwkv_products(core, "rw", [
                (b_out, a_in, before, lab_t), (a_in, b_out, after, lab), (k_out, a_in, before, lak_t),
                (b_out, r_in, until, lrb_t), (k_out, r_in, until, lrk_t),
                (b_out, None, None, b_tok), (k_out, None, None, k_tok), (v, None, None, v_tok)])
            rwkv_inverse(core, lab, lab_t, t_inv, tt_inv, level, y)
            rwkv_scan(core, a_in, r_in, lak_t, lrb_t, lrk_t, tt_inv, b_tok, k_tok, v_tok, fade, state, x, sa, o)
        rwkv_output(core, o, bonus, gate, mix)


def causal_tap(n):
    return lambda b: b[:, n:n + SEQ]


def second_block(core, x, w):
    with core.split_room(h2=[P, DT, SEQ]) as (h,), core.room(mix2=[P, DT, SEQ]) as (mix,):
        norm(core, "attn_norm", x, mix, lambda k: core.col("attn_norm", k), eps=NORM_EPS, center=False)
        split(core, [(mix, h)])
        with core.more_constants(ODD_CONST, w["const"]):
            nsa(core, w["w_in_2"], h, w["cmp"], mix)
            moba(core, w["w_in_2"], h, mix)
            rwkv(core, w["w_in_2"], h, w["lora"], mix)
        with core.room(y2=[P, DT, SEQ]) as (y,):
            split(core, [(mix, h)])
            gemm(core, "out2", w["w_out_2"], h, [(0, SEQ)], lambda tile, n: y[:, bass.ds(tile, 1), :], DT, 4)
            residual(core, x, y, None)

    def fill(parts):
        with core.room(normed=[P, DT, SEQ]) as (normed,):
            norm(core, "ffn_norm", x, normed, lambda k: core.col("ffn_norm", k), eps=NORM_EPS, center=False)
            split(core, [(normed, parts)])

    with glu_ffn(core, "ffn2", w["ffn_w_in_2"], D_FF, 0, w["ffn_w_out_2"], fill, lambda: core.room(y3=[P, DT, SEQ]),
                 SEQ + 2, lambda b: b[:, 2:SEQ + 2], [causal_tap(n) for n in range(3)],
                 lambda t, n: core.col("ffn2_conv_w", t, n), lambda t: core.col("ffn2_conv_b", t), ACT.Silu) as y:
        residual(core, x, y, None)
    norm(core, "final_norm", x, x, lambda k: core.col("final_norm", k), eps=NORM_EPS, center=False)


def condition(core, weights, cond, layer, mods):
    ring_n, width = 3, 512
    w = weights.rearrange("(k p) f -> p k f", p=P)
    slabs = weights.shape[1] // width
    steps = slabs // ring_n
    tiles = weights.shape[1] // P
    with core.room(ada_ring=[P, ring_n, DT, width], ada_rows=[2, slabs * width]) as (ring, rows), \
            core.stage("slab_in0", "slab_in1", "slab_in2", "slab_done", "banks_free", "slots_refilled", "turned", "biased") as (
                block, slab_in0, slab_in1, slab_in2, slab_done, banks_free, slots_refilled, turned, biased):
        slab_in = [slab_in0, slab_in1, slab_in2]

        @block.sync
        def _(sp):
            for u in range(ring_n):
                sp.dma_start(ring[:, u], w[:, :, u * width:(u + 1) * width]).then_inc(slab_in[u], 16)
            with sp.Fori(1, steps) as i:
                for u in range(ring_n):
                    feature = sp.snap((i * ring_n + u) * width)
                    sp.wait_ge(slab_done, (i - 1) * ring_n + u + 1)
                    sp.sem_inc(slots_refilled, 1)
                    sp.dma_start(ring[:, u], w[:, :, bass.ds(feature, width)]).then_inc(slab_in[u], 16)

        @block.tensor
        def _(pe):
            with pe.Fori(0, steps) as i:
                for u in range(ring_n):
                    pe.wait_ge(slab_in[u], (i + 1) * 16)
                    pe.wait_ge(banks_free, i * ring_n + u + 1)
                    for k in range(DT):
                        mm = pe.matmul(core.banks[u][0:2, :], cond[:, k, :], ring[:, u, k, :], start=(k == 0),
                                       stop=(k == DT - 1))
                    mm.then_inc(slab_done, 1)
            pe.wait_ge(banks_free, ring_n + slabs)
            for t in range(tiles):
                mm = pe.transpose(core.banks[4][:, 2 * t:2 * t + 2], rows[:, t * P:(t + 1) * P], core.const("ident")[0:2, 0:2])
            mm.then_inc(turned, 1)

        @block.scalar
        def _(act):
            act.sem_inc(banks_free, ring_n)
            with act.Fori(0, steps) as i:
                for u in range(ring_n):
                    act.wait_ge(slab_done, i * ring_n + u + 1)
                    act.activation(rows[:, bass.ds((i * ring_n + u) * width, width)], core.banks[u][0:2, :], ACT.Copy)\
                       .then_inc(banks_free, 1)

        @block.vector
        def _(dve):
            at = COL_AT[f"ada_b{layer}"]
            dve.wait_ge(turned, 1)
            dve.tensor_tensor(mods[:], core.banks[4][:, 0:2 * tiles].rearrange("p (t w) -> p t w", w=2),
                              spread(core.cols_sb[:, at:at + tiles], 2, 2), ALU.add).then_inc(biased, 1)


def conditioning(core, ada_w, mods):
    with core.room(cond=[P, DT, 2]) as (cond,):
        with core.stage("cond_done") as (block, cond_done):
            @block.scalar
            def _(act):
                at = COL_AT["c"]
                act.activation(cond[:].rearrange("p k w -> p (k w)"), core.cols_sb[:, at:at + 2 * DT], ACT.Silu)\
                   .then_inc(cond_done, 1)
        for layer in range(DEPTH):
            condition(core, ada_w[layer], cond, layer, mods[layer])
    with core.stage("raised") as (block, raised):
        @block.vector
        def _(dve):
            for layer in range(DEPTH):
                for part in (1, 4):
                    scale = mods[layer][:, part * DT:(part + 1) * DT, :]
                    dve.tensor_scalar(scale, scale, 1.0, None, ALU.add).then_inc(raised, 1)


def model(nc, x, ctx, const, cols, rows, lora, pos, ada_w, mix_w_dt, mix_w_in, mix_w_out, conf_w1, conf_w2, ffn_w_up, ffn_w_down,
          w_in_2, cmp_w1, cmp_w2, w_out_2, ffn_w_in_2, ffn_w_out_2, out):
    features = lambda a: a.rearrange("(k p) t -> p k t", p=P)
    with ExitStack() as stack:
        core = Core(nc, stack)
        mods = [stack.enter_context(nc.sbuf_tensor(f"mods{layer}", [P, 6 * DT, 2], F32)) for layer in range(DEPTH)]
        load(core, [(core.const_sb[:], const[:, 0:ALWAYS, :]), (core.cols_sb[:], cols)])
        conditioning(core, ada_w, mods)

        def mod(layer, part, who=0):
            return lambda k: mods[layer][:, part * DT + k, who:who + 1]

        def finish_half(name, layer, n, x_sb, y_sb):
            residual(core, x_sb, y_sb, mod(layer, 3 * n + 2))
            norm(core, name, x_sb, x_sb, lambda k: core.col("post_ln_g", k, 2 * layer + n),
                 lambda k: core.col("post_ln_b", k, 2 * layer + n))

        def ffn(layer, x_sb):
            def fill(parts):
                with core.room(modulated=[P, DT, SEQ]) as (modulated,):
                    modulate(core, x_sb, mod(layer, 3), mod(layer, 4), modulated)
                    split(core, [(modulated, parts)])

            with glu_ffn(core, f"ffn{layer}", ffn_w_up[layer], D_FF, 0, ffn_w_down[layer], fill,
                         lambda: core.room(ffn_y=[P, DT, SEQ]), GRID_PAD, grid_window(1, 1), GRID_TAPS,
                         lambda t, n: core.col(f"ffn_conv_w{layer}", t, n), lambda t: core.col("ffn_conv_b", t, layer),
                         ACT.Gelu) as y:
                finish_half(f"ln_ffn{layer}", layer, 1, x_sb, y)

        with core.room(x_sb=[P, DT, SEQ]) as (x_sb,):
            with core.split_room(h0=[P, DT, TOK]) as (h,), core.room(rows_sb=[P, 72]) as (rows_sb,):
                with core.room(tokens=[P, DT, TOK]) as (tokens,):
                    lat, both = slice(0, SEQ), slice(SEQ, TOK)
                    load(core, [(tokens[:, :, lat], features(x)), (tokens[:, :, both], features(ctx)), (rows_sb[:], rows)])
                    split(core, [(tokens[:, :, part], [side[:, :, part] for side in h]) for part in (lat, both)],
                          [(mod(0, 0), mod(0, 1)), (mod(0, 0, 1), mod(0, 1, 1))])
                even_mixer(core, mix_w_in[0], mix_w_dt, mix_w_out[0], h, x_sb, rows_sb, const)
            with core.room(x_again=[P, DT, SEQ]) as (x_again,):
                load(core, [(x_again[:], features(x))])
                with core.stage("scaled", "added") as (block, scaled, added):
                    @block.scalar
                    def _(act):
                        for k in range(DT):
                            act.activation(x_again[:, k, :], x_again[:, k, :], ACT.Identity, scale=ALPHA)\
                               .then_inc(scaled, 1)

                    @block.vector
                    def _(dve):
                        for k in range(DT):
                            dve.wait_ge(scaled, k + 1)
                            dve.scalar_tensor_tensor(out=x_sb[:, k, :], in0=x_sb[:, k, :], scalar=mod(0, 2)(k),
                                                     in1=x_again[:, k, :], op0=ALU.mult, op1=ALU.add).then_inc(added, 1)
            norm(core, "ln_mix0", x_sb, x_sb, lambda k: core.col("post_ln_g", k), lambda k: core.col("post_ln_b", k))
            ffn(0, x_sb)
            with core.split_room(h1=[P, DT, SEQ]) as (h,), core.room(y1=[P, DT, SEQ]) as (y,):
                modulate(core, x_sb, mod(1, 0), mod(1, 1), y)
                split(core, [(y, h)])
                conformer(core, conf_w1[0], conf_w2[0], h, y)
                finish_half("ln_mix1", 1, 0, x_sb, y)
            ffn(1, x_sb)
            second_block(core, x_sb, {"const": const, "w_in_2": w_in_2[0], "cmp": {"pos": pos, "w1": cmp_w1, "w2": cmp_w2}, "lora": lora,
                                      "w_out_2": w_out_2[0], "ffn_w_in_2": ffn_w_in_2[0], "ffn_w_out_2": ffn_w_out_2[0]})
            with core.stage("stored") as (block, stored):
                @block.sync
                def _(sp):
                    sp.dma_start(features(out), x_sb[:]).then_inc(stored, 16)
                    sp.wait_ge(stored, 16)


WEIGHTS = {
    "mix_w_in": "mix_w_in", "mix_w_out": "mix_w_out", "conf_w1": "conf_w1", "conf_w2": "conf_w2",
    "ffn_w_up": "ffn_w_up", "ffn_w_down": "ffn_w_down", "w_in_2": "w_in_2", "cmp_w1": "nsa_cmp_w1_2",
    "cmp_w2": "nsa_cmp_w2_2", "w_out_2": "w_out_2", "ffn_w_in_2": "ffn_w_in_2", "ffn_w_out_2": "ffn_w_out_2",
}


def laid_out(inputs):
    vectors = {name: inputs[name] for name in COLS if name in inputs}
    vectors["c"] = np.concatenate([inputs["c"], inputs["c_ctx"][None]])
    for layer in range(DEPTH):
        vectors[f"ada_b{layer}"] = inputs["ada_b"][layer]
        vectors[f"ffn_conv_w{layer}"] = inputs["ffn_conv_w"][layer]
    for name, source in (("attn_norm", "attn_norm_2"), ("ffn_norm", "ffn_norm_2"), ("final_norm", "final_norm_2"),
                         ("ffn2_conv_w", "ffn_conv_w_2"), ("ffn2_conv_b", "ffn_conv_b_2"), ("nsa_gain", "nsa_out_gain_2"),
                         ("moba_gain", "moba_out_gain_2")):
        vectors[name] = inputs[source]
    for name in ("mu", "w0", "a0", "k_k", "k_a", "r_k", "lnx_w", "lnx_b"):
        vectors[f"rw_{name}"] = inputs[f"rw_{name}_2"]
    arrays = {
        "x": np.ascontiguousarray(np.transpose(inputs["x"][0])),
        "ctx": np.ascontiguousarray(np.transpose(inputs["ctx"][0])),
        "const": constants(),
        "cols": columns(vectors),
        "rows": np.ascontiguousarray(np.concatenate([
            np.broadcast_to(np.reshape(inputs["ssd_dt_bias"], (1, 32)), (P, 32)),
            np.broadcast_to(np.reshape(inputs["ssd_a_log"], (1, 32)), (P, 32)),
            np.transpose(np.repeat(np.reshape(inputs["ssd_d"], (DT, 2)), SSD_P, axis=1))], axis=1)),
        "lora": np.ascontiguousarray(np.concatenate([inputs["rw_w2_2"][0], inputs["rw_a2_2"][0], inputs["rw_g2_2"][0]])),
        "pos": np.ascontiguousarray(np.transpose(np.reshape(inputs["nsa_cmp_pos_2"], (2, CMP_LEN // 2, P)), (0, 2, 1))),
    }
    steps = inputs["mix_w_in"][0][:, MIX_AT["dt"]:MIX_AT["q"]]
    arrays["ada_w"] = np.ascontiguousarray(inputs["ada_w"])
    arrays["mix_w_dt"] = np.ascontiguousarray(np.transpose(np.reshape(steps, (DT, P, 2 * SSD_HEADS)), (1, 0, 2)))
    for name, source in WEIGHTS.items():
        arrays[name] = np.ascontiguousarray(inputs[source])
    return arrays


def kernel(**inputs):
    import concourse.bacc as bacc
    from concourse.bass_utils import run_bass_kernel_spmd

    nc = bacc.Bacc("TRN2", target_bir_lowering=False, num_devices=1)
    arrays = {f"in_{name}": a for name, a in laid_out({k: np.asarray(v) for k, v in inputs.items()}).items()}
    args = [nc.dram_tensor(name, a.shape, mybir.dt.from_np(a.dtype), kind="ExternalInput").ap()
            for name, a in arrays.items()]
    out = nc.dram_tensor("out", (D, SEQ), F32, kind="ExternalOutput").ap()
    model(nc, *args, out)
    result = run_bass_kernel_spmd(nc, [arrays], core_ids=[0])
    return np.ascontiguousarray(np.transpose(result.results[0]["out"]))[None]
```
